# Optimizing a Trainium2 kernel written in Bass

```python
import jax, jax.numpy as jnp
from jax import lax
import numpy as np

D_MODEL = 1024
BATCH = 1
SEQ = 1024
DEPTH = 1

CONV_WIDTH = D_MODEL // 2
RWKV_WIDTH = D_MODEL - CONV_WIDTH
RWKV_HEAD = 64
RWKV_HEADS = RWKV_WIDTH // RWKV_HEAD
CONV_K = 31
DECAY_LORA = 64
A_LORA = 64
GATE_LORA = 160
D_FF = 2816
FFN_CONV_K = 3
N_RWKV_IN = 3 * RWKV_WIDTH + DECAY_LORA + A_LORA + GATE_LORA
N_IN = 2 * CONV_WIDTH + N_RWKV_IN
RWKV_SPLITS = (RWKV_WIDTH, 2 * RWKV_WIDTH, 3 * RWKV_WIDTH,
               3 * RWKV_WIDTH + DECAY_LORA, 3 * RWKV_WIDTH + DECAY_LORA + A_LORA)
RMS_EPS = 1e-6
LN_EPS = 1e-5
LNX_EPS = 64e-5


def rms_norm(x, g):
    xf = x.astype(jnp.float32)
    y = xf * lax.rsqrt(jnp.mean(xf * xf, axis=-1, keepdims=True) + RMS_EPS)
    return (y * g.astype(jnp.float32)).astype(x.dtype)

def layer_norm(x, eps):
    xf = x.astype(jnp.float32)
    mu = jnp.mean(xf, axis=-1, keepdims=True)
    d = xf - mu
    return d * lax.rsqrt(jnp.mean(d * d, axis=-1, keepdims=True) + eps)

def causal_dwconv(x, w, b):
    K, C = w.shape
    y = lax.conv_general_dilated(x, w[:, None, :].astype(x.dtype), window_strides=(1,),
                                 padding=[(K - 1, 0)],
                                 dimension_numbers=('NWC', 'WIO', 'NWC'),
                                 feature_group_count=C)
    return y + b

def wkv7_scan(r, decay, k, v, kk, a):
    B, T, H, N = r.shape

    def step(S, inp):
        r_t, w_t, k_t, v_t, kk_t, a_t = inp
        s_kk = jnp.einsum('bhij,bhj->bhi', S, kk_t)
        S = (S * w_t[:, :, None, :] - s_kk[..., None] * (a_t * kk_t)[:, :, None, :]
             + v_t[..., None] * k_t[:, :, None, :])
        return S, jnp.einsum('bhij,bhj->bhi', S, r_t)

    xs = tuple(jnp.moveaxis(z.astype(jnp.float32), 1, 0) for z in (r, decay, k, v, kk, a))
    S0 = jnp.zeros((B, H, N, N), jnp.float32)
    _, ys = lax.scan(step, S0, xs)
    return jnp.moveaxis(ys, 0, 1)

def token_mix(h, w_in, conv_dw_w, conv_dw_b, conv_ln_g, conv_ln_b, rwkv_mu, w0, w2,
              a0, a2, g2, k_k, k_a, r_k, lnx_g, lnx_b, w_out):
    B, T, _ = h.shape
    f32 = jnp.float32
    p = h @ w_in
    p_conv, p_rw = p[..., :2 * CONV_WIDTH], p[..., 2 * CONV_WIDTH:]

    u, u_gate = jnp.split(p_conv, 2, axis=-1)
    u = u * jax.nn.sigmoid(u_gate)
    u = causal_dwconv(u, conv_dw_w, conv_dw_b)
    u = jax.nn.silu((layer_norm(u, LN_EPS) * conv_ln_g + conv_ln_b).astype(h.dtype))

    prev = jnp.pad(p_rw, ((0, 0), (1, 0), (0, 0)))[:, :-1]
    p_rw = p_rw + (prev - p_rw) * rwkv_mu
    r, k, v, wd, ad, gd = jnp.split(p_rw, RWKV_SPLITS, axis=-1)
    w_log = -jax.nn.softplus(-(w0 + jnp.tanh(wd) @ w2).astype(f32)) - 0.5
    decay = jnp.exp(-jnp.exp(w_log))
    a = jax.nn.sigmoid(a0 + ad @ a2)
    g = jax.nn.sigmoid(gd) @ g2
    heads = lambda z: z.reshape(B, T, RWKV_HEADS, RWKV_HEAD)
    kk = heads(k * k_k).astype(f32)
    kk = kk / jnp.maximum(jnp.sqrt(jnp.sum(kk * kk, axis=-1, keepdims=True)), 1e-12)
    k = k * (1.0 + (a - 1.0) * k_a)
    rh, kh, vh = heads(r), heads(k), heads(v)
    y = wkv7_scan(rh, heads(decay), kh, vh, kk, heads(a))
    y = layer_norm(y, LNX_EPS).reshape(B, T, RWKV_WIDTH) * lnx_g + lnx_b
    bonus = jnp.sum((rh * kh * r_k).astype(f32), axis=-1, keepdims=True) * vh.astype(f32)
    y = ((y + bonus.reshape(B, T, RWKV_WIDTH)) * g).astype(h.dtype)

    return jnp.concatenate([u, y], axis=-1) @ w_out

def channel_mix(h, w_up, ffn_dw_w, ffn_dw_b, w_down):
    z = causal_dwconv(h @ w_up, ffn_dw_w, ffn_dw_b)
    z_gate, z_val = jnp.split(z, 2, axis=-1)
    return (jax.nn.silu(z_gate) * z_val) @ w_down

def first_inputs(seed: int = 0) -> dict:
    key = jax.random.key(seed)
    ks = jax.random.split(key, 32)
    L = DEPTH
    nrm = lambda k, shape, s: jax.random.normal(k, shape, jnp.float32) * s
    return {
        'x': nrm(ks[0], (BATCH, SEQ, D_MODEL), 1.0),
        'c': nrm(ks[1], (BATCH, D_MODEL), 1.0),
        'ada_w': nrm(ks[2], (L, D_MODEL, 6 * D_MODEL), 0.5 * D_MODEL ** -0.5),
        'ada_b': nrm(ks[3], (L, 6 * D_MODEL), 0.02),
        'mix_pre_g': 1.0 + nrm(ks[4], (L, D_MODEL), 0.05),
        'mix_post_g': 1.0 + nrm(ks[5], (L, D_MODEL), 0.05),
        'w_in': nrm(ks[6], (L, D_MODEL, N_IN), D_MODEL ** -0.5),
        'conv_dw_w': nrm(ks[7], (L, CONV_K, CONV_WIDTH), CONV_K ** -0.5),
        'conv_dw_b': nrm(ks[8], (L, CONV_WIDTH), 0.02),
        'conv_ln_g': 1.0 + nrm(ks[9], (L, CONV_WIDTH), 0.05),
        'conv_ln_b': nrm(ks[10], (L, CONV_WIDTH), 0.02),
        'rwkv_mu': jax.random.uniform(ks[11], (L, N_RWKV_IN), jnp.float32),
        'w0': jax.random.uniform(ks[12], (L, RWKV_WIDTH), jnp.float32, minval=-5.0, maxval=1.0),
        'w2': nrm(ks[13], (L, DECAY_LORA, RWKV_WIDTH), 0.5 * DECAY_LORA ** -0.5),
        'a0': nrm(ks[14], (L, RWKV_WIDTH), 0.5),
        'a2': nrm(ks[15], (L, A_LORA, RWKV_WIDTH), 0.5 * A_LORA ** -0.5),
        'g2': nrm(ks[16], (L, GATE_LORA, RWKV_WIDTH), GATE_LORA ** -0.5),
        'k_k': 0.85 + nrm(ks[17], (L, RWKV_WIDTH), 0.05),
        'k_a': 1.0 + nrm(ks[18], (L, RWKV_WIDTH), 0.05),
        'r_k': nrm(ks[19], (L, RWKV_HEADS, RWKV_HEAD), 0.1),
        'lnx_g': 1.0 + nrm(ks[20], (L, RWKV_WIDTH), 0.05),
        'lnx_b': nrm(ks[21], (L, RWKV_WIDTH), 0.02),
        'w_out': nrm(ks[22], (L, D_MODEL, D_MODEL), D_MODEL ** -0.5),
        'ffn_pre_g': 1.0 + nrm(ks[23], (L, D_MODEL), 0.05),
        'ffn_post_g': 1.0 + nrm(ks[24], (L, D_MODEL), 0.05),
        'w_up': nrm(ks[25], (L, D_MODEL, 2 * D_FF), D_MODEL ** -0.5),
        'ffn_dw_w': nrm(ks[26], (L, FFN_CONV_K, 2 * D_FF), FFN_CONV_K ** -0.5),
        'ffn_dw_b': nrm(ks[27], (L, 2 * D_FF), 0.02),
        'w_down': nrm(ks[28], (L, D_FF, D_MODEL), D_FF ** -0.5),
    }

def first_block(x, c, ada_w, ada_b, mix_pre_g, mix_post_g, w_in, conv_dw_w, conv_dw_b,
              conv_ln_g, conv_ln_b, rwkv_mu, w0, w2, a0, a2, g2, k_k, k_a, r_k,
              lnx_g, lnx_b, w_out, ffn_pre_g, ffn_post_g, w_up, ffn_dw_w, ffn_dw_b,
              w_down):
    for l in range(DEPTH):
        mod = jax.nn.silu(c) @ ada_w[l] + ada_b[l]
        sh_m, sc_m, gt_m, sh_f, sc_f, gt_f = jnp.split(mod[:, None, :], 6, axis=-1)
        h = rms_norm(x, mix_pre_g[l]) * (1.0 + sc_m) + sh_m
        m = token_mix(h, w_in[l], conv_dw_w[l], conv_dw_b[l], conv_ln_g[l], conv_ln_b[l],
                      rwkv_mu[l], w0[l], w2[l], a0[l], a2[l], g2[l], k_k[l], k_a[l],
                      r_k[l], lnx_g[l], lnx_b[l], w_out[l])
        x = x + gt_m * rms_norm(m, mix_post_g[l])
        h = rms_norm(x, ffn_pre_g[l]) * (1.0 + sc_f) + sh_f
        f = channel_mix(h, w_up[l], ffn_dw_w[l], ffn_dw_b[l], w_down[l])
        x = x + gt_f * rms_norm(f, ffn_post_g[l])
    return x


DEPTH_2 = 2

HEAD_DIM = 64
ATTN_WIDTH = D_MODEL
N_Q_HEADS = ATTN_WIDTH // HEAD_DIM
N_KV_HEADS = N_Q_HEADS // 4
Q_PER_KV = N_Q_HEADS // N_KV_HEADS
KV_WIDTH = N_KV_HEADS * HEAD_DIM
WINDOW = 128
ATTN_BLOCK = 128

D_INNER = D_MODEL
SSM_HEAD_DIM = 64
N_SSM_HEADS = D_INNER // SSM_HEAD_DIM
N_SSM_GROUPS = 2
SSM_HEADS_PER_GROUP = N_SSM_HEADS // N_SSM_GROUPS
D_STATE = 128
CONV_WIDTH_2 = 4
CHUNK = 128
CONV_CH = D_INNER + 2 * N_SSM_GROUPS * D_STATE

MIX_WIDTH = ATTN_WIDTH + D_INNER
IN_SPLITS = tuple(int(s) for s in np.cumsum([ATTN_WIDTH, KV_WIDTH, KV_WIDTH, ATTN_WIDTH, D_INNER, CONV_CH]))
IN_WIDTH = IN_SPLITS[-1] + N_SSM_HEADS

DEEPNORM_ALPHA = (2.0 * DEPTH_2) ** 0.25
DEEPNORM_BETA = (8.0 * DEPTH_2) ** -0.25
RMS_EPS_2 = 1e-5


def alibi_slopes():
    h = jnp.arange(1, N_Q_HEADS + 1, dtype=jnp.float32)
    return jnp.exp2(-8.0 * h / N_Q_HEADS)

def sliding_window_attention(q, k, v, sinks):
    b, l, _ = q.shape
    nb = l // ATTN_BLOCK
    q = q.reshape(b, nb, ATTN_BLOCK, N_KV_HEADS, Q_PER_KV, HEAD_DIM)

    def band(t):
        t = t.reshape(b, l, N_KV_HEADS, HEAD_DIM)
        t = jnp.pad(t, ((0, 0), (ATTN_BLOCK, 0), (0, 0), (0, 0)))
        t = t.reshape(b, nb + 1, ATTN_BLOCK, N_KV_HEADS, HEAD_DIM)
        return jnp.concatenate([t[:, :-1], t[:, 1:]], axis=2)

    kb, vb = band(k), band(v)
    scores = jnp.einsum("bnqkgd,bnskd->bnkgqs", q, kb).astype(jnp.float32) * (HEAD_DIM ** -0.5)
    qi = jnp.arange(ATTN_BLOCK)[:, None]
    sj = jnp.arange(2 * ATTN_BLOCK)[None, :]
    dist = qi - sj + ATTN_BLOCK
    blk = jnp.arange(nb)[:, None, None]
    valid = (dist >= 0) & (dist < WINDOW) & (blk * ATTN_BLOCK + sj - ATTN_BLOCK >= 0)
    slopes = alibi_slopes().reshape(N_KV_HEADS, Q_PER_KV)[:, :, None, None]
    scores = scores - slopes * dist.astype(jnp.float32)
    scores = jnp.where(valid[None, :, None, None], scores, -jnp.inf)
    sink = sinks.astype(jnp.float32).reshape(N_KV_HEADS, Q_PER_KV)[:, :, None, None]
    m = jnp.maximum(scores.max(axis=-1, keepdims=True), sink)
    p = jnp.exp(scores - m)
    probs = (p / (p.sum(axis=-1, keepdims=True) + jnp.exp(sink - m))).astype(v.dtype)
    out = jnp.einsum("bnkgqs,bnskd->bnqkgd", probs, vb)
    return out.reshape(b, l, ATTN_WIDTH)

def causal_depthwise_conv(u, w, bias):
    out = lax.conv_general_dilated(u, w[:, None, :], window_strides=(1,),
                                   padding=[(CONV_WIDTH_2 - 1, 0)],
                                   dimension_numbers=("NWC", "WIO", "NWC"),
                                   feature_group_count=u.shape[-1])
    return out + bias

def exp_segsum(a_cs):
    n = a_cs.shape[-1]
    diff = a_cs[..., :, None] - a_cs[..., None, :]
    mask = jnp.tril(jnp.ones((n, n), dtype=bool))
    return jnp.exp(jnp.where(mask, diff, -jnp.inf))

def ssd_chunked(xs, dt, a, bm, cm):
    b, l, _ = xs.shape
    nc = l // CHUNK
    G, HG, P, N = N_SSM_GROUPS, SSM_HEADS_PER_GROUP, SSM_HEAD_DIM, D_STATE
    xc = xs.reshape(b, nc, CHUNK, G, HG, P)
    dtc = dt.reshape(b, nc, CHUNK, G, HG)
    bc = bm.reshape(b, nc, CHUNK, G, N)
    cc = cm.reshape(b, nc, CHUNK, G, N)
    a_cs = jnp.moveaxis(jnp.cumsum(dtc * a.reshape(G, HG), axis=2), 2, -1)
    xdt = xc * dtc[..., None]
    cb = jnp.einsum("bclgn,bcsgn->bcgls", cc, bc)
    y_diag = jnp.einsum("bcgls,bcghls,bcsghp->bclghp", cb, exp_segsum(a_cs), xdt)
    decay_to_end = jnp.exp(a_cs[..., -1:] - a_cs)
    states = jnp.einsum("bclgn,bcghl,bclghp->bcghpn", bc, decay_to_end, xdt)
    chunk_decay = jnp.exp(a_cs[..., -1])

    def step(carry, inp):
        st, dec = inp
        return carry * dec[..., None, None] + st, carry

    init = jnp.zeros(states.shape[:1] + states.shape[2:], states.dtype)
    _, prev = lax.scan(step, init, (jnp.moveaxis(states, 1, 0), jnp.moveaxis(chunk_decay, 1, 0)))
    prev = jnp.moveaxis(prev, 0, 1)
    y_off = jnp.einsum("bclgn,bcghpn,bcghl->bclghp", cc, prev, jnp.exp(a_cs))
    return (y_diag + y_off).astype(xs.dtype).reshape(b, l, D_INNER)

def gated_rmsnorm(y, z, w):
    b, l, _ = y.shape
    g = (y * jax.nn.silu(z)).astype(jnp.float32).reshape(b, l, N_SSM_GROUPS, D_INNER // N_SSM_GROUPS)
    g = g * lax.rsqrt(jnp.mean(g * g, axis=-1, keepdims=True) + RMS_EPS_2)
    return (g.reshape(b, l, D_INNER) * w.astype(jnp.float32)).astype(y.dtype)

def layer_norm_2(x, g, bias):
    xf = x.astype(jnp.float32)
    mu = jnp.mean(xf, axis=-1, keepdims=True)
    var = jnp.mean(jnp.square(xf - mu), axis=-1, keepdims=True)
    return ((xf - mu) * lax.rsqrt(var + LN_EPS) * g + bias).astype(x.dtype)

def hybrid_layer(x, w_in, conv_w, conv_b, dt_bias, a_log, d_skip, ssm_norm_w, sinks, w_out, ln_g, ln_b):
    b, l, _ = x.shape
    proj = jnp.einsum("bld,de->ble", x, w_in)
    q, k, v, z_attn, z_ssm, xbc, dt_raw = jnp.split(proj, IN_SPLITS, axis=-1)
    attn = sliding_window_attention(q, k, v, sinks) * jax.nn.silu(z_attn)
    xbc = jax.nn.silu(causal_depthwise_conv(xbc, conv_w, conv_b))
    xs, bm, cm = jnp.split(xbc, [D_INNER, D_INNER + N_SSM_GROUPS * D_STATE], axis=-1)
    dt = jax.nn.softplus(dt_raw.astype(jnp.float32) + dt_bias.astype(jnp.float32))
    a = -jnp.exp(a_log.astype(jnp.float32))
    y = ssd_chunked(xs, dt, a, bm, cm)
    y = y + (xs.reshape(b, l, N_SSM_HEADS, SSM_HEAD_DIM) * d_skip[:, None]).reshape(b, l, D_INNER)
    ssm = gated_rmsnorm(y, z_ssm, ssm_norm_w)
    out = jnp.einsum("ble,ed->bld", jnp.concatenate([attn, ssm], axis=-1), w_out)
    return layer_norm_2(DEEPNORM_ALPHA * x + out, ln_g, ln_b)

def second_inputs(seed: int = 0) -> dict:
    key = jax.random.key(seed)
    ks = jax.random.split(key, 12)
    f32 = jnp.float32
    x = jax.random.normal(ks[0], (BATCH, SEQ, D_MODEL), f32)
    w_in = jax.random.normal(ks[1], (DEPTH_2, D_MODEL, IN_WIDTH), f32) * D_MODEL ** -0.5
    conv_w = jax.random.normal(ks[2], (DEPTH_2, CONV_WIDTH_2, CONV_CH), f32) * CONV_WIDTH_2 ** -0.5
    conv_b = jax.random.normal(ks[3], (DEPTH_2, CONV_CH), f32) * 0.02
    dt0 = jnp.exp(jax.random.uniform(ks[4], (DEPTH_2, N_SSM_HEADS), f32) * (jnp.log(0.1) - jnp.log(0.001)) + jnp.log(0.001))
    dt_bias = dt0 + jnp.log(-jnp.expm1(-dt0))
    a_log = jnp.log(jax.random.uniform(ks[5], (DEPTH_2, N_SSM_HEADS), f32, 1.0, 16.0))
    d_skip = 1.0 + 0.1 * jax.random.normal(ks[6], (DEPTH_2, N_SSM_HEADS), f32)
    ssm_norm_w = 1.0 + 0.02 * jax.random.normal(ks[7], (DEPTH_2, D_INNER), f32)
    sinks = jax.random.normal(ks[8], (DEPTH_2, N_Q_HEADS), f32)
    w_out = jax.random.normal(ks[9], (DEPTH_2, MIX_WIDTH, D_MODEL), f32) * (MIX_WIDTH ** -0.5 * DEEPNORM_BETA)
    ln_g = 1.0 + 0.02 * jax.random.normal(ks[10], (DEPTH_2, D_MODEL), f32)
    ln_b = 0.02 * jax.random.normal(ks[11], (DEPTH_2, D_MODEL), f32)
    return {"x": x, "w_in": w_in, "conv_w": conv_w, "conv_b": conv_b, "dt_bias": dt_bias,
            "a_log": a_log, "d_skip": d_skip, "ssm_norm_w": ssm_norm_w, "sinks": sinks,
            "w_out": w_out, "ln_g": ln_g, "ln_b": ln_b}

def second_block(x, w_in, conv_w, conv_b, dt_bias, a_log, d_skip, ssm_norm_w, sinks, w_out, ln_g, ln_b):
    h = x
    for i in range(DEPTH_2):
        h = hybrid_layer(h, w_in[i], conv_w[i], conv_b[i], dt_bias[i], a_log[i], d_skip[i],
                         ssm_norm_w[i], sinks[i], w_out[i], ln_g[i], ln_b[i])
    return h


def setup_inputs(seed=0):
    out = dict(first_inputs(seed))
    for name, value in second_inputs(seed + 1).items():
        if name != "x":
            out[name + "_2"] = value
    return out


def reference(
    x, c, ada_w, ada_b, mix_pre_g, mix_post_g, w_in, conv_dw_w, conv_dw_b, conv_ln_g, conv_ln_b,
    rwkv_mu, w0, w2, a0, a2, g2, k_k, k_a, r_k, lnx_g, lnx_b, w_out, ffn_pre_g, ffn_post_g,
    w_up, ffn_dw_w, ffn_dw_b, w_down, w_in_2, conv_w_2, conv_b_2, dt_bias_2, a_log_2, d_skip_2,
    ssm_norm_w_2, sinks_2, w_out_2, ln_g_2, ln_b_2,
):
    x = first_block(
        x, c, ada_w, ada_b, mix_pre_g, mix_post_g, w_in, conv_dw_w, conv_dw_b, conv_ln_g,
        conv_ln_b, rwkv_mu, w0, w2, a0, a2, g2, k_k, k_a, r_k, lnx_g, lnx_b, w_out, ffn_pre_g,
        ffn_post_g, w_up, ffn_dw_w, ffn_dw_b, w_down,
    )
    return second_block(
        x, w_in_2, conv_w_2, conv_b_2, dt_bias_2, a_log_2, d_skip_2, ssm_norm_w_2, sinks_2,
        w_out_2, ln_g_2, ln_b_2,
    )


_drawn_inputs = setup_inputs


def setup_inputs(seed=0):
    import zlib

    import numpy as np

    out = dict(_drawn_inputs(seed))
    spreads = {}
    factors = {'mix_post_g': 3.131,
     'conv_dw_b': 6.601,
     'conv_ln_g': 3.947,
     'conv_ln_b': 8.0,
     'w2': 4.409,
     'k_k': 4.347,
     'k_a': 3.777,
     'lnx_g': 5.781,
     'lnx_b': 8.0,
     'ffn_pre_g': 2.762,
     'ffn_post_g': 3.897,
     'ffn_dw_b': 6.919,
     'conv_b_2': 5.768,
     'd_skip_2': 2.752,
     'ssm_norm_w_2': 8.0,
     'sinks_2': 5.386}
    for name, (base, spread) in spreads.items():
        noise = np.random.default_rng([zlib.crc32(name.encode()), seed]).standard_normal(out[name].shape)
        drawn = base * np.exp(spread * noise) if base else spread * noise
        out[name] = __import__('jax').numpy.asarray(drawn.astype(out[name].dtype))
    for name, factor in factors.items():
        out[name] = (out[name] * factor).astype(out[name].dtype)
    return out
```

```python
from collections import namedtuple
from contextlib import ExitStack

import numpy as np

import concourse.bass as bass
from concourse import mybir

F32 = mybir.dt.float32
ACT = mybir.ActivationFunctionType
ALU = mybir.AluOpType
AX = mybir.AxisListType.X

P = 128
T = 1024
D = 1024
TT = T // P
KT = D // P
NH = T // 2
CW = 512
CT = CW // P
CONV_K = 31
CPAD = CONV_K - 1
HD = 64
RH = CW // HD
LORA = 64
GLORA = 160
CH = 64
BLK = 16
D_FF = 2816
FT = D_FF // P
RMS_EPS, LN_EPS, LNX_EPS, RMS_EPS_2 = 1e-6, 1e-5, 64e-5, 1e-5
DECAY = float(np.exp(-0.5))

LAYERS = 2
QH, KVH = 16, 4
KVW = KVH * HD
DI = 1024
SH = DI // HD
SG = 2
HG = SH // SG
NS = 128
XBC = DI + 2 * SG * NS
XT = XBC // P
O_Q, O_K, O_V, O_ZA = 0, D, D + KVW, D + 2 * KVW
O_ZS = O_ZA + D
O_XBC = O_ZS + DI
O_DT = O_XBC + XBC
IN_W = O_DT + SH
ALPHA = (2.0 * LAYERS) ** 0.25
CK2 = 4

COLS = {}
for _name, _n in [
    ("c", KT), ("ada_b", 4 * KT), ("pre_g", 2 * KT), ("mu", 15), ("conv_b", CT), ("conv_ln_g", CT),
    ("conv_ln_b", CT), ("w0", CT), ("a0", CT), ("k_k", CT), ("k_a", CT), ("r_k", CT),
    ("conv_w", CT * CONV_K), ("ffn_b", 2 * FT), ("ffn_w", 2 * FT * 3),
    ("conv_b_2", LAYERS * XT), ("conv_w_2", LAYERS * XT * CK2),
]:
    COLS[_name] = (sum(n for _, n in COLS.values()), _n)
NCOLS = sum(n for _, n in COLS.values())

CONSTS = {}
for _name, _n in [
    ("ident", P), ("ones", P), ("headones", P), ("mask_incl_up", P), ("mask_diag_up", P), ("mask_incl_up_2", P), ("mask_strict_up", P),
    ("mask_diag_low", P), ("mask_off_low", P), ("chunk_row", T), ("tri", P), ("neg_up", P), ("minus_last", P),
    ("ident_heads", HD),
]:
    CONSTS[_name] = (sum(n for _, n in CONSTS.values()), _n)
NCONSTS = sum(n for _, n in CONSTS.values())


def shape_constants():
    i, j = np.arange(P)[:, None], np.arange(P)[None, :]
    chunk = (i // CH) == (j // CH)
    block = (i // BLK) == (j // BLK)
    parts = {
        "ident": i == j, "ones": i >= 0 * j, "headones": (i // HD) == (j // HD),
        "mask_diag_up": block & (i < j), "mask_incl_up": chunk & (i <= j), "mask_strict_up": chunk & (i < j),
        "mask_incl_up_2": chunk & (i <= j), "ident_heads": (i % HD) == np.arange(HD)[None, :],
        "mask_diag_low": block & (i > j), "mask_off_low": chunk & ~block & (i > j),
        "chunk_row": np.broadcast_to(np.arange(T) % CH != 0, (P, T)), "tri": i <= j,
        "neg_up": np.where(i > j, -1e30, 0.0), "minus_last": np.where((i == P - 1) & (j >= 0), -1.0, 0.0),
    }
    consts = np.concatenate([np.asarray(parts[n]).astype(np.float32) for n in CONSTS], axis=1)
    q, s = np.arange(P)[:, None], np.arange(2 * P)[None, :]
    dist = q - s + P
    slopes = 2.0 ** (-8.0 * np.arange(1, QH + 1) / QH)
    alibi = np.where((dist >= 0) & (dist < P), -8.0 * slopes[:, None, None] * dist, -1e30)
    return consts, np.ascontiguousarray(alibi.transpose(1, 0, 2).astype(np.float32))


def flat(ap):
    return ap.rearrange("p a b -> p (a b)")


def alloc(m, ctx, name, shape):
    m.tensors += 1
    return ctx.enter_context(m.nc.sbuf_tensor(f"{name}_sb{m.tensors}", shape, F32))


class Machine:

    def __init__(self, nc, t):
        self.nc, self.t = nc, t
        self.ctx = ExitStack()
        self.tensors = 0
        self.phases = 0
        self.used = []


def make(nc, t):
    m = Machine(nc, t)
    sb = lambda name, shape: alloc(m, m.ctx, name, shape)
    m.PS = m.ctx.enter_context(nc.psum_tensor("PS", [P, 8, 512], F32))
    m.cols = sb("cols", [P, NCOLS])
    m.consts = sb("consts", [P, NCONSTS])
    m.mod_shift = sb("mod_shift", [P, 2, KT])
    m.mod_scale = sb("mod_scale", [P, 2, KT])
    m.small = sb("small", [P, 64])
    m.HT = sb("HT", [P, KT, T])
    m.col = lambda name, k=0, n=1: m.cols[:, COLS[name][0] + k:COLS[name][0] + k + n]
    m.const = lambda name: m.consts[:, CONSTS[name][0]:CONSTS[name][0] + CONSTS[name][1]]
    return m


class Chain:

    def __init__(self, eng, sem):
        self.eng, self.sem, self.n = eng, sem, 0

    def __call__(self, ins):
        self.n += 1
        ins.then_inc(self.sem, 1)
        self.eng.wait_ge(self.sem, self.n)


def phase(m, names):
    m.phases += 1
    handles = [m.nc.alloc_semaphore(f"{n}_{m.phases}") for n in names.split()]
    m.used += handles
    return namedtuple("Signals", names)(*handles)


def recycle(m):
    m.nc.clear_and_free_semaphores(m.used)
    m.used = []
    m.nc.all_engine_barrier()


def modulation(m, X, GM):
    nc, t, PS = m.nc, m.t, m.PS
    with ExitStack() as ctx:
        W = alloc(m, ctx, "ada_slots", [P, 3, KT, 512])
        rows = alloc(m, ctx, "gate_rows", [P, 2, 2, D])
        silu_c = alloc(m, ctx, "silu_c", [P, KT])
        silu_cb = alloc(m, ctx, "silu_cb", [P, KT, P])
        biased = alloc(m, ctx, "biased", [P, 2, 2 * KT])
        s = phase(m, "par_in x_in rows_in w_in0 w_in1 w_in2 slot_free silu silub col_done row_done biased scaled gate")
        w_in = [s.w_in0, s.w_in1, s.w_in2]
        block = ctx.enter_context(nc.Block())

        @block.sync
        def _(sp):
            sp.dma_start(m.cols[:], t.cols).then_inc(s.par_in, 16)
            sp.dma_start(m.consts[:], t.consts).then_inc(s.par_in, 16)
            with sp.Fori(0, 2) as i:
                at = [sp.snap(i * (3 * D) + b * 512) for b in range(6)]
                for b in range(6):
                    sp.wait_ge(s.slot_free, i * 6 + b + 1)
                    sp.dma_start(W[:, b % 3], t.ada_w[:, bass.ds(at[b], 512)].rearrange("(k p) n -> p k n", p=P)
                                 ).then_inc(w_in[b % 3], 16)

        @block.gpsimd
        def _(pool):
            for i, g in enumerate((t.mix_post_g, t.ffn_post_g)):
                pool.dma_start(rows[:, i, 0], t.ada_b[:, (3 * i + 2) * D:(3 * i + 3) * D].to_broadcast([P, D])
                               ).then_inc(s.rows_in, 16)
                pool.dma_start(rows[:, i, 1], g.to_broadcast([P, D])).then_inc(s.rows_in, 16)

        @block.scalar
        def _(act):
            for k in range(TT):
                act.dma_start(X[:, k], t.x[k * P:(k + 1) * P]).then_inc(s.x_in, 16)
            act.wait_ge(s.par_in, 32)
            nc.scalar.activation(silu_c[:], m.col("c", 0, KT), ACT.Silu).then_inc(s.silu, 1)

        @block.vector
        def _(dve):
            dve.wait_ge(s.silu, 1)
            for k in range(KT):
                nc.vector.tensor_scalar(silu_cb[:, k], m.const("ones"), silu_c[:, k:k + 1], None, ALU.mult
                                        ).then_inc(s.silub, 1)
            dve.wait_ge(s.col_done, 2)
            nc.vector.tensor_tensor(flat(biased[:]), PS[:, 0, 0:4 * KT], m.col("ada_b", 0, 4 * KT), ALU.add
                                    ).then_inc(s.biased, 1)
            dve.wait_ge(s.biased, 1)
            nc.vector.tensor_copy(m.mod_shift[:], biased[:, :, 0:KT]).then_inc(s.scaled, 1)
            nc.vector.scalar_tensor_tensor(out=m.mod_scale[:], in0=biased[:, :, KT:2 * KT], scalar=1.0,
                                           in1=m.col("pre_g", 0, 2 * KT).rearrange("p (a b) -> p a b", a=2),
                                           op0=ALU.add, op1=ALU.mult).then_inc(s.scaled, 1)
            dve.wait_ge(s.rows_in, 64)
            dve.wait_ge(s.x_in, 16 * TT)
            dve.wait_ge(s.row_done, 2)
            for i in range(2):
                nc.vector.tensor_tensor(GM[:, i], flat(PS[:, 2 + 2 * i:4 + 2 * i]), rows[:, i, 0], ALU.add
                                        ).then_inc(s.gate, 1)
            dve.wait_ge(s.gate, 2)
            for i in range(2):
                nc.vector.tensor_tensor(GM[:, i], GM[:, i], rows[:, i, 1], ALU.mult).then_inc(s.gate, 1)

        @block.tensor
        def _(pe):
            pe.sem_inc(s.slot_free, 3)
            pe.wait_ge(s.silub, KT)
            with pe.Fori(0, 2) as i:
                for b in range(6):
                    pe.wait_ge(w_in[b % 3], (i * 2 + b // 3 + 1) * 16)
                    if b < 4:
                        for j in range(4):
                            for k in range(KT):
                                last = pe.matmul(PS[:, 0, bass.ds(i * 16 + b * 4 + j, 1)],
                                                 W[:, b % 3, k, j * P:(j + 1) * P], silu_c[:, k:k + 1],
                                                 start=k == 0, stop=k == KT - 1)
                        if b == 3:
                            last.then_inc(s.col_done, 1)
                            pe.wait_ge(s.col_done, i + 1)
                            pe.sem_inc(s.slot_free, 1)
                            continue
                    else:
                        for k in range(KT):
                            last = pe.matmul(PS[:, bass.ds(i * 2 + b - 2, 1), :], silu_cb[:, k], W[:, b % 3, k],
                                             start=k == 0, stop=k == KT - 1)
                        if b == 5:
                            last.then_inc(s.row_done, 1)
                            pe.wait_ge(s.row_done, i + 1)
                            pe.sem_inc(s.slot_free, 1)
                            continue
                    last.then_inc(s.slot_free, 1)


def to_channels(m, X, norm=None):
    nc, PS, HT = m.nc, m.PS, m.HT
    with ExitStack() as ctx:
        src = X
        if norm is not None:
            src = alloc(m, ctx, "normed", [P, TT, D])
        s = phase(m, "sq eps rms rstd normed turned ev_act ev_dve")
        block = ctx.enter_context(nc.Block())
        ss, rstd, eps = m.small[:, 0:TT], m.small[:, TT:2 * TT], m.small[:, 2 * TT:2 * TT + 1]

        @block.tensor
        def _(pe):
            for half in range(2):
                if norm is not None:
                    pe.wait_ge(s.normed, 4 * half + 4)
                for k in range(KT):
                    if half:
                        pe.wait_ge(s.ev_dve if k % 2 else s.ev_act, k // 2 + 1)
                    for j in range(4):
                        last = pe.transpose(PS[:, k, j * P:(j + 1) * P],
                                            src[:, 4 * half + j, k * P:(k + 1) * P], m.const("ident"))
                    last.then_inc(s.turned, 1)

        @block.scalar
        def _(act):
            if norm is not None:
                for k in range(TT):
                    nc.scalar.activation(src[:, k], X[:, k], ACT.Square, accum_out=ss[:, k:k + 1]).then_inc(s.sq, 1)
                act.wait_ge(s.sq, TT)
                act.wait_ge(s.eps, 1)
                nc.scalar.activation(rstd, ss, ACT.Sqrt, scale=1.0 / D, bias=eps).then_inc(s.rms, 1)
            for n in range(0, 2 * KT, 2):
                half, k = n // KT, n % KT
                act.wait_ge(s.turned, n + 1)
                out = HT[:, k, half * NH:(half + 1) * NH]
                if norm is None:
                    nc.scalar.copy(out, PS[:, k, :]).then_inc(s.ev_act, 1)
                else:
                    nc.scalar.activation(out, PS[:, k, :], ACT.Identity, scale=m.mod_scale[:, norm, k:k + 1],
                                         bias=m.mod_shift[:, norm, k:k + 1]).then_inc(s.ev_act, 1)

        @block.vector
        def _(dve):
            if norm is not None:
                nc.vector.memset(eps, RMS_EPS).then_inc(s.eps, 1)
                dve.wait_ge(s.rms, 1)
                nc.vector.reciprocal(rstd, rstd).then_inc(s.rstd, 1)
                dve.wait_ge(s.rstd, 1)
                for k in range(TT):
                    nc.vector.tensor_scalar(src[:, k], X[:, k], rstd[:, k:k + 1], None, ALU.mult
                                            ).then_inc(s.normed, 1)
            for n in range(1, 2 * KT, 2):
                half, k = n // KT, n % KT
                dve.wait_ge(s.turned, n + 1)
                out = HT[:, k, half * NH:(half + 1) * NH]
                if norm is None:
                    nc.vector.tensor_copy(out, PS[:, k, :]).then_inc(s.ev_dve, 1)
                else:
                    nc.vector.tensor_scalar(out, PS[:, k, :], m.mod_scale[:, norm, k:k + 1],
                                            m.mod_shift[:, norm, k:k + 1], ALU.mult, ALU.add).then_inc(s.ev_dve, 1)


def tile_product(m, pe, W, slot, c, bank, width=P):
    for half in range(2):
        for k in range(KT):
            last = pe.matmul(m.PS[0:width, 2 * bank + half, :], W[:, slot, k, c * P:c * P + width],
                             m.HT[:, k, half * NH:(half + 1) * NH], start=k == 0, stop=k == KT - 1)
    return last


def bank2(m, b, rows=P):
    return m.PS[0:rows, 2 * b:2 * b + 2, :].rearrange("p a b -> p (a b)")


def in_projection(m, MIX, RKVQ, LO, W):
    nc, t, PS = m.nc, m.t, m.PS
    with ExitStack() as ctx:
        U = alloc(m, ctx, "U", [P, CT, T + 32])
        sig = alloc(m, ctx, "sig", [P, 2, T])
        om = alloc(m, ctx, "one_minus_mu", [P, 15])
        s = phase(m, "w_in0 w_in1 slot_free tile_done ps_free om pad gated part conv lora")
        w_in = [s.w_in0, s.w_in1]
        block = ctx.enter_context(nc.Block())
        mu = lambda k: m.col("mu", k)

        def load(sp, slot, c, at, width=P):
            sp.dma_start(W[:, slot, :, c * P:c * P + width],
                         t.w_in[:, bass.ds(at, width)].rearrange("(k p) n -> p k n", p=P)).then_inc(w_in[slot], 16)

        @block.sync
        def _(sp):
            with sp.Fori(0, 2) as i:
                at = [[sp.snap(i * 2 * P + j * P + c * CW) for c in range(2)] for j in range(2)]
                for j in range(2):
                    sp.wait_ge(s.slot_free, i * 2 + j + 1)
                    for c in range(2):
                        load(sp, j, c, at[j][c])
            with sp.Fori(0, 3) as i:
                at = [[sp.snap(i * CW + (2 * j + c) * P + 2 * CW) for c in range(2)] for j in range(2)]
                for j in range(2):
                    sp.wait_ge(s.slot_free, i * 2 + j + 5)
                    for c in range(2):
                        load(sp, j, c, at[j][c])
            base = 5 * CW
            sp.wait_ge(s.slot_free, 11)
            load(sp, 0, 0, base)
            load(sp, 0, 1, base + P)
            sp.wait_ge(s.slot_free, 12)
            load(sp, 1, 0, base + 2 * P, 32)

        @block.tensor
        def _(pe):
            pe.sem_inc(s.slot_free, 2)
            with pe.Fori(0, 5) as i:
                for j in range(2):
                    pe.wait_ge(w_in[j], (i + 1) * 32)
                    for c in range(2):
                        pe.wait_ge(s.ps_free, i * 4 + 2 * j + c + 1)
                        tile_product(m, pe, W, j, c, 2 * j + c).then_inc(s.tile_done, 1)
                    pe.wait_ge(s.tile_done, i * 4 + 2 * j + 2)
                    pe.sem_inc(s.slot_free, 1)
            for n, (j, c, width) in enumerate(((0, 0, P), (0, 1, P), (1, 0, 32))):
                if c == 0:
                    pe.wait_ge(w_in[j], 5 * 32 + (32 if j == 0 else 16))
                pe.wait_ge(s.ps_free, 20 + n + 1)
                tile_product(m, pe, W, j, c, n, width).then_inc(s.tile_done, 1)

        @block.scalar
        def _(act):
            with act.Fori(0, 2) as i:
                for j in range(2):
                    act.wait_ge(s.tile_done, i * 4 + 2 * j + 2)
                    act.wait_ge(s.ps_free, i * 4 + 2 * j + 2)
                    nc.scalar.activation(sig[:, j], bank2(m, 2 * j + 1), ACT.Sigmoid).then_inc(s.gated, 1)
            act.wait_ge(s.om, 1)
            with act.Fori(0, 3) as i:
                for j in range(4):
                    act.wait_ge(s.tile_done, i * 4 + j + 9)
                    nc.scalar.activation(RKVQ[:, bass.ds(i * 4 + j, 1), :].rearrange("p a b -> p (a b)"),
                                         bank2(m, j), ACT.Identity, scale=om[:, bass.ds(i * 4 + j, 1)]
                                         ).then_inc(s.part, 1)
            for n in range(3):
                rows = 32 if n == 2 else P
                act.wait_ge(s.tile_done, 21 + n)
                nc.scalar.activation(LO[0:rows, n], bank2(m, n, rows), ACT.Identity,
                                     scale=om[0:rows, 12 + n:13 + n]).then_inc(s.part, 1)
            for n in range(3):
                rows = (LORA, P, 32)[n]
                act.wait_ge(s.lora, n + 1)
                nc.scalar.activation(LO[0:rows, n], LO[0:rows, n], ACT.Sigmoid if n else ACT.Tanh)

        @block.vector
        def _(dve):
            dve.sem_inc(s.ps_free, 4)
            nc.vector.tensor_scalar(om[:], m.col("mu", 0, 15), -1.0, 1.0, ALU.mult, ALU.add).then_inc(s.om, 1)
            nc.vector.memset(U[:, :, 0:CPAD], 0.0).then_inc(s.pad, 1)
            with dve.Fori(0, 2) as i:
                for j in range(2):
                    dve.wait_ge(s.gated, i * 2 + j + 1)
                    u = U[:, bass.ds(i * 2 + j, 1), CPAD:CPAD + T].rearrange("p a b -> p (a b)")
                    nc.vector.tensor_tensor(u, bank2(m, 2 * j), sig[:, j], ALU.mult).then_inc(s.ps_free, 2)
            dve.wait_ge(s.pad, 1)

            def conv(q, first):
                out = MIX[:, bass.ds(q, 1), :].rearrange("p a b -> p (a b)")
                for k in range(CONV_K):
                    u = U[:, bass.ds(q, 1), k:k + T].rearrange("p a b -> p (a b)")
                    w = m.cols[:, bass.ds(q * CONV_K + COLS["conv_w"][0] + k, 1)]
                    if k == 0:
                        ins = nc.vector.tensor_scalar(out, u, w, m.cols[:, bass.ds(q + COLS["conv_b"][0], 1)],
                                                      ALU.mult, ALU.add)
                    else:
                        ins = nc.vector.scalar_tensor_tensor(out=out, in0=u, scalar=w, in1=out,
                                                             op0=ALU.mult, op1=ALU.add)
                    ins.then_inc(s.conv, 1)
                    dve.wait_ge(s.conv, first + k + 1)

            with dve.Fori(0, 3) as i:
                for j in range(4):
                    dve.wait_ge(s.part, i * 4 + j + 1)
                    row = RKVQ[:, bass.ds(i * 4 + j, 1), 1:T].rearrange("p a b -> p (a b)")
                    nc.vector.scalar_tensor_tensor(out=row, in0=bank2(m, j)[:, 0:T - 1],
                                                   scalar=m.cols[:, bass.ds(i * 4 + COLS["mu"][0] + j, 1)], in1=row,
                                                   op0=ALU.mult, op1=ALU.add).then_inc(s.ps_free, 1)
                conv(i, i * CONV_K)
            for n in range(3):
                rows = 32 if n == 2 else P
                dve.wait_ge(s.part, 12 + n + 1)
                nc.vector.scalar_tensor_tensor(out=LO[0:rows, n, 1:T], in0=bank2(m, n, rows)[:, 0:T - 1],
                                               scalar=m.col("mu", 12 + n)[0:rows], in1=LO[0:rows, n, 1:T],
                                               op0=ALU.mult, op1=ALU.add).then_inc(s.lora, 1)
            conv(3, 3 * CONV_K)


def conv_branch(m, MIX):
    nc, PS = m.nc, m.PS
    with ExitStack() as ctx:
        mean = alloc(m, ctx, "mean", [P, T])
        rstd = alloc(m, ctx, "rstd", [P, T])
        sq = alloc(m, ctx, "squares", [P, CT, T])
        s = phase(m, "eps sums mean centred sq vars root chain out")
        block = ctx.enter_context(nc.Block())
        eps = m.small[:, 0:1]

        @block.tensor
        def _(pe):
            def sum_tiles(src, bank):
                for half in range(2):
                    for q in range(CT):
                        last = pe.matmul(PS[:, 2 * bank + half, :], m.const("ones"),
                                         src[:, q, half * NH:(half + 1) * NH], start=q == 0, stop=q == CT - 1)
                last.then_inc(s.sums, 1)

            sum_tiles(MIX, 0)
            pe.wait_ge(s.sq, CT)
            sum_tiles(sq, 1)

        @block.scalar
        def _(act):
            act.wait_ge(s.sums, 1)
            nc.scalar.mul(mean[:], bank2(m, 0), 1.0 / CW).then_inc(s.mean, 1)
            for q in range(CT):
                act.wait_ge(s.centred, q + 1)
                nc.scalar.activation(sq[:, q], MIX[:, q], ACT.Square).then_inc(s.sq, 1)
            act.wait_ge(s.sums, 2)
            act.wait_ge(s.eps, 1)
            nc.scalar.activation(rstd[:], bank2(m, 1), ACT.Sqrt, scale=1.0 / CW, bias=eps).then_inc(s.root, 1)
            for q in range(CT):
                act.wait_ge(s.out, q + 1)
                nc.scalar.activation(MIX[:, q], MIX[:, q], ACT.Silu, scale=m.col("conv_ln_g", q),
                                     bias=m.col("conv_ln_b", q))

        @block.vector
        def _(dve):
            nc.vector.memset(eps, LN_EPS).then_inc(s.eps, 1)
            dve.wait_ge(s.mean, 1)
            for q in range(CT):
                nc.vector.tensor_tensor(MIX[:, q], MIX[:, q], mean[:], ALU.subtract).then_inc(s.centred, 1)
            dve.wait_ge(s.root, 1)
            nc.vector.reciprocal(rstd[:], rstd[:]).then_inc(s.chain, 1)
            dve.wait_ge(s.chain, 1)
            for q in range(CT):
                nc.vector.tensor_tensor(MIX[:, q], MIX[:, q], rstd[:], ALU.mult).then_inc(s.out, 1)


def rwkv_operands(m, RKVQ, LO, G2, A, CS, PC, bonus):
    nc, t, PS = m.nc, m.t, m.PS
    with ExitStack() as ctx:
        WA = alloc(m, ctx, "lora_w", [P, CW])
        rk_col = alloc(m, ctx, "rk_col", [P, CT, 2])
        om = alloc(m, ctx, "one_minus_ka", [P, CT])
        sq = alloc(m, ctx, "key_squares", [P, 2, T])
        nrm = alloc(m, ctx, "key_norm", [P, 2, T])
        tmp = alloc(m, ctx, "tmp", [P, 2, T])
        ex = alloc(m, ctx, "exps", [P, 3, T])
        SG_ = CS
        s = phase(m, "w_in g_in z sig sq ss root kkn scan dif e1 e2 e3 rk bonus cd cdb e3_used chain small ks")
        block = ctx.enter_context(nc.Block())
        R = lambda q: RKVQ[:, q]
        K = lambda q: RKVQ[:, CT + q]
        Q = lambda q: RKVQ[:, 3 * CT + q]

        @block.sync
        def _(sp):
            sp.dma_start(WA[0:LORA], t.w2).then_inc(s.w_in, 16)
            sp.dma_start(WA[LORA:P], t.a2).then_inc(s.w_in, 16)
            sp.dma_start(G2[:, 0], t.g2[0:P]).then_inc(s.g_in, 16)
            sp.dma_start(G2[0:GLORA - P, 1], t.g2[P:GLORA]).then_inc(s.g_in, 16)
            sp.wait_ge(s.g_in, 32)

        @block.tensor
        def _(pe):
            pe.wait_ge(s.w_in, 32)
            for q in range(CT):
                if q >= 2:
                    pe.wait_ge(s.sig, 2 * (q - 1))
                for side in range(2):
                    for half in range(2):
                        last = pe.matmul(PS[:, 4 * (q % 2) + 2 * side + half, :],
                                         WA[LORA * side:LORA * side + LORA, q * P:(q + 1) * P],
                                         LO[LORA * side:LORA * side + LORA, 0, half * NH:(half + 1) * NH],
                                         start=True, stop=True)
                last.then_inc(s.z, 1)
            for q in range(CT):
                pe.wait_ge(s.sq, q + 1)
                pe.wait_ge(s.sig, 2 * CT)
                if q >= 2:
                    pe.wait_ge(s.root, q - 1)
                for half in range(2):
                    last = pe.matmul(PS[:, 2 * (q % 2) + half, :], m.const("headones"),
                                     sq[:, q % 2, half * NH:(half + 1) * NH], start=True, stop=True)
                last.then_inc(s.ss, 1)
            for q in range(CT):
                pe.wait_ge(s.rk, q + 1)
                for k in range(TT):
                    last = pe.matmul(PS[:, 4, k * RH + 2 * q:k * RH + 2 * q + 2], tmp[:, q % 2, k * P:(k + 1) * P],
                                     rk_col[:, q], start=True, stop=True)
                last.then_inc(s.bonus, 1)

        @block.scalar
        def _(act):
            for q in range(CT):
                act.wait_ge(s.z, q + 1)
                nc.scalar.activation(SG_[:, q], bank2(m, 2 * (q % 2)), ACT.Sigmoid, bias=m.col("w0", q)
                                     ).then_inc(s.sig, 1)
                nc.scalar.activation(A[:, q], bank2(m, 2 * (q % 2) + 1), ACT.Sigmoid, bias=m.col("a0", q)
                                     ).then_inc(s.sig, 1)
            for q in range(CT):
                if q >= 2:
                    act.wait_ge(s.ss, q - 1)
                nc.scalar.activation(sq[:, q % 2], K(q), ACT.Square, scale=m.col("k_k", q)).then_inc(s.sq, 1)
                if q >= 2:
                    act.wait_ge(s.kkn, q - 1)
                act.wait_ge(s.ss, q + 1)
                nc.scalar.activation(nrm[:, q % 2], bank2(m, q % 2), ACT.Sqrt).then_inc(s.root, 1)
            for q in range(CT):
                if q:
                    act.wait_ge(s.e3_used, q)
                act.wait_ge(s.dif, q + 1)
                nc.scalar.activation(ex[:, 0], tmp[:, q % 2], ACT.Exp, scale=-DECAY).then_inc(s.e1, 1)
                nc.scalar.activation(ex[:, 1], CS[:, q], ACT.Exp, scale=DECAY).then_inc(s.e2, 1)
                nc.scalar.activation(ex[:, 2], CS[:, q], ACT.Exp, scale=-DECAY).then_inc(s.e3, 1)

        @block.vector
        def _(dve):
            do = Chain(dve, s.chain)
            v = nc.vector
            do(v.tensor_scalar(om[:], m.col("k_a", 0, CT), -1.0, 1.0, ALU.mult, ALU.add))
            do(v.tensor_tensor(rk_col[:], m.col("r_k", 0, CT).unsqueeze(2).to_broadcast([P, CT, 2]),
                               m.const("headones")[:, 0:P:HD].unsqueeze(1).to_broadcast([P, CT, 2]), ALU.mult))
            for q in range(CT):
                v.tensor_scalar(Q(q), K(q), m.col("k_k", q), None, ALU.mult)
                dve.wait_ge(s.root, q + 1)
                n = nrm[:, q % 2]
                do(v.tensor_scalar(n, n, 1e-12, None, ALU.max))
                do(v.reciprocal(n, n))
                v.tensor_tensor(Q(q), Q(q), n, ALU.mult).then_inc(s.kkn, 1)
            for q in range(CT):
                if q >= 2:
                    dve.wait_ge(s.bonus, q - 1)
                do(v.tensor_scalar(tmp[:, q % 2], A[:, q], m.col("k_a", q), om[:, q:q + 1], ALU.mult, ALU.add))
                do(v.tensor_tensor(K(q), K(q), tmp[:, q % 2], ALU.mult))
                v.tensor_tensor(tmp[:, q % 2], R(q), K(q), ALU.mult).then_inc(s.rk, 1)
            for q in range(CT):
                d = tmp[:, q % 2]
                if q < 2:
                    dve.wait_ge(s.bonus, q + 3)
                do(v.tensor_copy(d, SG_[:, q]))
                do(v.tensor_tensor_scan(CS[:, q], m.const("chunk_row"), d, 0.0, ALU.mult, ALU.add))
                if q >= 2:
                    dve.wait_ge(s.e1, q - 1)
                v.tensor_tensor(d, CS[:, q], d, ALU.subtract).then_inc(s.dif, 1)
                do(v.scalar_tensor_tensor(out=A[:, q], in0=A[:, q], scalar=-1.0, in1=Q(q), op0=ALU.mult,
                                          op1=ALU.mult))
                dve.wait_ge(s.e1, q + 1)
                v.tensor_tensor(Q(q), Q(q), ex[:, 0], ALU.mult)
                dve.wait_ge(s.e2, q + 1)
                v.tensor_tensor(A[:, q], A[:, q], ex[:, 1], ALU.mult)
                v.tensor_tensor(K(q), K(q), ex[:, 1], ALU.mult)
                dve.wait_ge(s.e3, q + 1)
                v.tensor_copy(PC[:, q], ex[:, 2, CH - 1::CH])
                v.tensor_tensor(R(q), R(q), ex[:, 2], ALU.mult).then_inc(s.e3_used, 1)
            v.tensor_copy(bonus[:], PS[:, 4, 0:TT * RH])


def rwkv_recurrence(m, RKVQ, A, PC, LO, G2, bonus):
    nc, t, PS = m.nc, m.t, m.PS
    HB = 4
    with ExitStack() as ctx:
        tok = m.HT[:, 4:6].rearrange("p a (g i c) -> p (a g) i c", g=1, i=4)
        BR = m.HT[:, 6:8].rearrange("p g (h a c) -> p g h a c", h=HB, a=2)
        GR = alloc(m, ctx, "k_products", [P, 2, HB, 2, P])
        ND = alloc(m, ctx, "n_blocks", [P, 2, HB, P])
        NE = alloc(m, ctx, "n_rest", [P, 2, HB, P])
        P2 = alloc(m, ctx, "power2", [P, 2, 2, HB, P])
        P4 = alloc(m, ctx, "power4", [P, 2, 2, HB, P])
        IB = alloc(m, ctx, "block_inverse", [P, 2, HB, P])
        P8 = P2[:, :, 0]
        XR = P4[:, :, 0]
        FR = P4[:, :, 1]
        ZZ = ND
        WU = P2[:, :, 1]
        MT = alloc(m, ctx, "transition", [P, 2, 2, 2, HD])
        ZT = alloc(m, ctx, "read_out", [P, CT, P])
        S = alloc(m, ctx, "state", [P, CT, HD])
        Y = alloc(m, ctx, "y", [P, CW])
        Y2 = alloc(m, ctx, "y_tmp", [P, CW])
        VB = alloc(m, ctx, "v_bonus", [P, 2, CW])
        GT = alloc(m, ctx, "gate", [P, CW])
        LNX = alloc(m, ctx, "lnx_rows", [P, 2, CW])
        st = alloc(m, ctx, "stats", [P, 4, RH])
        s = phase(m, "rows_in pe order act dve pool eps chain achain init squared y_ready y_out mean_ready")
        block = ctx.enter_context(nc.Block())

        inner = [("TRa", "act"), ("TRb", "act"), ("PBa", "dve"), ("PBb", "dve"), ("N", "dve"), ("PGa", "dve"),
                 ("PGb", "dve"), ("SQ1a", "dve"), ("SQ1b", "act"), ("AP1", "dve"), ("SQ2a", "dve"),
                 ("SQ2b", "act"), ("AP2", "dve"), ("SQ3", "act"), ("GV", "act"), ("AP3", "dve"), ("FR", "act"),
                 ("Z", "act"), ("H1", "dve"), ("H2", "dve"), ("H3", "dve"), ("MT", "dve"), ("ZT", "dve")]
        plan = []
        for k in range(TT):
            for n, (name, eng) in enumerate(inner):
                plan += [(k, g, name, eng, 3 * g + n % 3) for g in range(2)]
                if name == "GV" and k:
                    plan.append((k - 1, 0, "YT", "act", 3 * 0 + (n + 1) % 3))
            plan += [(k, 0, "S0", "dve", 7), (k, 0, "S1", "dve", 7), (k, 0, "Y", "dve", 6), (k, 0, "GT", "act", 0)]
        plan.append((TT - 1, 0, "YT", "act", 1))
        count, filled, emptied, before, last_in = {"act": 0, "dve": 0}, {}, {}, {}, {}
        for n, (k, g, name, eng, bank) in enumerate(plan):
            count[eng] += 1
            key = (k, g, name)
            filled[key], emptied[key], before[key] = n + 1, (eng, count[eng]), last_in.get(bank)
            last_in[bank] = key
        banks = {(k, g, name): bank for k, g, name, _, bank in plan}

        def empty(eng, key):
            who, n = emptied[key]
            eng.wait_ge(s.act if who == "act" else s.dve, n)

        ftile = lambda g, h: 2 * g + h // 2
        hb = lambda h: HD * (h % 2)
        MIX_Y = RKVQ[:, 2 * CT:3 * CT]

        @block.sync
        def _(sp):
            sp.dma_start(LNX[:, 0], t.lnx_g.to_broadcast([P, CW])).then_inc(s.rows_in, 16)
            sp.dma_start(LNX[:, 1], t.lnx_b.to_broadcast([P, CW])).then_inc(s.rows_in, 16)

        @block.tensor
        def _(pe):
            pe.wait_ge(s.init, 1)
            fences = [0]

            def fence(ins):
                fences[0] += 1
                ins.then_inc(s.order, 1)
                pe.wait_ge(s.order, fences[0])

            for k, g, name, eng, bank in plan:
                key = (k, g, name)
                if before[key] is not None:
                    empty(pe, before[key])
                B = PS[:, bank, :]
                B4 = B.rearrange("p (h c) -> p h c", h=HB)
                cols = slice(k * P, (k + 1) * P)
                v, nb, kn, q = (tok[:, g, i] for i in range(4))
                if name in ("TRa", "TRb"):
                    if k and name == "TRa":
                        pe.wait_ge(s.pool, k * 2)
                    for i in range(2):
                        for f in range(2):
                            src = (RKVQ[:, 2 * CT + 2 * g + f], A[:, 2 * g + f], RKVQ[:, CT + 2 * g + f],
                                   RKVQ[:, 3 * CT + 2 * g + f])[2 * (name == "TRb") + i]
                            last = pe.transpose(B[:, (2 * i + f) * P:(2 * i + f + 1) * P], src[:, cols],
                                                m.const("ident"))
                elif name in ("PBa", "PBb", "PGa", "PGb"):
                    for i in range(2):
                        h = 2 * i + (name[2] == "b")
                        f, b = ftile(g, h), hb(h)
                        left = A[b:b + HD, f, cols] if name[1] == "B" else RKVQ[b:b + HD, CT + f, cols]
                        last = pe.matmul(B[:, i * 2 * P:(i + 1) * 2 * P].rearrange("p (a c) -> p a c", a=2), left,
                                         RKVQ[b:b + HD, f:f + 3 * CT + 1:3 * CT, cols], start=True, stop=True)
                elif name == "N":
                    for h in (0, 2, 1, 3):
                        if h == 1:
                            fence(last)
                        f, b = ftile(g, h), hb(h)
                        last = pe.matmul(B4[:, h], RKVQ[b:b + HD, 3 * CT + f, cols], A[b:b + HD, f, cols],
                                         start=True, stop=True)
                elif name in ("SQ1a", "SQ1b", "AP1", "SQ2a", "SQ2b", "AP2", "SQ3", "AP3", "FR", "Z", "H1", "H2",
                              "H3"):
                    needs = {"SQ1a": ("N", "PBb"), "SQ1b": (), "AP1": ("SQ1a",), "SQ2a": ("SQ1b",), "SQ2b": (),
                             "AP2": ("SQ2a", "AP1"), "SQ3": ("SQ2b",), "AP3": ("SQ3", "AP2"), "FR": ("AP3",),
                             "Z": ("GV",), "H1": ("FR", "Z"), "H2": ("H1",), "H3": ("H2",)}[name]
                    for need in needs:
                        empty(pe, (k, g, need))
                    for h in range(HB):
                        left, right = {
                            "SQ1a": (BR[:, g, h, 1], ND[:, g, h]), "SQ1b": (ND[:, g, h], BR[:, g, h, 1]),
                            "AP1": (P2[:, g, 0, h], IB[:, g, h]),
                            "SQ2a": (P2[:, g, 1, h], P2[:, g, 0, h]), "SQ2b": (P2[:, g, 0, h], P2[:, g, 1, h]),
                            "AP2": (P4[:, g, 0, h], IB[:, g, h]), "SQ3": (P4[:, g, 1, h], P4[:, g, 0, h]),
                            "AP3": (P8[:, g, h], IB[:, g, h]), "FR": (NE[:, g, h], IB[:, g, h]),
                            "Z": (IB[:, g, h], XR[:, g, h]), "H1": (FR[:, g, h], ZZ[:, g, h]),
                            "H2": (FR[:, g, h], WU[:, g, h]), "H3": (FR[:, g, h], WU[:, g, h]),
                        }[name]
                        last = pe.matmul(B4[:, h], left, right, start=True, stop=True)
                elif name == "GV":
                    empty(pe, (k, g, "PGb"))
                    empty(pe, (k, g, "TRa"))
                    for h in range(HB):
                        last = pe.matmul(B[:, h * HD:(h + 1) * HD], GR[:, g, h, 1], v[:, h * HD:(h + 1) * HD],
                                         start=True, stop=True)
                elif name == "MT":
                    empty(pe, (k, g, "H3"))
                    for c in range(2):
                        if c:
                            fence(last)
                        for h in range(HB):
                            rows, b = slice(c * CH, (c + 1) * CH), hb(h)
                            last = pe.matmul(B[b:b + HD, (2 * (h // 2) + c) * HD:(2 * (h // 2) + c + 1) * HD],
                                             WU[rows, g, h, 0:HD], nb[rows, h * HD:(h + 1) * HD],
                                             start=True, stop=True)
                elif name == "ZT":
                    for h in range(HB):
                        b = hb(h)
                        last = pe.matmul(B[b:b + HD, (h // 2) * P:(h // 2 + 1) * P], WU[:, g, h, 0:HD],
                                         BR[:, g, h, 0], start=True, stop=True)
                elif name in ("S0", "S1"):
                    c = int(name[1])
                    if c == 0:
                        for gg in range(2):
                            empty(pe, (k, gg, "MT"))
                            empty(pe, (k, gg, "ZT"))
                    else:
                        empty(pe, (k, 0, "S0"))
                    if c == 0:
                        if before[(k, 0, "Y")] is not None:
                            empty(pe, before[(k, 0, "Y")])
                    rows = slice(c * CH, (c + 1) * CH)
                    every = [(gg, h) for gg in range(2) for h in range(HB)]
                    out = lambda gg, h: B[hb(h):hb(h) + HD, ftile(gg, h) * HD:(ftile(gg, h) + 1) * HD]
                    y_at = lambda gg, h: slice((4 * gg + h) * HD, (4 * gg + h + 1) * HD)
                    for gg, h in every:
                        hs = slice(h * HD, (h + 1) * HD)
                        pe.matmul(out(gg, h), tok[rows, gg, 2, hs], tok[rows, gg, 0, hs],
                                  start=gg == 0 and h < 2, stop=False, skip_group_check=True)
                        last = pe.matmul(out(gg, h), tok[rows, gg, 1, hs], WU[rows, gg, h, HD:P], start=False,
                                         stop=False, skip_group_check=True)
                    if c == 0:
                        for gg, h in every:
                            pe.matmul(PS[:, 6, y_at(gg, h)], GR[:, gg, h, 0], tok[:, gg, 0, h * HD:(h + 1) * HD],
                                      start=gg == 0 and h == 0, stop=False, skip_group_check=True)
                            last = pe.matmul(PS[:, 6, y_at(gg, h)], BR[:, gg, h, 0], WU[:, gg, h, HD:P],
                                             start=False, stop=False, skip_group_check=True)
                    for odd in range(2):
                        fence(last)
                        for gg, h in every:
                            if h % 2 == odd:
                                f, b = ftile(gg, h), hb(h)
                                pe.matmul(out(gg, h), MT[b:b + HD, gg, h // 2, c], S[b:b + HD, f], start=False,
                                          stop=True, skip_group_check=True)
                                last = pe.matmul(PS[rows, 6, y_at(gg, h)], ZT[b:b + HD, f, rows], S[b:b + HD, f],
                                                 start=False, stop=True, skip_group_check=True)
                elif name == "Y":
                    pe.sem_inc(s.pe, 1)
                    continue
                elif name == "GT":
                    if k:
                        pe.wait_ge(s.y_ready, k)
                    pe.matmul(B, LO[:, 1, cols], G2[:, 0], start=True, stop=False)
                    last = pe.matmul(B, LO[0:GLORA - P, 2, cols], G2[0:GLORA - P, 1], start=False, stop=True)
                elif name == "YT":
                    pe.wait_ge(s.y_ready, k + 1)
                    for q_ in range(CT):
                        last = pe.transpose(B[:, q_ * P:(q_ + 1) * P], Y[:, q_ * P:(q_ + 1) * P], m.const("ident"))
                last.then_inc(s.pe, 1)
                if name == "S1":
                    pe.wait_ge(s.pe, filled[key])

        @block.scalar
        def _(act):
            for k, g, name, eng, bank in plan:
                if eng != "act":
                    continue
                key = (k, g, name)
                act.wait_ge(s.pe, filled[key])
                B = PS[:, bank, :]
                ins = None
                if name == "TRa":
                    ins = nc.scalar.copy(tok[:, g, 0:2].rearrange("p a c -> p (a c)"), B)
                elif name == "TRb":
                    ins = nc.scalar.copy(tok[:, g, 2:4].rearrange("p a c -> p (a c)"), B)
                elif name == "GV":
                    act.wait_ge(s.act, emptied[(k, g, "TRb")][1])
                    nc.scalar.copy(XR[:, g, :, 0:HD], tok[:, g, 3].rearrange("p (h c) -> p h c", h=HB))
                    ins = nc.scalar.copy(XR[:, g, :, HD:P], B[:, 0:HB * HD].rearrange("p (h c) -> p h c", h=HB))
                elif name == "GT":
                    ins = nc.scalar.copy(GT[:], B)
                elif name == "YT":
                    ins = nc.scalar.copy(MIX_Y[:, :, k * P:(k + 1) * P], B.rearrange("p (q c) -> p q c", q=CT))
                else:
                    out = {"SQ1b": P2[:, g, 1], "SQ2b": P4[:, g, 1], "SQ3": P8[:, g], "FR": FR[:, g],
                           "Z": ZZ[:, g]}[name]
                    ins = nc.scalar.copy(flat(out), B)
                ins.then_inc(s.act, 1)
                if name == "GT":
                    act.wait_ge(s.squared, 2 * k + 1)
                    nc.scalar.activation(Y2[:], Y[:], ACT.Square).then_inc(s.achain, 1)
                    act.wait_ge(s.squared, 2 * k + 2)
                    nc.scalar.activation(st[:, 1], st[:, 1], ACT.Sqrt, scale=1.0 / HD, bias=m.small[:, 0:1]
                                         ).then_inc(s.achain, 1)

        @block.gpsimd
        def _(pool):
            for k in range(TT):
                if k >= 2:
                    pool.wait_ge(s.y_ready, k - 1)
                for g in range(2):
                    empty(pool, (k, g, "TRa"))
                    nc.gpsimd.tensor_tensor(
                        VB[:, k % 2, g * 2 * P:(g + 1) * 2 * P].rearrange("p (h c) -> p h c", h=HB),
                        tok[:, g, 0].rearrange("p (h c) -> p h c", h=HB),
                        bonus[:, k * RH + g * HB:k * RH + (g + 1) * HB].unsqueeze(2).to_broadcast([P, HB, HD]),
                        ALU.mult).then_inc(s.pool, 1)

        @block.vector
        def _(dve):
            do = Chain(dve, s.chain)
            v = nc.vector
            v.memset(m.small[:, 0:1], LNX_EPS).then_inc(s.eps, 1)
            v.memset(S[:], 0.0).then_inc(s.init, 1)
            dve.wait_ge(s.rows_in, 32)
            heads = lambda ap: ap.rearrange("p (h c) -> p h c", h=RH)
            wide = lambda ap: ap.unsqueeze(2).to_broadcast([P, RH, HD])

            def mask(name, n=1):
                at = CONSTS[name][0]
                return m.consts[:, at:at + n * P].unsqueeze(1).to_broadcast([P, HB // n, n * P])

            for k, g, name, eng, bank in plan:
                if eng != "dve":
                    continue
                key = (k, g, name)
                dve.wait_ge(s.pe, filled[key])
                B = PS[:, bank, :]
                B4 = B.rearrange("p (h c) -> p h c", h=HB)
                B2 = B.rearrange("p (h c) -> p h c", h=2)
                cols = slice(k * P, (k + 1) * P)
                if name in ("PBa", "PBb"):
                    h = int(name[2] == "b")
                    ins = v.tensor_tensor(BR[:, g, h:HB:2].rearrange("p h a c -> p h (a c)"), B2,
                                          mask("mask_incl_up", 2), ALU.mult)
                elif name in ("PGa", "PGb"):
                    h = int(name[2] == "b")
                    ins = v.tensor_tensor(GR[:, g, h:HB:2].rearrange("p h a c -> p h (a c)"), B2,
                                          mask("mask_incl_up_2", 2), ALU.mult)
                elif name == "N":
                    dve.wait_ge(s.dve, emptied[(k, g, "PBb")][1])
                    v.tensor_tensor(IB[:, g], BR[:, g, :, 1], mask("ident"), ALU.add)
                    v.tensor_tensor(ND[:, g], B4, mask("mask_diag_low"), ALU.mult)
                    ins = v.tensor_tensor(NE[:, g], B4, mask("mask_off_low"), ALU.mult)
                elif name in ("SQ1a", "SQ2a"):
                    ins = v.tensor_copy(flat((P2 if name == "SQ1a" else P4)[:, g, 0]), B)
                elif name in ("AP1", "AP2", "AP3"):
                    ins = v.tensor_tensor(flat(IB[:, g]), flat(IB[:, g]), B, ALU.add)
                elif name in ("H1", "H2", "H3"):
                    ins = v.tensor_tensor(flat(WU[:, g]), flat(ZZ[:, g]), B, ALU.add)
                elif name == "MT":
                    at = CONSTS["ident_heads"][0]
                    ident = m.consts[:, at:at + HD].unsqueeze(1).to_broadcast([P, 4, HD])
                    ins = v.tensor_tensor(MT[:, g].rearrange("p f c j -> p (f c) j"),
                                          B[:, 0:4 * HD].rearrange("p (f j) -> p f j", f=4), ident, ALU.add)
                elif name == "ZT":
                    ins = v.tensor_tensor(ZT[:, 2 * g:2 * g + 2], B[:, 0:2 * P].rearrange("p (f c) -> p f c", f=2),
                                          RKVQ[:, 2 * g:2 * g + 2, cols], ALU.add)
                elif name in ("S0", "S1"):
                    c = int(name[1])
                    ins = v.tensor_tensor(S[:], B[:, 0:CT * HD].rearrange("p (f i) -> p f i", f=CT),
                                          PC[:, :, 2 * k + c].unsqueeze(2).to_broadcast([P, CT, HD]), ALU.mult)
                elif name == "Y":
                    if k:
                        dve.wait_ge(s.pe, filled[(k - 1, 0, "YT")])
                    do(v.tensor_reduce(st[:, 0], heads(B), AX, ALU.add))
                    do(v.tensor_scalar(st[:, 0], st[:, 0], 1.0 / HD, None, ALU.mult))
                    ins = v.tensor_tensor(heads(Y[:]), heads(B), wide(st[:, 0]), ALU.subtract)
                ins.then_inc(s.dve, 1)
                if name == "Y":
                    dve.wait_ge(s.dve, emptied[key][1])
                    v.sem_inc(s.squared, 1)
                    dve.wait_ge(s.achain, 2 * k + 1)
                    v.tensor_reduce(st[:, 1], heads(Y2[:]), AX, ALU.add).then_inc(s.squared, 1)
                    dve.wait_ge(s.achain, 2 * k + 2)
                    do(v.reciprocal(st[:, 2], st[:, 1]))
                    do(v.tensor_tensor(heads(Y[:]), heads(Y[:]), wide(st[:, 2]), ALU.mult))
                    do(v.tensor_tensor(Y[:], Y[:], LNX[:, 0], ALU.mult))
                    do(v.tensor_tensor(Y[:], Y[:], LNX[:, 1], ALU.add))
                    dve.wait_ge(s.pool, 2 * k + 2)
                    do(v.tensor_tensor(Y[:], Y[:], VB[:, k % 2], ALU.add))
                    empty(dve, (k, 0, "GT"))
                    v.tensor_tensor(Y[:], Y[:], GT[:], ALU.mult).then_inc(s.y_ready, 1)


def out_projection(m, tiles, w, GM, X):
    nc, t, PS = m.nc, m.t, m.PS
    with ExitStack() as ctx:
        W = alloc(m, ctx, "w_out", [P, KT, D])
        tmp = alloc(m, ctx, "scaled", [P, 2, D])
        junk = alloc(m, ctx, "junk", [P, D])
        s = phase(m, "w_in x_in eps prod rooted ps_free chain done")
        block = ctx.enter_context(nc.Block())
        ss, rstd, eps = m.small[:, 0:TT], m.small[:, TT:2 * TT], m.small[:, 2 * TT:2 * TT + 1]

        @block.sync
        def _(sp):
            sp.dma_start(W[:], w.rearrange("(k p) n -> p k n", p=P)).then_inc(s.w_in, 16)
            sp.dma_start(X[:], t.x.rearrange("(k p) n -> p k n", p=P)).then_inc(s.x_in, 16)

        @block.tensor
        def _(pe):
            pe.wait_ge(s.w_in, 16)
            for k in range(TT):
                if k >= 4:
                    pe.wait_ge(s.ps_free, k - 3)
                for half in range(2):
                    for q in range(KT):
                        last = pe.matmul(PS[:, 2 * (k % 4) + half, :], tiles[q][:, k * P:(k + 1) * P],
                                         W[:, q, half * NH:(half + 1) * NH], start=q == 0, stop=q == KT - 1)
                last.then_inc(s.prod, 1)

        @block.scalar
        def _(act):
            act.wait_ge(s.eps, 1)
            for k in range(TT):
                act.wait_ge(s.prod, k + 1)
                nc.scalar.activation(junk[:], bank2(m, k % 4), ACT.Square, accum_out=ss[:, k:k + 1]
                                     ).then_inc(s.chain, 1)
                act.wait_ge(s.chain, k + 1)
                nc.scalar.activation(rstd[:, k:k + 1], ss[:, k:k + 1], ACT.Sqrt, scale=1.0 / D, bias=eps
                                     ).then_inc(s.rooted, 1)

        @block.vector
        def _(dve):
            v = nc.vector
            v.memset(eps, RMS_EPS).then_inc(s.eps, 1)
            dve.wait_ge(s.x_in, 16)
            for k in range(TT):
                dve.wait_ge(s.rooted, k + 1)
                v.reciprocal(rstd[:, k:k + 1], rstd[:, k:k + 1]).then_inc(s.done, 1)
                dve.wait_ge(s.done, 2 * k + 1)
                v.scalar_tensor_tensor(out=tmp[:, k % 2], in0=bank2(m, k % 4), scalar=rstd[:, k:k + 1],
                                       in1=GM, op0=ALU.mult, op1=ALU.mult).then_inc(s.ps_free, 1)
                dve.wait_ge(s.ps_free, k + 1)
                v.tensor_tensor(X[:, k], X[:, k], tmp[:, k % 2], ALU.add).then_inc(s.done, 1)


def up_projection(m, MID):
    nc, t, PS = m.nc, m.t, m.PS
    with ExitStack() as ctx:
        W = alloc(m, ctx, "up_slots", [P, 2, KT, 2 * P])
        Z = alloc(m, ctx, "z", [P, 2, 2, T])
        s = phase(m, "w_in0 w_in1 slot_free tile_done ps_free tap2 chain silu mid")
        w_in = [s.w_in0, s.w_in1]
        block = ctx.enter_context(nc.Block())
        col = lambda name, at: m.cols[:, bass.ds(at + COLS[name][0], 1)]

        @block.sync
        def _(sp):
            with sp.Fori(0, FT // 2) as i:
                at = [[sp.snap(i * 2 * P + j * P + c * D_FF) for c in range(2)] for j in range(2)]
                for j in range(2):
                    sp.wait_ge(s.slot_free, i * 2 + j + 1)
                    for c in range(2):
                        sp.dma_start(W[:, j, :, c * P:(c + 1) * P],
                                     t.w_up[:, bass.ds(at[j][c], P)].rearrange("(k p) n -> p k n", p=P)
                                     ).then_inc(w_in[j], 16)

        @block.tensor
        def _(pe):
            pe.sem_inc(s.slot_free, 2)
            with pe.Fori(0, FT // 2) as i:
                for j in range(2):
                    pe.wait_ge(w_in[j], (i + 1) * 32)
                    for c in range(2):
                        pe.wait_ge(s.ps_free, i * 4 + 2 * j + c + 1)
                        tile_product(m, pe, W, j, c, 2 * j + c).then_inc(s.tile_done, 1)
                    pe.wait_ge(s.tile_done, i * 4 + 2 * j + 2)
                    pe.sem_inc(s.slot_free, 1)

        @block.scalar
        def _(act):
            with act.Fori(0, FT // 2) as i:
                for j in range(2):
                    act.wait_ge(s.mid, i * 2 + j + 1)
                    for c in range(2):
                        ch = i * 2 + (j + c * FT)
                        act.wait_ge(s.tile_done, i * 4 + 2 * j + c + 1)
                        nc.scalar.activation(Z[:, j, c], bank2(m, 2 * j + c), ACT.Identity,
                                             scale=col("ffn_w", i * 6 + (j + c * FT) * 3 + 2), bias=col("ffn_b", ch)
                                             ).then_inc(s.tap2, 1)
                    act.wait_ge(s.ps_free, i * 4 + 2 * j + 1 + 4)
                    nc.scalar.activation(Z[:, j, 0], Z[:, j, 0], ACT.Silu).then_inc(s.silu, 1)

        @block.vector
        def _(dve):
            v = nc.vector
            dve.sem_inc(s.ps_free, 4)
            dve.sem_inc(s.mid, 2)
            with dve.Fori(0, FT // 2) as i:
                for j in range(2):
                    for c in range(2):
                        n = 2 * j + c
                        dve.wait_ge(s.tap2, i * 4 + n + 1)
                        for tap in (1, 2):
                            z = Z[:, j, c, tap:T]
                            ins = v.scalar_tensor_tensor(out=z, in0=bank2(m, n)[:, 0:T - tap],
                                                         scalar=col("ffn_w", i * 6 + (j + c * FT) * 3 + 2 - tap),
                                                         in1=z, op0=ALU.mult, op1=ALU.add)
                            if tap == 1:
                                ins.then_inc(s.chain, 1)
                                dve.wait_ge(s.chain, i * 4 + n + 1)
                        ins.then_inc(s.ps_free, 1)
                    dve.wait_ge(s.silu, i * 2 + j + 1)
                    dve.wait_ge(s.ps_free, i * 4 + 2 * j + 2 + 4)
                    v.tensor_tensor(MID[:, bass.ds(i * 2 + j, 1), :].rearrange("p a b -> p (a b)"), Z[:, j, 0],
                                    Z[:, j, 1], ALU.mult).then_inc(s.mid, 1)


def down_projection(m, MID, GM, X, dst):
    nc, t, PS = m.nc, m.t, m.PS
    QW, KC = D // 4, FT // 2
    F = m.HT
    with ExitStack() as ctx:
        W = alloc(m, ctx, "down_slots", [P, 2, KC, QW])
        s = phase(m, "w_in0 w_in1 slot_free prod ps_free moved eps sq rooted chain out stored")
        w_in = [s.w_in0, s.w_in1]
        block = ctx.enter_context(nc.Block())
        ss, rstd, eps = m.small[:, 0:TT], m.small[:, TT:2 * TT], m.small[:, 2 * TT:2 * TT + 1]

        @block.sync
        def _(sp):
            with sp.Fori(0, 4) as i:
                at = sp.snap(i * QW)
                for c in range(2):
                    sp.wait_ge(s.slot_free, i * 2 + c + 1)
                    sp.dma_start(W[:, c], t.w_down[c * KC * P:(c + 1) * KC * P, bass.ds(at, QW)]
                                 .rearrange("(k p) n -> p k n", p=P)).then_inc(w_in[c], 16)
            for k in range(TT):
                sp.wait_ge(s.out, TT + k + 1)
                sp.dma_start(dst[k * P:(k + 1) * P], X[:, k]).then_inc(s.stored, 16)
            sp.wait_ge(s.stored, 16 * TT)

        @block.tensor
        def _(pe):
            pe.sem_inc(s.slot_free, 2)
            with pe.Fori(0, 2) as i:
                for r in range(2):
                    for c in range(2):
                        pe.wait_ge(w_in[c], (i * 2 + r + 1) * 16)
                        for k in range(TT):
                            if c == 0 and k % 2 == 0:
                                pe.wait_ge(s.ps_free, i * 8 + 4 * r + k // 2 + 1)
                            for q in range(KC):
                                last = pe.matmul(PS[:, 4 * r + k // 2, (k % 2) * QW:(k % 2 + 1) * QW],
                                                 MID[:, c * KC + q, k * P:(k + 1) * P], W[:, c, q],
                                                 start=c == 0 and q == 0 and k % 2 == 0,
                                                 stop=c == 1 and q == KC - 1, skip_group_check=True)
                            if c == 1 and k % 2 == 1:
                                last.then_inc(s.prod, 1)
                            elif c == 0 and k == TT - 1:
                                last.then_inc(s.slot_free, 1)
                        if c == 1:
                            pe.wait_ge(s.prod, i * 8 + 4 * r + 4)
                            pe.sem_inc(s.slot_free, 1)

        @block.scalar
        def _(act):
            act.sem_inc(s.ps_free, 8)
            with act.Fori(0, 2) as i:
                for r in range(2):
                    for b in range(4):
                        act.wait_ge(s.prod, i * 8 + 4 * r + b + 1)
                        nc.scalar.copy(F[:, 2 * b:2 * b + 2, bass.ds(i * 2 * QW + r * QW, QW)],
                                       PS[:, 4 * r + b, :].rearrange("p (k n) -> p k n", k=2)).then_inc(s.ps_free, 1)
            act.wait_ge(s.ps_free, 24)
            act.wait_ge(s.eps, 1)
            for k in range(TT):
                if k:
                    act.wait_ge(s.sq, k)
                nc.scalar.activation(flat(W[:, 0, 0:4]), F[:, k], ACT.Square, accum_out=ss[:, k:k + 1]
                                     ).then_inc(s.sq, 1)
            act.wait_ge(s.sq, TT)
            nc.scalar.activation(rstd, ss, ACT.Sqrt, scale=1.0 / D, bias=eps).then_inc(s.rooted, 1)

        @block.vector
        def _(dve):
            do = Chain(dve, s.chain)
            v = nc.vector
            v.memset(eps, RMS_EPS).then_inc(s.eps, 1)
            dve.wait_ge(s.rooted, 1)
            do(v.reciprocal(rstd, rstd))
            for k in range(TT):
                v.scalar_tensor_tensor(out=F[:, k], in0=F[:, k], scalar=rstd[:, k:k + 1], in1=GM,
                                       op0=ALU.mult, op1=ALU.mult).then_inc(s.out, 1)
            dve.wait_ge(s.out, TT)
            for k in range(TT):
                v.tensor_tensor(X[:, k], X[:, k], F[:, k], ALU.add).then_inc(s.out, 1)




def load_channels(m, src):
    nc, PS, HT = m.nc, m.PS, m.HT
    with ExitStack() as ctx:
        X = alloc(m, ctx, "x_tokens", [P, TT, D])
        s = phase(m, "in0 in1 in2 in3 in4 in5 in6 in7 turned ev_act ev_dve")
        x_in = [s.in0, s.in1, s.in2, s.in3, s.in4, s.in5, s.in6, s.in7]
        block = ctx.enter_context(nc.Block())

        @block.sync
        def _(sp):
            for k in range(TT):
                sp.dma_start(X[:, k], src[k * P:(k + 1) * P]).then_inc(x_in[k], 16)

        @block.tensor
        def _(pe):
            for half in range(2):
                for j in range(4):
                    pe.wait_ge(x_in[4 * half + j], 16)
                for k in range(KT):
                    if half:
                        pe.wait_ge(s.ev_dve if k % 2 else s.ev_act, k // 2 + 1)
                    for j in range(4):
                        last = pe.transpose(PS[:, k, j * P:(j + 1) * P], X[:, 4 * half + j, k * P:(k + 1) * P],
                                            m.const("ident"))
                    last.then_inc(s.turned, 1)

        @block.scalar
        def _(act):
            for n in range(0, 2 * KT, 2):
                act.wait_ge(s.turned, n + 1)
                nc.scalar.copy(HT[:, n % KT, n // KT * NH:(n // KT + 1) * NH], PS[:, n % KT, :]
                               ).then_inc(s.ev_act, 1)

        @block.vector
        def _(dve):
            for n in range(1, 2 * KT, 2):
                dve.wait_ge(s.turned, n + 1)
                nc.vector.tensor_copy(HT[:, n % KT, n // KT * NH:(n // KT + 1) * NH], PS[:, n % KT, :]
                                      ).then_inc(s.ev_dve, 1)


def qkv_projection(m, w, QT, KH, V):
    nc, PS = m.nc, m.PS
    with ExitStack() as ctx:
        W = alloc(m, ctx, "qkv_slots", [P, 2, KT, 512])
        s = phase(m, "w_in0 w_in1 tile_done moved swapped")
        w_in = [s.w_in0, s.w_in1]
        block = ctx.enter_context(nc.Block())

        @block.sync
        def _(sp):
            for b in range(3):
                if b == 2:
                    sp.wait_ge(s.tile_done, 4)
                sp.dma_start(W[:, b % 2], w[:, b * 512:(b + 1) * 512].rearrange("(k p) n -> p k n", p=P)
                             ).then_inc(w_in[b % 2], 16)
            sp.wait_ge(s.moved, 10)
            sp.dma_start(KH[0:HD, 2:4], KH[HD:P, 0:2]).then_inc(s.swapped, 16)
            sp.dma_start(KH[HD:P, 2:4], KH[0:HD, 0:2]).then_inc(s.swapped, 16)
            sp.wait_ge(s.swapped, 32)

        @block.tensor
        def _(pe):
            for n in range(10):
                b, i = n // 4, n % 4
                if i == 0:
                    pe.wait_ge(w_in[b % 2], 16 * (b // 2 + 1))
                if n >= 4:
                    pe.wait_ge(s.moved, n - 3)
                last = tile_product(m, pe, W, b % 2, i, i)
                last.then_inc(s.tile_done, 1)
            for l in range(TT):
                if l % 2 == 0:
                    pe.wait_ge(s.moved, 7 + l // 4)
                for k in range(KT):
                    last = pe.matmul(PS[:, 4 + l // 2, (l % 2) * KVW:(l % 2 + 1) * KVW],
                                     m.HT[:, k, l * P:(l + 1) * P], W[:, 0, k, KVW:2 * KVW],
                                     start=k == 0, stop=k == KT - 1)
                if l % 2:
                    last.then_inc(s.tile_done, 1)

        @block.scalar
        def _(act):
            for n in range(10):
                act.wait_ge(s.tile_done, n + 1)
                nc.scalar.copy(QT[:, n] if n < 8 else KH[:, n - 8], bank2(m, n % 4)).then_inc(s.moved, 1)
            for n in range(4):
                act.wait_ge(s.tile_done, 11 + n)
                nc.scalar.copy(V[:, 2 * n:2 * n + 2], PS[:, 4 + n, :].rearrange("p (l c) -> p l c", l=2))


def attention(m, sinks, QT, KH, V, AT):
    nc, t, PS = m.nc, m.t, m.PS
    G4 = 4
    with ExitStack() as ctx:
        BIAS = alloc(m, ctx, "alibi", [P, QH, 2 * P])
        SC = alloc(m, ctx, "scores", [P, 2, G4, 2 * P])
        PT = alloc(m, ctx, "probs_turned", [P, 2, 2, G4 * P])
        SK = alloc(m, ctx, "sinks", [P, QH])
        MX = alloc(m, ctx, "maxima", [P, 2, G4])
        NM = alloc(m, ctx, "minus_max", [P, 2, G4])
        DN = alloc(m, ctx, "sums", [P, 2, G4])
        ES = alloc(m, ctx, "sink_terms", [P, 2, G4])
        RD = alloc(m, ctx, "inverse_sums", [P, 2, G4])
        s = phase(m, "par_in sink_in scored biased neg exps rden chain probs turned moved0 moved1 outed stored")
        block = ctx.enter_context(nc.Block())
        units = [(nb, g) for nb in range(TT) for g in range(KVH)]
        N = len(units)
        lo = lambda nb: P if nb == 0 else 0

        @block.sync
        def _(sp):
            sp.dma_start(BIAS[:], t.alibi).then_inc(s.par_in, 16)
            sp.dma_start(SK[:], sinks.to_broadcast([P, QH])).then_inc(s.sink_in, 16)

        @block.tensor
        def _(pe):
            def scores(u):
                nb, g = units[u]
                if u >= 2:
                    pe.wait_ge(s.biased, u - 1)
                for i in range(G4):
                    at, b = (i // 2) * 2 * P, HD * (i % 2)
                    last = pe.matmul(PS[:, 2 * (u % 2) + i % 2, at + lo(nb):at + 2 * P],
                                     QT[b:b + HD, 2 * g + i // 2, nb * P:(nb + 1) * P],
                                     KH[b:b + HD, g // 2 + (2 if i % 2 != g % 2 else 0),
                                        (nb - 1) * P + lo(nb):(nb + 1) * P], start=True, stop=True)
                last.then_inc(s.scored, 1)

            def turn(u):
                nb, g = units[u]
                pe.wait_ge(s.probs, u + 1)
                for a in range(2):
                    if u:
                        pe.wait_ge(s.moved1 if a else s.moved0, u)
                    if a == 0 and nb == 0:
                        pe.sem_inc(s.turned, 1)
                        continue
                    for i in range(G4):
                        at = ((i % 2) * 2 + i // 2) * P
                        last = pe.transpose(PS[:, 4 + a, at:at + P], SC[:, u % 2, i, a * P:(a + 1) * P],
                                            m.const("ident"))
                    last.then_inc(s.turned, 1)

            def out(u):
                nb, g = units[u]
                bank = 6 + (u // 2) % 2
                pe.wait_ge(s.moved0, u + 1)
                pe.wait_ge(s.moved1, u + 1)
                if g % 2 == 0 and u >= 4:
                    pe.wait_ge(s.stored, u // 2 - 1)
                for odd in range(2):
                    for a in range(1 if nb == 0 else 0, 2):
                        last = pe.matmul(PS[odd * HD:(odd + 1) * HD, bank, (g % 2) * 2 * P:(g % 2 + 1) * 2 * P],
                                         V[:, nb - 1 + a, g * HD:(g + 1) * HD],
                                         PT[:, u % 2, a, odd * 2 * P:(odd + 1) * 2 * P],
                                         start=a == 0 or nb == 0, stop=a == 1)
                last.then_inc(s.outed, 1)

            for u in range(N + 2):
                if u < N:
                    scores(u)
                if 1 <= u <= N:
                    turn(u - 1)
                if u >= 2:
                    out(u - 2)

        @block.scalar
        def _(act):
            act.wait_ge(s.sink_in, 16)
            for u in range(N + 3):
                if u < N:
                    nb, g = units[u]
                    act.wait_ge(s.neg, u + 1)
                    nc.scalar.activation(ES[:, u % 2], ES[:, u % 2], ACT.Exp).then_inc(s.exps, 1)
                    for i in range(G4):
                        p = SC[:, u % 2, i, lo(nb):2 * P]
                        nc.scalar.activation(p, p, ACT.Exp, bias=NM[:, u % 2, i:i + 1],
                                             accum_out=DN[:, u % 2, i:i + 1]).then_inc(s.exps, 1)
                if 1 <= u <= N:
                    w = u - 1
                    act.wait_ge(s.turned, 2 * w + 1)
                    if w >= 2:
                        act.wait_ge(s.outed, w - 1)
                    if units[w][0] == 0:
                        act.sem_inc(s.moved0, 1)
                    else:
                        nc.scalar.copy(PT[:, w % 2, 0], PS[:, 4, :]).then_inc(s.moved0, 1)
                if u >= 3 and (u - 3) % 2 == 1:
                    w = u - 3
                    nb, g = units[w]
                    act.wait_ge(s.outed, w + 1)
                    nc.scalar.copy(AT[:, G4 * (g // 2):G4 * (g // 2) + G4, nb * P:(nb + 1) * P],
                                   PS[:, 6 + (w // 2) % 2, :].rearrange("p (i q) -> p i q", i=G4)
                                   ).then_inc(s.stored, 1)

        @block.vector
        def _(dve):
            do = Chain(dve, s.chain)
            v = nc.vector
            dve.wait_ge(s.par_in, 16)
            dve.wait_ge(s.sink_in, 16)
            for u in range(N + 1):
                if u < N:
                    nb, g = units[u]
                    dve.wait_ge(s.scored, u + 1)
                    if u >= 2:
                        dve.wait_ge(s.turned, 2 * (u - 1))
                    for i in range(G4):
                        h, at = G4 * g + i, (i // 2) * 2 * P
                        ins = v.tensor_tensor_reduce(
                            SC[:, u % 2, i, lo(nb):2 * P], PS[:, 2 * (u % 2) + i % 2, at + lo(nb):at + 2 * P],
                            BIAS[:, h, lo(nb):2 * P], HD ** -0.5, SK[:, h:h + 1], ALU.add, ALU.max,
                            MX[:, u % 2, i:i + 1])
                    ins.then_inc(s.biased, 1)
                    dve.wait_ge(s.biased, u + 1)
                    do(v.tensor_tensor(ES[:, u % 2], SK[:, G4 * g:G4 * g + G4], MX[:, u % 2], ALU.subtract))
                    v.tensor_scalar(NM[:, u % 2], MX[:, u % 2], -1.0, None, ALU.mult).then_inc(s.neg, 1)
                if u >= 1:
                    w = u - 1
                    dve.wait_ge(s.exps, 5 * w + 5)
                    do(v.tensor_tensor(DN[:, w % 2], DN[:, w % 2], ES[:, w % 2], ALU.add))
                    v.reciprocal(RD[:, w % 2], DN[:, w % 2]).then_inc(s.rden, 1)
                    dve.wait_ge(s.turned, 2 * w + 2)
                    if w >= 2:
                        dve.wait_ge(s.outed, w - 1)
                    v.tensor_copy(PT[:, w % 2, 1], PS[:, 5, :]).then_inc(s.moved1, 1)

        @block.gpsimd
        def _(pool):
            for u in range(N):
                nb, g = units[u]
                pool.wait_ge(s.rden, u + 1)
                p = SC[:, u % 2, :, lo(nb):2 * P]
                nc.gpsimd.tensor_tensor(p, p, RD[:, u % 2].unsqueeze(2).to_broadcast([P, G4, 2 * P - lo(nb)]),
                                        ALU.mult).then_inc(s.probs, 1)


def gates_and_xbc(m, layer, w, AT, XB, DT):
    nc, t, PS = m.nc, m.t, m.PS
    with ExitStack() as ctx:
        W = alloc(m, ctx, "xbc_slots", [P, 2, KT, 512])
        WD = alloc(m, ctx, "dt_w", [P, KT, SH])
        gate = alloc(m, ctx, "attn_gate", [P, 2, T])
        s = phase(m, "w_in0 w_in1 d_in tile_done act_free dve_free tap silu gated chain")
        w_in = [s.w_in0, s.w_in1]
        block = ctx.enter_context(nc.Block())
        starts = [O_ZA, O_ZA + 512] + [O_XBC + 512 * b for b in range(3)]
        tiles = 4 * len(starts)

        @block.sync
        def _(sp):
            with nc.allow_non_contiguous_dma(reason="64 bytes of each row"):
                sp.dma_start(WD[:], w[:, O_DT:IN_W].rearrange("(k p) n -> p k n", p=P)).then_inc(s.d_in, 16)
            for b, at in enumerate(starts):
                if b >= 2:
                    sp.wait_ge(s.tile_done, 4 * (b - 1))
                sp.dma_start(W[:, b % 2], w[:, at:at + 512].rearrange("(k p) n -> p k n", p=P)
                             ).then_inc(w_in[b % 2], 16)

        def freed(eng, n):
            if n < 8:
                eng.wait_ge(s.act_free, n + 1)
            else:
                eng.wait_ge(s.dve_free, n - 8 + 1)

        @block.tensor
        def _(pe):
            for n in range(tiles):
                b, i = n // 4, n % 4
                if i == 0:
                    pe.wait_ge(w_in[b % 2], 16 * (b // 2 + 1))
                if n >= 4:
                    freed(pe, n - 4)
                last = tile_product(m, pe, W, b % 2, i, i)
                last.then_inc(s.tile_done, 1)
            pe.wait_ge(s.d_in, 16)
            freed(pe, tiles - 4)
            for l in range(TT):
                for k in range(KT):
                    last = pe.matmul(PS[:, 0, l * SH:(l + 1) * SH], m.HT[:, k, l * P:(l + 1) * P], WD[:, k],
                                     start=k == 0, stop=k == KT - 1)
            last.then_inc(s.tile_done, 1)

        @block.scalar
        def _(act):
            for n in range(8):
                act.wait_ge(s.tile_done, n + 1)
                if n >= 2:
                    act.wait_ge(s.gated, n - 1)
                nc.scalar.activation(gate[:, n % 2], bank2(m, n % 4), ACT.Silu).then_inc(s.act_free, 1)
            for n in range(XT + 1):
                if n < XT:
                    act.wait_ge(s.tile_done, 9 + n)
                    ch = layer * XT + n
                    nc.scalar.activation(XB[:, n], bank2(m, n % 4), ACT.Identity, bias=m.col("conv_b_2", ch),
                                         scale=m.col("conv_w_2", ch * CK2 + CK2 - 1)).then_inc(s.tap, 1)
                if n >= 1:
                    act.wait_ge(s.dve_free, n)
                    nc.scalar.activation(XB[:, n - 1], XB[:, n - 1], ACT.Silu)
            act.wait_ge(s.tile_done, tiles + 1)
            nc.scalar.copy(DT[:], PS[:, 0, 0:TT * SH])

        @block.vector
        def _(dve):
            v = nc.vector
            do = Chain(dve, s.chain)
            for n in range(8):
                dve.wait_ge(s.act_free, n + 1)
                v.tensor_tensor(AT[:, n], AT[:, n], gate[:, n % 2], ALU.mult).then_inc(s.gated, 1)
            for n in range(XT):
                dve.wait_ge(s.tap, n + 1)
                ch = layer * XT + n
                for tap in range(1, CK2):
                    ins = v.scalar_tensor_tensor(out=XB[:, n, tap:T], in0=bank2(m, n % 4)[:, 0:T - tap],
                                                 scalar=m.col("conv_w_2", ch * CK2 + CK2 - 1 - tap),
                                                 in1=XB[:, n, tap:T], op0=ALU.mult, op1=ALU.add)
                    if tap < CK2 - 1:
                        do(ins)
                ins.then_inc(s.dve_free, 1)


def step_sizes(m, dt_bias, a_log, DT, NA, EI, DE, CD, DA):
    nc, t, PS = m.nc, m.t, m.PS
    C = TT * SH
    with ExitStack() as ctx:
        rows = alloc(m, ctx, "dt_rows", [P, 2, SH])
        tmp = alloc(m, ctx, "dt_tmp", [P, 5, C])
        s = phase(m, "par_in ab e chain sums acs last ex")
        block = ctx.enter_context(nc.Block())
        ax, e, sv, z, poly = (tmp[:, i] for i in range(5))
        by_head = lambda ap: ap.rearrange("p (c h) -> p c h", h=SH)

        @block.sync
        def _(sp):
            sp.dma_start(rows[:, 0], dt_bias.to_broadcast([P, SH])).then_inc(s.par_in, 16)
            sp.dma_start(rows[:, 1], a_log.to_broadcast([P, SH])).then_inc(s.par_in, 16)

        @block.scalar
        def _(act):
            act.wait_ge(s.par_in, 32)
            nc.scalar.activation(rows[:, 1], rows[:, 1], ACT.Exp).then_inc(s.e, 1)
            act.wait_ge(s.ab, 1)
            nc.scalar.activation(ax, DT[:], ACT.Abs).then_inc(s.e, 1)
            act.wait_ge(s.e, 2)
            nc.scalar.activation(e, ax, ACT.Exp, scale=-1.0).then_inc(s.e, 1)
            act.wait_ge(s.sums, 1)
            nc.scalar.activation(EI[:], PS[:, 0, 0:C], ACT.Exp).then_inc(s.ex, 1)
            nc.scalar.mul(NA[:], PS[:, 0, 0:C], -1.0).then_inc(s.acs, 1)
            act.wait_ge(s.last, 1)
            nc.scalar.activation(CD[:], PS[:, 1, 0:C], ACT.Exp).then_inc(s.ex, 1)
            act.wait_ge(s.ex, 3)
            nc.scalar.activation(DE[:], DE[:], ACT.Exp)

        @block.vector
        def _(dve):
            v = nc.vector
            do = Chain(dve, s.chain)
            dve.wait_ge(s.par_in, 32)
            v.tensor_tensor(by_head(DT[:]), by_head(DT[:]), rows[:, 0].unsqueeze(1).to_broadcast([P, TT, SH]),
                            ALU.add).then_inc(s.ab, 1)
            dve.wait_ge(s.e, 3)
            do(v.tensor_scalar(sv, e, 2.0, None, ALU.add))
            do(v.reciprocal(sv, sv))
            do(v.tensor_tensor(sv, sv, e, ALU.mult))
            do(v.tensor_tensor(z, sv, sv, ALU.mult))
            do(v.tensor_scalar(poly, z, 2.0 / 17, 2.0 / 15, ALU.mult, ALU.add))
            for n in range(13, 0, -2):
                do(v.tensor_tensor(poly, poly, z, ALU.mult))
                do(v.tensor_scalar(poly, poly, 2.0 / n, None, ALU.add))
            do(v.tensor_tensor(poly, poly, sv, ALU.mult))
            do(v.scalar_tensor_tensor(out=DT[:], in0=DT[:], scalar=0.0, in1=poly, op0=ALU.max, op1=ALU.add))
            do(v.scalar_tensor_tensor(out=by_head(DA[:]), in0=by_head(DT[:]), scalar=-1.0,
                                      in1=rows[:, 1].unsqueeze(1).to_broadcast([P, TT, SH]), op0=ALU.mult,
                                      op1=ALU.mult))
            dve.wait_ge(s.acs, 1)
            dve.wait_ge(s.last, 1)
            dve.wait_ge(s.ex, 2)
            v.tensor_tensor(DE[:], PS[:, 1, 0:C], NA[:], ALU.add).then_inc(s.ex, 1)

        @block.tensor
        def _(pe):
            pe.wait_ge(s.chain, 5 + 2 * 7 + 3)
            pe.matmul(PS[:, 0, 0:C], m.const("tri"), DA[:], start=True, stop=True).then_inc(s.sums, 1)
            pe.wait_ge(s.acs, 1)
            pe.matmul(PS[:, 1, 0:C], m.const("minus_last"), NA[:], start=True, stop=True).then_inc(s.last, 1)


def state_space(m, w, d_skip, norm_w, XB, DT, DA, NA, EI, DE, CD):
    nc, t, PS, HT = m.nc, m.t, m.PS, m.HT
    BF16 = mybir.dt.bfloat16
    GW = DI // SG
    with ExitStack() as ctx:
        W = alloc(m, ctx, "z_w", [P, KT, DI])
        E = alloc(m, ctx, "decays", [P, SH, P])
        XS = alloc(m, ctx, "x_by_token", [P, DI])
        XDT = alloc(m, ctx, "x_dt", [P, DI])
        XDE = alloc(m, ctx, "x_dt_decayed", [P, DI])
        Y = alloc(m, ctx, "y", [P, 2, DI])
        ZS = alloc(m, ctx, "z_gate", [P, DI])
        tmp = alloc(m, ctx, "y_tmp", [P, DI])
        BC = alloc(m, ctx, "b_and_cb", [P, 512])
        S = alloc(m, ctx, "state", [P, DI])
        NW = alloc(m, ctx, "norm_rows", [P, DI])
        DS = alloc(m, ctx, "skip_rows", [P, SH])
        st = alloc(m, ctx, "group_stats", [P, 2, SG])
        eps = m.small[:, 0:1]
        identb = ctx.enter_context(nc.sbuf_tensor(f"ident_bf16_{m.phases}", [P, P], BF16))
        negb = ctx.enter_context(nc.sbuf_tensor(f"neg_bf16_{m.phases}", [P, 4, P], BF16))
        s = phase(m, "w_in rows_in pe act dve pool masks m_ready chain gated squares rooted normed y_sum")
        block = ctx.enter_context(nc.Block())

        order = [("X", "act", 0, 2), ("B", "act", 7, 1), ("R0", "act", 4, 1), ("R1", "act", 5, 1),
                 ("Z", "act", 6, 2), ("R2", "act", 4, 1), ("R3", "act", 5, 1), ("G", "act", 0, 2),
                 ("YO", "dve", 2, 2), ("ST", "dve", 6, 2), ("YD", "dve", 0, 2)]
        plan = [(c - (name == "G"), name, eng, bank, n) for c in range(TT) for name, eng, bank, n in order
                if name != "G" or c]
        plan.append((TT - 1, "G", "act", 0, 2))
        count, filled, emptied, before, last_in = {"act": 0, "dve": 0}, {}, {}, {}, {}
        for i, (c, name, eng, bank, n) in enumerate(plan):
            count[eng] += 1
            filled[c, name], emptied[c, name] = i + 1, (eng, count[eng])
            before[c, name] = sorted({last_in[b] for b in range(bank, bank + n) if b in last_in})
            for b in range(bank, bank + n):
                last_in[b] = (c, name)

        def empty(eng, key):
            who, n = emptied[key]
            eng.wait_ge(s.act if who == "act" else s.dve, n)

        by_head = lambda ap: ap.rearrange("p (h c) -> p h c", h=SH)
        wide = lambda ap, c: ap[:, c * SH:(c + 1) * SH].unsqueeze(2).to_broadcast([P, SH, HD])

        @block.sync
        def _(sp):
            sp.dma_start(W[:], w[:, O_ZS:O_XBC].rearrange("(k p) n -> p k n", p=P)).then_inc(s.w_in, 16)
            sp.dma_start(DS[:], d_skip.to_broadcast([P, SH])).then_inc(s.rows_in, 16)
            sp.dma_start(NW[:], norm_w.to_broadcast([P, DI])).then_inc(s.rows_in, 16)

        @block.tensor
        def _(pe):
            pe.wait_ge(s.masks, 3)
            for c, name, eng, bank, n in plan:
                for key in before[c, name]:
                    empty(pe, key)
                B = PS[:, bank, :]
                cols = slice(c * P, (c + 1) * P)
                if name == "X":
                    for q in range(KT):
                        last = pe.transpose(PS[:, bank + q // 4, (q % 4) * P:(q % 4 + 1) * P], XB[:, q, cols],
                                            m.const("ident"))
                elif name == "B":
                    for g in range(SG):
                        pe.transpose(B[:, g * P:(g + 1) * P], XB[:, KT + g, cols], m.const("ident"))
                    for g in range(SG):
                        last = pe.matmul(B[:, (2 + g) * P:(3 + g) * P], XB[:, KT + g, cols],
                                         XB[:, KT + SG + g, cols], start=True, stop=True)
                elif name[0] == "R":
                    r = int(name[1])
                    pe.matmul(B, identb[:], negb[:].rearrange("p a b -> p (a b)"), start=True, stop=False,
                              skip_group_check=True)
                    for i in range(4):
                        at = c * SH + 4 * r + i
                        last = pe.matmul(B[:, i * P:(i + 1) * P], DA[:, at:at + 1].to_broadcast([P, P]),
                                         m.const("tri"), start=False, stop=i == 3, skip_group_check=True)
                elif name == "Z":
                    if c == 0:
                        pe.wait_ge(s.w_in, 16)
                    for half in range(2):
                        for k in range(KT):
                            last = pe.matmul(PS[:, bank + half, :], HT[:, k, cols],
                                             W[:, k, half * NH:(half + 1) * NH], start=k == 0, stop=k == KT - 1)
                elif name == "G":
                    pe.wait_ge(s.normed, c + 1)
                    for q in range(KT):
                        last = pe.transpose(PS[:, bank + q // 4, (q % 4) * P:(q % 4 + 1) * P],
                                            Y[:, c % 2, q * P:(q + 1) * P], m.const("ident"))
                elif name == "YO":
                    if c:
                        empty(pe, (c - 1, "ST"))
                    for g in range(SG):
                        last = pe.matmul(PS[:, bank + g, :], XB[:, KT + SG + g, cols], S[:, g * GW:(g + 1) * GW],
                                         start=True, stop=True)
                elif name == "ST":
                    empty(pe, (c, "B"))
                    pe.wait_ge(s.pool, 3 * c + 3)
                    for g in range(SG):
                        last = pe.matmul(PS[:, bank + g, :], BC[:, g * P:(g + 1) * P], XDE[:, g * GW:(g + 1) * GW],
                                         start=True, stop=True)
                elif name == "YD":
                    pe.wait_ge(s.m_ready, 4 * c + 4)
                    for h in range(SH):
                        last = pe.matmul(PS[:, bank + h // 8, (h % 8) * HD:(h % 8 + 1) * HD], E[:, h],
                                         XDT[:, h * HD:(h + 1) * HD], start=True, stop=True)
                last.then_inc(s.pe, 1)

        @block.scalar
        def _(act):
            def squares(c):
                act.wait_ge(s.gated, c + 1)
                for g in range(SG):
                    nc.scalar.activation(tmp[:, g * GW:(g + 1) * GW], Y[:, c % 2, g * GW:(g + 1) * GW], ACT.Square,
                                         accum_out=st[:, 0, g:g + 1]).then_inc(s.squares, 1)
                act.wait_ge(s.squares, 2 * c + 2)
                nc.scalar.activation(st[:, 1], st[:, 0], ACT.Sqrt, scale=1.0 / GW, bias=eps).then_inc(s.rooted, 1)

            for c, name, eng, bank, n in plan:
                if eng != "act":
                    continue
                if name == "Z" and c:
                    squares(c - 1)
                if name == "G" and c == TT - 1:
                    squares(c)
                act.wait_ge(s.pe, filled[c, name])
                B = PS[:, bank, :]
                both = bank2(m, bank // 2)
                if name == "X":
                    if c:
                        act.wait_ge(s.pool, 3 * c)
                    ins = nc.scalar.copy(XS[:], both)
                elif name == "B":
                    ins = nc.scalar.copy(BC[:], B)
                elif name[0] == "R":
                    for i in range(4):
                        h = 4 * int(name[1]) + i
                        ins = nc.scalar.activation(E[:, h], B[:, i * P:(i + 1) * P], ACT.Exp,
                                                   bias=NA[:, c * SH + h:c * SH + h + 1])
                elif name == "Z":
                    ins = nc.scalar.activation(ZS[:], both, ACT.Silu)
                elif name == "G":
                    ins = nc.scalar.copy(HT[:, :, c * P:(c + 1) * P], PS[:, bank:bank + 2, :].rearrange(
                        "p a (b c) -> p (a b) c", b=4))
                ins.then_inc(s.act, 1)

        @block.gpsimd
        def _(pool):
            pool.wait_ge(s.rows_in, 32)
            v = nc.gpsimd
            for c in range(TT):
                empty(pool, (c, "X"))
                if c:
                    pool.wait_ge(s.pe, filled[c - 1, "YD"])
                v.tensor_tensor(by_head(XDT[:]), by_head(XS[:]), wide(DT, c), ALU.mult).then_inc(s.pool, 1)
                if c >= 2:
                    pool.wait_ge(s.pe, filled[c - 2, "G"])
                v.tensor_tensor(by_head(Y[:, c % 2]), by_head(XS[:]), DS[:].unsqueeze(2).to_broadcast([P, SH, HD]),
                                ALU.mult).then_inc(s.pool, 1)
                pool.wait_ge(s.pool, 3 * c + 1)
                v.tensor_tensor(by_head(XDE[:]), by_head(XDT[:]), wide(DE, c), ALU.mult).then_inc(s.pool, 1)

        @block.vector
        def _(dve):
            v = nc.vector
            do = Chain(dve, s.chain)
            v.tensor_copy(identb[:], m.const("ident")).then_inc(s.masks, 1)
            v.tensor_copy(negb[:], m.const("neg_up").unsqueeze(1).to_broadcast([P, 4, P])).then_inc(s.masks, 1)
            v.memset(eps, RMS_EPS_2)
            v.memset(S[:], 0.0).then_inc(s.masks, 1)
            dve.wait_ge(s.rows_in, 32)

            def normalise(c):
                dve.wait_ge(s.rooted, c + 1)
                do(v.reciprocal(st[:, 1], st[:, 1]))
                for g in range(SG):
                    gs = slice(g * GW, (g + 1) * GW)
                    ins = v.scalar_tensor_tensor(out=Y[:, c % 2, gs], in0=Y[:, c % 2, gs], scalar=st[:, 1, g:g + 1],
                                                 in1=NW[:, gs], op0=ALU.mult, op1=ALU.mult)
                    if g == 0:
                        do(ins)
                ins.then_inc(s.normed, 1)

            for c in range(TT):
                for r in range(4):
                    if r == 2 and c:
                        normalise(c - 1)
                    empty(dve, (c, "B"))
                    empty(dve, (c, f"R{r}"))
                    cb = BC[:, (2 + r // 2) * P:(3 + r // 2) * P].unsqueeze(1).to_broadcast([P, 4, P])
                    v.tensor_tensor(E[:, 4 * r:4 * r + 4], E[:, 4 * r:4 * r + 4], cb, ALU.mult).then_inc(s.m_ready, 1)
                pair = lambda b: PS[:, b:b + 2, :].rearrange("p a (h c) -> p (a h) c", c=HD)
                y = by_head(Y[:, c % 2])
                dve.wait_ge(s.pe, filled[c, "YO"])
                v.tensor_tensor(by_head(tmp[:]), pair(2), wide(EI, c), ALU.mult).then_inc(s.dve, 1)
                do(v.tensor_tensor(by_head(S[:]), by_head(S[:]), wide(CD, c), ALU.mult))
                dve.wait_ge(s.dve, emptied[c, "YO"][1])
                dve.wait_ge(s.pool, 3 * c + 2)
                do(v.tensor_tensor(Y[:, c % 2], Y[:, c % 2], tmp[:], ALU.add))
                dve.wait_ge(s.pe, filled[c, "ST"])
                v.tensor_tensor(S[:], S[:], PS[:, 6:8, :].rearrange("p a b -> p (a b)"), ALU.add).then_inc(s.dve, 1)
                dve.wait_ge(s.pe, filled[c, "YD"])
                v.tensor_tensor(y, y, pair(0), ALU.add).then_inc(s.dve, 1)
                dve.wait_ge(s.dve, emptied[c, "YD"][1])
                empty(dve, (c, "Z"))
                v.tensor_tensor(Y[:, c % 2], Y[:, c % 2], ZS[:], ALU.mult).then_inc(s.gated, 1)
            normalise(TT - 1)


def mix_and_norm(m, w, ln_g, ln_b, AT, src, dst):
    nc, t, PS = m.nc, m.t, m.PS
    with ExitStack() as ctx:
        W = alloc(m, ctx, "w_out", [P, 2, 2 * KT, NH])
        X = alloc(m, ctx, "x_tokens", [P, TT, D])
        LN = alloc(m, ctx, "ln_rows", [P, 2, D])
        s = phase(m, "w_in0 w_in1 x_in rows_in prod added eps summed mean centred squared root chain out stored")
        w_in = [s.w_in0, s.w_in1]
        block = ctx.enter_context(nc.Block())
        sums, mean, rstd, eps = (m.small[:, i * TT:(i + 1) * TT] for i in range(4))
        eps = eps[:, 0:1]
        junk = W[:, 0, 0:2].rearrange("p a b -> p (a b)")
        part = lambda q: AT[:, q] if q < KT else m.HT[:, q - KT]

        @block.sync
        def _(sp):
            for half in range(2):
                sp.dma_start(W[:, half], w[:, half * NH:(half + 1) * NH].rearrange("(k p) n -> p k n", p=P)
                             ).then_inc(w_in[half], 16)
                if half == 0:
                    sp.dma_start(X[:], src.rearrange("(k p) n -> p k n", p=P)).then_inc(s.x_in, 16)
            sp.dma_start(LN[:, 0], ln_g.to_broadcast([P, D])).then_inc(s.rows_in, 16)
            sp.dma_start(LN[:, 1], ln_b.to_broadcast([P, D])).then_inc(s.rows_in, 16)
            for k in range(TT):
                sp.wait_ge(s.out, k + 1)
                sp.dma_start(dst[k * P:(k + 1) * P], X[:, k]).then_inc(s.stored, 16)
            sp.wait_ge(s.stored, 16 * TT)

        @block.tensor
        def _(pe):
            for half in range(2):
                pe.wait_ge(w_in[half], 16)
                for k in range(TT):
                    if half:
                        pe.wait_ge(s.added, k + 1)
                    for q in range(2 * KT):
                        last = pe.matmul(PS[:, k, :], part(q)[:, k * P:(k + 1) * P], W[:, half, q],
                                         start=q == 0, stop=q == 2 * KT - 1)
                    last.then_inc(s.prod, 1)

        @block.scalar
        def _(act):
            act.wait_ge(s.eps, 1)
            for k in range(TT):
                act.wait_ge(s.added, TT + k + 1)
                if k:
                    act.wait_ge(s.squared, k)
                nc.scalar.activation(junk, X[:, k], ACT.Identity, accum_out=sums[:, k:k + 1]).then_inc(s.summed, 1)
                act.wait_ge(s.centred, k + 1)
                act.wait_ge(s.summed, k + 1)
                nc.scalar.activation(junk, X[:, k], ACT.Square, accum_out=sums[:, k:k + 1]).then_inc(s.squared, 1)
                act.wait_ge(s.squared, k + 1)
                nc.scalar.activation(rstd[:, k:k + 1], sums[:, k:k + 1], ACT.Sqrt, scale=1.0 / D, bias=eps
                                     ).then_inc(s.root, 1)

        @block.vector
        def _(dve):
            v = nc.vector
            do = Chain(dve, s.chain)
            v.memset(eps, LN_EPS).then_inc(s.eps, 1)
            dve.wait_ge(s.x_in, 16)
            dve.wait_ge(s.rows_in, 32)
            for half in range(2):
                for k in range(TT):
                    x = X[:, k, half * NH:(half + 1) * NH]
                    dve.wait_ge(s.prod, half * TT + k + 1)
                    v.scalar_tensor_tensor(out=x, in0=x, scalar=ALPHA, in1=PS[:, k, :], op0=ALU.mult, op1=ALU.add
                                           ).then_inc(s.added, 1)
                    if half:
                        dve.wait_ge(s.summed, k + 1)
                        do(v.tensor_scalar(mean[:, k:k + 1], sums[:, k:k + 1], 1.0 / D, None, ALU.mult))
                        v.tensor_scalar(X[:, k], X[:, k], mean[:, k:k + 1], None, ALU.subtract).then_inc(s.centred, 1)
                        dve.wait_ge(s.root, k + 1)
                        do(v.reciprocal(rstd[:, k:k + 1], rstd[:, k:k + 1]))
                        do(v.scalar_tensor_tensor(out=X[:, k], in0=X[:, k], scalar=rstd[:, k:k + 1], in1=LN[:, 0],
                                                  op0=ALU.mult, op1=ALU.mult))
                        v.tensor_tensor(X[:, k], X[:, k], LN[:, 1], ALU.add).then_inc(s.out, 1)


def move(m, src, dst):
    nc = m.nc
    with nc.Block() as block:
        @block.vector
        def _(dve):
            for k in range(0, TT, 2):
                nc.vector.tensor_copy(dst[:, k], src[:, k])

        @block.scalar
        def _(act):
            for k in range(1, TT, 2):
                nc.scalar.copy(dst[:, k], src[:, k])


def first_block(m, dst):
    nc, t = m.nc, m.t
    with ExitStack() as whole:
        GM = alloc(m, whole, "gates", [P, 2, D])
        with ExitStack() as ctx:
            X = alloc(m, ctx, "x", [P, TT, D])
            modulation(m, X, GM)
            to_channels(m, X, 0)
        with ExitStack() as ctx:
            MIX = alloc(m, ctx, "mix", [P, CT, T])
            RKVQ = alloc(m, ctx, "rkvq", [P, 4 * CT, T])
            LO = alloc(m, ctx, "lora", [P, 3, T])
            with ExitStack() as slots:
                W = alloc(m, slots, "w_in_slots", [P, 2, KT, 2 * P])
                in_projection(m, MIX, RKVQ, LO, W)
            conv_branch(m, MIX)
            with ExitStack() as inner:
                G2 = alloc(m, inner, "g2", [P, 2, CW])
                PC = alloc(m, inner, "chunk_decay", [P, CT, T // CH])
                bonus = alloc(m, inner, "bonus", [P, TT * RH])
                rwkv_operands(m, RKVQ, LO, G2, m.HT[:, 0:CT], m.HT[:, CT:2 * CT], PC, bonus)
                rwkv_recurrence(m, RKVQ, m.HT[:, 0:CT], PC, LO, G2, bonus)
            tiles = [MIX[:, q] for q in range(CT)] + [RKVQ[:, 2 * CT + q] for q in range(CT)]
            out_projection(m, tiles, t.w_out, GM[:, 0], m.HT)
        X = alloc(m, whole, "x_mixed", [P, TT, D])
        move(m, m.HT, X)
        to_channels(m, X, 1)
        with ExitStack() as ctx:
            MID = alloc(m, ctx, "mid", [P, FT, T])
            up_projection(m, MID)
            down_projection(m, MID, GM[:, 1], X, dst)


def second_layer(m, i, src, dst):
    t = m.t
    row = lambda ap: ap[i:i + 1]
    with ExitStack() as whole:
        AT = alloc(m, whole, "attn_out", [P, KT, T])
        load_channels(m, src)
        with ExitStack() as ctx:
            QT = alloc(m, ctx, "q", [P, KT, T])
            KH = alloc(m, ctx, "k", [P, 4, T])
            V = alloc(m, ctx, "v", [P, TT, KVW])
            qkv_projection(m, t.w_in_2[i], QT, KH, V)
            attention(m, row(t.sinks_2), QT, KH, V, AT)
        with ExitStack() as ctx:
            XB = alloc(m, ctx, "xbc", [P, XT, T])
            DT, DA, NA, EI, DE, CD = (alloc(m, ctx, n, [P, TT * SH]) for n in ("dt", "dta", "na", "ei", "de", "cd"))
            gates_and_xbc(m, i, t.w_in_2[i], AT, XB, DT)
            step_sizes(m, row(t.dt_bias_2), row(t.a_log_2), DT, NA, EI, DE, CD, DA)
            state_space(m, t.w_in_2[i], row(t.d_skip_2), row(t.ssm_norm_w_2), XB, DT, DA, NA, EI, DE, CD)
        mix_and_norm(m, t.w_out_2[i], row(t.ln_g_2), row(t.ln_b_2), AT, src, dst)


def hybrid_kernel(nc, t):
    m = make(nc, t)
    x1 = nc.dram_tensor("after_first_block", (T, D), F32, kind="Internal").ap()
    x2 = nc.dram_tensor("after_first_layer", (T, D), F32, kind="Internal").ap()
    first_block(m, x1)
    recycle(m)
    second_layer(m, 0, x1, x2)
    recycle(m)
    second_layer(m, 1, x2, t.out)
    m.ctx.close()


def laid_out(inputs):
    import numpy as _np

    a = {k: _np.ascontiguousarray(v) for k, v in inputs.items()}
    column = lambda v: v.reshape(-1, P).T
    taps = lambda w: _np.transpose(w.reshape(w.shape[0], -1, P), (2, 1, 0)).reshape(P, -1)
    mu = _np.zeros((15 * P,), a["rwkv_mu"].dtype)
    mu[:a["rwkv_mu"].shape[1]] = a["rwkv_mu"][0]
    ada = a["ada_b"][0].reshape(6, D)
    parts = {
        "c": column(a["c"][0]), "ada_b": _np.concatenate([column(ada[i]) for i in (0, 1, 3, 4)], axis=1),
        "pre_g": _np.concatenate([column(a["mix_pre_g"][0]), column(a["ffn_pre_g"][0])], axis=1),
        "mu": column(mu), "conv_b": column(a["conv_dw_b"][0]), "conv_ln_g": column(a["conv_ln_g"][0]),
        "conv_ln_b": column(a["conv_ln_b"][0]), "w0": column(a["w0"][0]), "a0": column(a["a0"][0]),
        "k_k": column(a["k_k"][0]), "k_a": column(a["k_a"][0]), "r_k": column(a["r_k"][0].reshape(-1)),
        "conv_w": taps(a["conv_dw_w"][0]), "ffn_b": column(a["ffn_dw_b"][0]), "ffn_w": taps(a["ffn_dw_w"][0]),
        "conv_b_2": _np.concatenate([column(a["conv_b_2"][i]) for i in range(LAYERS)], axis=1),
        "conv_w_2": _np.concatenate([taps(a["conv_w_2"][i]) for i in range(LAYERS)], axis=1),
    }
    consts, alibi = shape_constants()
    arrays = {
        "cols": _np.ascontiguousarray(_np.concatenate([parts[n] for n in COLS], axis=1)),
        "consts": consts, "alibi": alibi, "x": a["x"][0],
    }
    for name in ("ada_w", "w_in", "w_out", "w_up", "w_down", "w2", "a2", "g2"):
        arrays[name] = a[name][0]
    for name in ("ada_b", "mix_post_g", "ffn_post_g", "lnx_g", "lnx_b"):
        arrays[name] = a[name]
    for name in ("w_in_2", "w_out_2"):
        arrays[name] = a[name]
    for name in ("dt_bias_2", "a_log_2", "d_skip_2", "ssm_norm_w_2", "sinks_2", "ln_g_2", "ln_b_2"):
        arrays[name] = a[name]
    return {k: _np.ascontiguousarray(v) for k, v in arrays.items()}


def kernel(**inputs):
    from collections import namedtuple as _namedtuple

    import concourse.bacc as _bacc
    from concourse import mybir as _mybir
    from concourse.bass_utils import run_bass_kernel_spmd as _run

    nc = _bacc.Bacc("TRN2", target_bir_lowering=False, num_devices=1)
    arrays = laid_out(inputs)
    tensors = {
        n: nc.dram_tensor(n, a.shape, _mybir.dt.from_np(a.dtype), kind="ExternalInput").ap()
        for n, a in arrays.items()
    }
    tensors["out"] = nc.dram_tensor("out", (T, D), F32, kind="ExternalOutput").ap()
    t = _namedtuple("Tensors", list(tensors))(*tensors.values())
    hybrid_kernel(nc, t)
    r = _run(nc, [arrays], core_ids=[0])
    return r.results[0]["out"].reshape(1, T, D)
```

```python
from collections import namedtuple
from contextlib import ExitStack

import numpy as np

import concourse.bass as bass
from concourse import mybir

F32 = mybir.dt.float32
F32R = mybir.dt.float32r
ACT = mybir.ActivationFunctionType
ALU = mybir.AluOpType
AX = mybir.AxisListType.X

P = 128
T = 1024
D = 1024
TT = T // P
KT = D // P
NH = T // 2
CW = 512
CT = CW // P
CONV_K = 31
CPAD = CONV_K - 1
HD = 64
RH = CW // HD
LORA = 64
GLORA = 160
CH = 64
BLK = 16
D_FF = 2816
FT = D_FF // P
RMS_EPS, LN_EPS, LNX_EPS, RMS_EPS_2 = 1e-6, 1e-5, 64e-5, 1e-5
DECAY = float(np.exp(-0.5))

LAYERS = 2
QH, KVH = 16, 4
KVW = KVH * HD
DI = 1024
SH = DI // HD
SG = 2
HG = SH // SG
NS = 128
XBC = DI + 2 * SG * NS
XT = XBC // P
O_Q, O_K, O_V, O_ZA = 0, D, D + KVW, D + 2 * KVW
O_ZS = O_ZA + D
O_XBC = O_ZS + DI
O_DT = O_XBC + XBC
IN_W = O_DT + SH
ALPHA = (2.0 * LAYERS) ** 0.25
CK2 = 4

COLS = {}
for _name, _n in [
    ("c", KT), ("ada_b", 4 * KT), ("pre_g", 2 * KT), ("mu", 15), ("conv_b", CT), ("conv_ln_g", CT),
    ("conv_ln_b", CT), ("w0", CT), ("a0", CT), ("k_k", CT), ("k_a", CT), ("r_k", CT),
    ("conv_w", CT * CONV_K), ("ffn_b", 2 * FT), ("ffn_w", 2 * FT * 3),
    ("conv_b_2", LAYERS * XT), ("conv_w_2", LAYERS * XT * CK2),
    ("norm_w_2", LAYERS * KT),
]:
    COLS[_name] = (sum(n for _, n in COLS.values()), _n)
NCOLS = sum(n for _, n in COLS.values())

CONSTS = {}
for _name, _n in [
    ("ident", P), ("ones", P), ("headones", P), ("mask_incl_up", P), ("mask_diag_up", P), ("mask_incl_up_2", P), ("mask_strict_up", P),
    ("mask_diag_low", P), ("mask_off_low", P), ("chunk_row", T), ("tri", P), ("neg_up", P), ("minus_last", P),
    ("ident_heads", HD),
]:
    CONSTS[_name] = (sum(n for _, n in CONSTS.values()), _n)
NCONSTS = sum(n for _, n in CONSTS.values())


def shape_constants():
    i, j = np.arange(P)[:, None], np.arange(P)[None, :]
    chunk = (i // CH) == (j // CH)
    block = (i // BLK) == (j // BLK)
    parts = {
        "ident": i == j, "ones": i >= 0 * j, "headones": (i // HD) == (j // HD),
        "mask_diag_up": block & (i < j), "mask_incl_up": chunk & (i <= j), "mask_strict_up": chunk & (i < j),
        "mask_incl_up_2": chunk & (i <= j), "ident_heads": (i % HD) == np.arange(HD)[None, :],
        "mask_diag_low": block & (i > j), "mask_off_low": chunk & ~block & (i > j),
        "chunk_row": np.broadcast_to(np.arange(T) % CH != 0, (P, T)), "tri": i <= j,
        "neg_up": np.where(i > j, -1e30, 0.0), "minus_last": np.where((i == P - 1) & (j >= 0), -1.0, 0.0),
    }
    consts = np.concatenate([np.asarray(parts[n]).astype(np.float32) for n in CONSTS], axis=1)
    q, s = np.arange(P)[:, None], np.arange(2 * P)[None, :]
    dist = q - s + P
    slopes = 2.0 ** (-8.0 * np.arange(1, QH + 1) / QH)
    alibi = np.where((dist >= 0) & (dist < P), -8.0 * slopes[:, None, None] * dist, -1e30)
    return consts, np.ascontiguousarray(alibi.transpose(1, 0, 2).astype(np.float32))


def flat(ap):
    return ap.rearrange("p a b -> p (a b)")


def alloc(m, ctx, name, shape, dtype=F32):
    m.tensors += 1
    return ctx.enter_context(m.nc.sbuf_tensor(f"{name}_sb{m.tensors}", shape, dtype))


class Machine:

    def __init__(self, nc, t):
        self.nc, self.t = nc, t
        self.ctx = ExitStack()
        self.tensors = 0
        self.phases = 0
        self.used = []


def make(nc, t):
    m = Machine(nc, t)
    sb = lambda name, shape: alloc(m, m.ctx, name, shape)
    m.PS = m.ctx.enter_context(nc.psum_tensor("PS", [P, 8, 512], F32))
    m.cols = sb("cols", [P, NCOLS])
    m.consts = sb("consts", [P, NCONSTS])
    m.mod_shift = sb("mod_shift", [P, 2, KT])
    m.mod_scale = sb("mod_scale", [P, 2, KT])
    m.small = sb("small", [P, 64])
    m.HT = sb("HT", [P, KT, T])
    m.col = lambda name, k=0, n=1: m.cols[:, COLS[name][0] + k:COLS[name][0] + k + n]
    m.const = lambda name: m.consts[:, CONSTS[name][0]:CONSTS[name][0] + CONSTS[name][1]]
    return m


class Chain:

    def __init__(self, eng, sem):
        self.eng, self.sem, self.n = eng, sem, 0

    def __call__(self, ins):
        self.n += 1
        ins.then_inc(self.sem, 1)
        self.eng.wait_ge(self.sem, self.n)


def phase(m, names):
    m.phases += 1
    handles = [m.nc.alloc_semaphore(f"{n}_{m.phases}") for n in names.split()]
    m.used += handles
    return namedtuple("Signals", names)(*handles)


def recycle(m):
    m.nc.clear_and_free_semaphores(m.used)
    m.used = []
    m.nc.all_engine_barrier()


def modulation(m, X, GM):
    nc, t, PS = m.nc, m.t, m.PS
    with ExitStack() as ctx:
        W = alloc(m, ctx, "ada_slots", [P, 3, KT, 512])
        rows = alloc(m, ctx, "gate_rows", [P, 2, 2, D])
        silu_c = alloc(m, ctx, "silu_c", [P, KT])
        silu_cb = alloc(m, ctx, "silu_cb", [P, KT, P])
        biased = alloc(m, ctx, "biased", [P, 2, 2 * KT])
        s = phase(m, "par_in x_in rows_in w_in0 w_in1 w_in2 slot_free silu silub col_done row_done biased scaled gate")
        w_in = [s.w_in0, s.w_in1, s.w_in2]
        block = ctx.enter_context(nc.Block())

        @block.sync
        def _(sp):
            sp.dma_start(m.cols[:], t.cols).then_inc(s.par_in, 16)
            sp.dma_start(m.consts[:], t.consts).then_inc(s.par_in, 16)
            with sp.Fori(0, 2) as i:
                at = [sp.snap(i * (3 * D) + b * 512) for b in range(6)]
                for b in range(6):
                    sp.wait_ge(s.slot_free, i * 6 + b + 1)
                    sp.dma_start(W[:, b % 3], t.ada_w[:, bass.ds(at[b], 512)].rearrange("(k p) n -> p k n", p=P)
                                 ).then_inc(w_in[b % 3], 16)

        @block.gpsimd
        def _(pool):
            for i, g in enumerate((t.mix_post_g, t.ffn_post_g)):
                pool.dma_start(rows[:, i, 0], t.ada_b[:, (3 * i + 2) * D:(3 * i + 3) * D].to_broadcast([P, D])
                               ).then_inc(s.rows_in, 16)
                pool.dma_start(rows[:, i, 1], g.to_broadcast([P, D])).then_inc(s.rows_in, 16)

        @block.scalar
        def _(act):
            for k in range(TT):
                act.dma_start(X[:, k], t.x[k * P:(k + 1) * P]).then_inc(s.x_in, 16)
            act.wait_ge(s.par_in, 32)
            nc.scalar.activation(silu_c[:], m.col("c", 0, KT), ACT.Silu).then_inc(s.silu, 1)

        @block.vector
        def _(dve):
            dve.wait_ge(s.silu, 1)
            for k in range(KT):
                nc.vector.tensor_scalar(silu_cb[:, k], m.const("ones"), silu_c[:, k:k + 1], None, ALU.mult
                                        ).then_inc(s.silub, 1)
            dve.wait_ge(s.col_done, 2)
            nc.vector.tensor_tensor(flat(biased[:]), PS[:, 0, 0:4 * KT], m.col("ada_b", 0, 4 * KT), ALU.add
                                    ).then_inc(s.biased, 1)
            dve.wait_ge(s.biased, 1)
            nc.vector.tensor_copy(m.mod_shift[:], biased[:, :, 0:KT]).then_inc(s.scaled, 1)
            nc.vector.scalar_tensor_tensor(out=m.mod_scale[:], in0=biased[:, :, KT:2 * KT], scalar=1.0,
                                           in1=m.col("pre_g", 0, 2 * KT).rearrange("p (a b) -> p a b", a=2),
                                           op0=ALU.add, op1=ALU.mult).then_inc(s.scaled, 1)
            dve.wait_ge(s.rows_in, 64)
            dve.wait_ge(s.x_in, 16 * TT)
            dve.wait_ge(s.row_done, 2)
            for i in range(2):
                nc.vector.tensor_tensor(GM[:, i], flat(PS[:, 2 + 2 * i:4 + 2 * i]), rows[:, i, 0], ALU.add
                                        ).then_inc(s.gate, 1)
            dve.wait_ge(s.gate, 2)
            for i in range(2):
                nc.vector.tensor_tensor(GM[:, i], GM[:, i], rows[:, i, 1], ALU.mult).then_inc(s.gate, 1)

        @block.tensor
        def _(pe):
            pe.sem_inc(s.slot_free, 3)
            pe.wait_ge(s.silub, KT)
            with pe.Fori(0, 2) as i:
                for b in range(6):
                    pe.wait_ge(w_in[b % 3], (i * 2 + b // 3 + 1) * 16)
                    if b < 4:
                        for j in range(4):
                            for k in range(KT):
                                last = pe.matmul(PS[:, 0, bass.ds(i * 16 + b * 4 + j, 1)],
                                                 W[:, b % 3, k, j * P:(j + 1) * P], silu_c[:, k:k + 1],
                                                 start=k == 0, stop=k == KT - 1)
                        if b == 3:
                            last.then_inc(s.col_done, 1)
                            pe.wait_ge(s.col_done, i + 1)
                            pe.sem_inc(s.slot_free, 1)
                            continue
                    else:
                        for k in range(KT):
                            last = pe.matmul(PS[:, bass.ds(i * 2 + b - 2, 1), :], silu_cb[:, k], W[:, b % 3, k],
                                             start=k == 0, stop=k == KT - 1)
                        if b == 5:
                            last.then_inc(s.row_done, 1)
                            pe.wait_ge(s.row_done, i + 1)
                            pe.sem_inc(s.slot_free, 1)
                            continue
                    last.then_inc(s.slot_free, 1)


def to_channels(m, X, norm=None):
    nc, PS, HT = m.nc, m.PS, m.HT
    with ExitStack() as ctx:
        src = X
        if norm is not None:
            src = alloc(m, ctx, "normed", [P, TT, D])
        s = phase(m, "sq eps rms rstd normed turned ev_act ev_dve")
        block = ctx.enter_context(nc.Block())
        ss, rstd, eps = m.small[:, 0:TT], m.small[:, TT:2 * TT], m.small[:, 2 * TT:2 * TT + 1]

        @block.tensor
        def _(pe):
            for half in range(2):
                if norm is not None:
                    pe.wait_ge(s.normed, 4 * half + 4)
                for k in range(KT):
                    if half:
                        pe.wait_ge(s.ev_dve if k % 2 else s.ev_act, k // 2 + 1)
                    for j in range(4):
                        last = pe.transpose(PS[:, k, j * P:(j + 1) * P],
                                            src[:, 4 * half + j, k * P:(k + 1) * P], m.const("ident"))
                    last.then_inc(s.turned, 1)

        @block.scalar
        def _(act):
            if norm is not None:
                for k in range(TT):
                    nc.scalar.activation(src[:, k], X[:, k], ACT.Square, accum_out=ss[:, k:k + 1]).then_inc(s.sq, 1)
                act.wait_ge(s.sq, TT)
                act.wait_ge(s.eps, 1)
                nc.scalar.activation(rstd, ss, ACT.Sqrt, scale=1.0 / D, bias=eps).then_inc(s.rms, 1)
            for n in range(0, 2 * KT, 2):
                half, k = n // KT, n % KT
                act.wait_ge(s.turned, n + 1)
                out = HT[:, k, half * NH:(half + 1) * NH]
                if norm is None:
                    nc.scalar.copy(out, PS[:, k, :]).then_inc(s.ev_act, 1)
                else:
                    nc.scalar.activation(out, PS[:, k, :], ACT.Identity, scale=m.mod_scale[:, norm, k:k + 1],
                                         bias=m.mod_shift[:, norm, k:k + 1]).then_inc(s.ev_act, 1)

        @block.vector
        def _(dve):
            if norm is not None:
                nc.vector.memset(eps, RMS_EPS).then_inc(s.eps, 1)
                dve.wait_ge(s.rms, 1)
                nc.vector.reciprocal(rstd, rstd).then_inc(s.rstd, 1)
                dve.wait_ge(s.rstd, 1)
                for k in range(TT):
                    nc.vector.tensor_scalar(src[:, k], X[:, k], rstd[:, k:k + 1], None, ALU.mult
                                            ).then_inc(s.normed, 1)
            for n in range(1, 2 * KT, 2):
                half, k = n // KT, n % KT
                dve.wait_ge(s.turned, n + 1)
                out = HT[:, k, half * NH:(half + 1) * NH]
                if norm is None:
                    nc.vector.tensor_copy(out, PS[:, k, :]).then_inc(s.ev_dve, 1)
                else:
                    nc.vector.tensor_scalar(out, PS[:, k, :], m.mod_scale[:, norm, k:k + 1],
                                            m.mod_shift[:, norm, k:k + 1], ALU.mult, ALU.add).then_inc(s.ev_dve, 1)


def tile_product(m, pe, W, slot, c, bank, width=P):
    for half in range(2):
        for k in range(KT):
            last = pe.matmul(m.PS[0:width, 2 * bank + half, :], W[:, slot, k, c * P:c * P + width],
                             m.HT[:, k, half * NH:(half + 1) * NH], start=k == 0, stop=k == KT - 1)
    return last


def bank2(m, b, rows=P):
    return m.PS[0:rows, 2 * b:2 * b + 2, :].rearrange("p a b -> p (a b)")


def in_projection(m, MIX, RKVQ, LO, W):
    nc, t, PS = m.nc, m.t, m.PS
    with ExitStack() as ctx:
        U = alloc(m, ctx, "U", [P, CT, T + 32])
        sig = alloc(m, ctx, "sig", [P, 2, T])
        om = alloc(m, ctx, "one_minus_mu", [P, 15])
        s = phase(m, "w_in0 w_in1 slot_free tile_done ps_free om pad gated part conv lora")
        w_in = [s.w_in0, s.w_in1]
        block = ctx.enter_context(nc.Block())
        mu = lambda k: m.col("mu", k)

        def load(sp, slot, c, at, width=P):
            sp.dma_start(W[:, slot, :, c * P:c * P + width],
                         t.w_in[:, bass.ds(at, width)].rearrange("(k p) n -> p k n", p=P)).then_inc(w_in[slot], 16)

        @block.sync
        def _(sp):
            with sp.Fori(0, 2) as i:
                at = [[sp.snap(i * 2 * P + j * P + c * CW) for c in range(2)] for j in range(2)]
                for j in range(2):
                    sp.wait_ge(s.slot_free, i * 2 + j + 1)
                    for c in range(2):
                        load(sp, j, c, at[j][c])
            with sp.Fori(0, 3) as i:
                at = [[sp.snap(i * CW + (2 * j + c) * P + 2 * CW) for c in range(2)] for j in range(2)]
                for j in range(2):
                    sp.wait_ge(s.slot_free, i * 2 + j + 5)
                    for c in range(2):
                        load(sp, j, c, at[j][c])
            base = 5 * CW
            sp.wait_ge(s.slot_free, 11)
            load(sp, 0, 0, base)
            load(sp, 0, 1, base + P)
            sp.wait_ge(s.slot_free, 12)
            load(sp, 1, 0, base + 2 * P, 32)

        @block.tensor
        def _(pe):
            pe.sem_inc(s.slot_free, 2)
            with pe.Fori(0, 5) as i:
                for j in range(2):
                    pe.wait_ge(w_in[j], (i + 1) * 32)
                    for c in range(2):
                        pe.wait_ge(s.ps_free, i * 4 + 2 * j + c + 1)
                        tile_product(m, pe, W, j, c, 2 * j + c).then_inc(s.tile_done, 1)
                    pe.wait_ge(s.tile_done, i * 4 + 2 * j + 2)
                    pe.sem_inc(s.slot_free, 1)
            for n, (j, c, width) in enumerate(((0, 0, P), (0, 1, P), (1, 0, 32))):
                if c == 0:
                    pe.wait_ge(w_in[j], 5 * 32 + (32 if j == 0 else 16))
                pe.wait_ge(s.ps_free, 20 + n + 1)
                tile_product(m, pe, W, j, c, n, width).then_inc(s.tile_done, 1)

        @block.scalar
        def _(act):
            with act.Fori(0, 2) as i:
                for j in range(2):
                    act.wait_ge(s.tile_done, i * 4 + 2 * j + 2)
                    act.wait_ge(s.ps_free, i * 4 + 2 * j + 2)
                    nc.scalar.activation(sig[:, j], bank2(m, 2 * j + 1), ACT.Sigmoid).then_inc(s.gated, 1)
            act.wait_ge(s.om, 1)
            with act.Fori(0, 3) as i:
                for j in range(4):
                    act.wait_ge(s.tile_done, i * 4 + j + 9)
                    nc.scalar.activation(RKVQ[:, bass.ds(i * 4 + j, 1), :].rearrange("p a b -> p (a b)"),
                                         bank2(m, j), ACT.Identity, scale=om[:, bass.ds(i * 4 + j, 1)]
                                         ).then_inc(s.part, 1)
            for n in range(3):
                rows = 32 if n == 2 else P
                act.wait_ge(s.tile_done, 21 + n)
                nc.scalar.activation(LO[0:rows, n], bank2(m, n, rows), ACT.Identity,
                                     scale=om[0:rows, 12 + n:13 + n]).then_inc(s.part, 1)
            for n in range(3):
                rows = (LORA, P, 32)[n]
                act.wait_ge(s.lora, n + 1)
                nc.scalar.activation(LO[0:rows, n], LO[0:rows, n], ACT.Sigmoid if n else ACT.Tanh)

        @block.vector
        def _(dve):
            dve.sem_inc(s.ps_free, 4)
            nc.vector.tensor_scalar(om[:], m.col("mu", 0, 15), -1.0, 1.0, ALU.mult, ALU.add).then_inc(s.om, 1)
            nc.vector.memset(U[:, :, 0:CPAD], 0.0).then_inc(s.pad, 1)
            with dve.Fori(0, 2) as i:
                for j in range(2):
                    dve.wait_ge(s.gated, i * 2 + j + 1)
                    u = U[:, bass.ds(i * 2 + j, 1), CPAD:CPAD + T].rearrange("p a b -> p (a b)")
                    nc.vector.tensor_tensor(u, bank2(m, 2 * j), sig[:, j], ALU.mult).then_inc(s.ps_free, 2)
            dve.wait_ge(s.pad, 1)

            def conv(q, first):
                out = MIX[:, bass.ds(q, 1), :].rearrange("p a b -> p (a b)")
                for k in range(CONV_K):
                    u = U[:, bass.ds(q, 1), k:k + T].rearrange("p a b -> p (a b)")
                    w = m.cols[:, bass.ds(q * CONV_K + COLS["conv_w"][0] + k, 1)]
                    if k == 0:
                        ins = nc.vector.tensor_scalar(out, u, w, m.cols[:, bass.ds(q + COLS["conv_b"][0], 1)],
                                                      ALU.mult, ALU.add)
                    else:
                        ins = nc.vector.scalar_tensor_tensor(out=out, in0=u, scalar=w, in1=out,
                                                             op0=ALU.mult, op1=ALU.add)
                    ins.then_inc(s.conv, 1)
                    dve.wait_ge(s.conv, first + k + 1)

            with dve.Fori(0, 3) as i:
                for j in range(4):
                    dve.wait_ge(s.part, i * 4 + j + 1)
                    row = RKVQ[:, bass.ds(i * 4 + j, 1), 1:T].rearrange("p a b -> p (a b)")
                    nc.vector.scalar_tensor_tensor(out=row, in0=bank2(m, j)[:, 0:T - 1],
                                                   scalar=m.cols[:, bass.ds(i * 4 + COLS["mu"][0] + j, 1)], in1=row,
                                                   op0=ALU.mult, op1=ALU.add).then_inc(s.ps_free, 1)
                conv(i, i * CONV_K)
            for n in range(3):
                rows = 32 if n == 2 else P
                dve.wait_ge(s.part, 12 + n + 1)
                nc.vector.scalar_tensor_tensor(out=LO[0:rows, n, 1:T], in0=bank2(m, n, rows)[:, 0:T - 1],
                                               scalar=m.col("mu", 12 + n)[0:rows], in1=LO[0:rows, n, 1:T],
                                               op0=ALU.mult, op1=ALU.add).then_inc(s.lora, 1)
            conv(3, 3 * CONV_K)


def conv_branch(m, MIX):
    nc, PS = m.nc, m.PS
    with ExitStack() as ctx:
        mean = alloc(m, ctx, "mean", [P, T])
        rstd = alloc(m, ctx, "rstd", [P, T])
        sq = alloc(m, ctx, "squares", [P, CT, T])
        s = phase(m, "eps sums mean centred sq vars root chain out")
        block = ctx.enter_context(nc.Block())
        eps = m.small[:, 0:1]

        @block.tensor
        def _(pe):
            def sum_tiles(src, bank):
                for half in range(2):
                    for q in range(CT):
                        last = pe.matmul(PS[:, 2 * bank + half, :], m.const("ones"),
                                         src[:, q, half * NH:(half + 1) * NH], start=q == 0, stop=q == CT - 1)
                last.then_inc(s.sums, 1)

            sum_tiles(MIX, 0)
            pe.wait_ge(s.sq, CT)
            sum_tiles(sq, 1)

        @block.scalar
        def _(act):
            act.wait_ge(s.sums, 1)
            nc.scalar.mul(mean[:], bank2(m, 0), 1.0 / CW).then_inc(s.mean, 1)
            for q in range(CT):
                act.wait_ge(s.centred, q + 1)
                nc.scalar.activation(sq[:, q], MIX[:, q], ACT.Square).then_inc(s.sq, 1)
            act.wait_ge(s.sums, 2)
            act.wait_ge(s.eps, 1)
            nc.scalar.activation(rstd[:], bank2(m, 1), ACT.Sqrt, scale=1.0 / CW, bias=eps).then_inc(s.root, 1)
            for q in range(CT):
                act.wait_ge(s.out, q + 1)
                nc.scalar.activation(MIX[:, q], MIX[:, q], ACT.Silu, scale=m.col("conv_ln_g", q),
                                     bias=m.col("conv_ln_b", q))

        @block.vector
        def _(dve):
            nc.vector.memset(eps, LN_EPS).then_inc(s.eps, 1)
            dve.wait_ge(s.mean, 1)
            for q in range(CT):
                nc.vector.tensor_tensor(MIX[:, q], MIX[:, q], mean[:], ALU.subtract).then_inc(s.centred, 1)
            dve.wait_ge(s.root, 1)
            nc.vector.reciprocal(rstd[:], rstd[:]).then_inc(s.chain, 1)
            dve.wait_ge(s.chain, 1)
            for q in range(CT):
                nc.vector.tensor_tensor(MIX[:, q], MIX[:, q], rstd[:], ALU.mult).then_inc(s.out, 1)


def rwkv_operands(m, RKVQ, LO, G2, A, CS, PC, bonus):
    nc, t, PS = m.nc, m.t, m.PS
    with ExitStack() as ctx:
        WA = alloc(m, ctx, "lora_w", [P, CW])
        rk_col = alloc(m, ctx, "rk_col", [P, CT, 2])
        om = alloc(m, ctx, "one_minus_ka", [P, CT])
        sq = alloc(m, ctx, "key_squares", [P, 2, T])
        nrm = alloc(m, ctx, "key_norm", [P, 2, T])
        tmp = alloc(m, ctx, "tmp", [P, 2, T])
        ex = alloc(m, ctx, "exps", [P, 3, T])
        SG_ = CS
        s = phase(m, "w_in g_in z sig sq ss root kkn scan dif e1 e2 e3 rk bonus cd cdb e3_used chain small ks")
        block = ctx.enter_context(nc.Block())
        R = lambda q: RKVQ[:, q]
        K = lambda q: RKVQ[:, CT + q]
        Q = lambda q: RKVQ[:, 3 * CT + q]

        @block.sync
        def _(sp):
            sp.dma_start(WA[0:LORA], t.w2).then_inc(s.w_in, 16)
            sp.dma_start(WA[LORA:P], t.a2).then_inc(s.w_in, 16)
            sp.dma_start(G2[:, 0], t.g2[0:P]).then_inc(s.g_in, 16)
            sp.dma_start(G2[0:GLORA - P, 1], t.g2[P:GLORA]).then_inc(s.g_in, 16)
            sp.wait_ge(s.g_in, 32)

        @block.tensor
        def _(pe):
            pe.wait_ge(s.w_in, 32)
            for q in range(CT):
                if q >= 2:
                    pe.wait_ge(s.sig, 2 * (q - 1))
                for side in range(2):
                    for half in range(2):
                        last = pe.matmul(PS[:, 4 * (q % 2) + 2 * side + half, :],
                                         WA[LORA * side:LORA * side + LORA, q * P:(q + 1) * P],
                                         LO[LORA * side:LORA * side + LORA, 0, half * NH:(half + 1) * NH],
                                         start=True, stop=True)
                last.then_inc(s.z, 1)
            for q in range(CT):
                pe.wait_ge(s.sq, q + 1)
                pe.wait_ge(s.sig, 2 * CT)
                if q >= 2:
                    pe.wait_ge(s.root, q - 1)
                for half in range(2):
                    last = pe.matmul(PS[:, 2 * (q % 2) + half, :], m.const("headones"),
                                     sq[:, q % 2, half * NH:(half + 1) * NH], start=True, stop=True)
                last.then_inc(s.ss, 1)
            for q in range(CT):
                pe.wait_ge(s.rk, q + 1)
                for k in range(TT):
                    last = pe.matmul(PS[:, 4, k * RH + 2 * q:k * RH + 2 * q + 2], tmp[:, q % 2, k * P:(k + 1) * P],
                                     rk_col[:, q], start=True, stop=True)
                last.then_inc(s.bonus, 1)

        @block.scalar
        def _(act):
            for q in range(CT):
                act.wait_ge(s.z, q + 1)
                nc.scalar.activation(SG_[:, q], bank2(m, 2 * (q % 2)), ACT.Sigmoid, bias=m.col("w0", q)
                                     ).then_inc(s.sig, 1)
                nc.scalar.activation(A[:, q], bank2(m, 2 * (q % 2) + 1), ACT.Sigmoid, bias=m.col("a0", q)
                                     ).then_inc(s.sig, 1)
            for q in range(CT):
                if q >= 2:
                    act.wait_ge(s.ss, q - 1)
                nc.scalar.activation(sq[:, q % 2], K(q), ACT.Square, scale=m.col("k_k", q)).then_inc(s.sq, 1)
                if q >= 2:
                    act.wait_ge(s.kkn, q - 1)
                act.wait_ge(s.ss, q + 1)
                nc.scalar.activation(nrm[:, q % 2], bank2(m, q % 2), ACT.Sqrt).then_inc(s.root, 1)
            for q in range(CT):
                if q:
                    act.wait_ge(s.e3_used, q)
                act.wait_ge(s.dif, q + 1)
                nc.scalar.activation(ex[:, 0], tmp[:, q % 2], ACT.Exp, scale=-DECAY).then_inc(s.e1, 1)
                nc.scalar.activation(ex[:, 1], CS[:, q], ACT.Exp, scale=DECAY).then_inc(s.e2, 1)
                nc.scalar.activation(ex[:, 2], CS[:, q], ACT.Exp, scale=-DECAY).then_inc(s.e3, 1)

        @block.vector
        def _(dve):
            do = Chain(dve, s.chain)
            v = nc.vector
            do(v.tensor_scalar(om[:], m.col("k_a", 0, CT), -1.0, 1.0, ALU.mult, ALU.add))
            do(v.tensor_tensor(rk_col[:], m.col("r_k", 0, CT).unsqueeze(2).to_broadcast([P, CT, 2]),
                               m.const("headones")[:, 0:P:HD].unsqueeze(1).to_broadcast([P, CT, 2]), ALU.mult))
            for q in range(CT):
                v.tensor_scalar(Q(q), K(q), m.col("k_k", q), None, ALU.mult)
                dve.wait_ge(s.root, q + 1)
                n = nrm[:, q % 2]
                do(v.tensor_scalar(n, n, 1e-12, None, ALU.max))
                do(v.reciprocal(n, n))
                v.tensor_tensor(Q(q), Q(q), n, ALU.mult).then_inc(s.kkn, 1)
            for q in range(CT):
                if q >= 2:
                    dve.wait_ge(s.bonus, q - 1)
                do(v.tensor_scalar(tmp[:, q % 2], A[:, q], m.col("k_a", q), om[:, q:q + 1], ALU.mult, ALU.add))
                do(v.tensor_tensor(K(q), K(q), tmp[:, q % 2], ALU.mult))
                v.tensor_tensor(tmp[:, q % 2], R(q), K(q), ALU.mult).then_inc(s.rk, 1)
            for q in range(CT):
                d = tmp[:, q % 2]
                if q < 2:
                    dve.wait_ge(s.bonus, q + 3)
                do(v.tensor_copy(d, SG_[:, q]))
                do(v.tensor_tensor_scan(CS[:, q], m.const("chunk_row"), d, 0.0, ALU.mult, ALU.add))
                if q >= 2:
                    dve.wait_ge(s.e1, q - 1)
                v.tensor_tensor(d, CS[:, q], d, ALU.subtract).then_inc(s.dif, 1)
                do(v.scalar_tensor_tensor(out=A[:, q], in0=A[:, q], scalar=-1.0, in1=Q(q), op0=ALU.mult,
                                          op1=ALU.mult))
                dve.wait_ge(s.e1, q + 1)
                v.tensor_tensor(Q(q), Q(q), ex[:, 0], ALU.mult)
                dve.wait_ge(s.e2, q + 1)
                v.tensor_tensor(A[:, q], A[:, q], ex[:, 1], ALU.mult)
                v.tensor_tensor(K(q), K(q), ex[:, 1], ALU.mult)
                dve.wait_ge(s.e3, q + 1)
                v.tensor_copy(PC[:, q], ex[:, 2, CH - 1::CH])
                v.tensor_tensor(R(q), R(q), ex[:, 2], ALU.mult).then_inc(s.e3_used, 1)
            v.tensor_copy(bonus[:], PS[:, 4, 0:TT * RH])


def rwkv_recurrence(m, RKVQ, A, PC, LO, G2, bonus):
    nc, t, PS = m.nc, m.t, m.PS
    HB = 4
    with ExitStack() as ctx:
        tok = m.HT[:, 4:6].rearrange("p a (g i c) -> p (a g) i c", g=1, i=4)
        BR = m.HT[:, 6:8].rearrange("p g (h a c) -> p g h a c", h=HB, a=2)
        GR = alloc(m, ctx, "k_products", [P, 2, HB, 2, P])
        ND = alloc(m, ctx, "n_blocks", [P, 2, HB, P])
        NE = alloc(m, ctx, "n_rest", [P, 2, HB, P])
        P2 = alloc(m, ctx, "power2", [P, 2, 2, HB, P])
        P4 = alloc(m, ctx, "power4", [P, 2, 2, HB, P])
        IB = alloc(m, ctx, "block_inverse", [P, 2, HB, P])
        P8 = P2[:, :, 0]
        XR = P4[:, :, 0]
        FR = P4[:, :, 1]
        ZZ = ND
        WU = P2[:, :, 1]
        MT = alloc(m, ctx, "transition", [P, 2, 2, 2, HD])
        ZT = alloc(m, ctx, "read_out", [P, CT, P])
        S = alloc(m, ctx, "state", [P, CT, HD])
        Y = alloc(m, ctx, "y", [P, CW])
        Y2 = alloc(m, ctx, "y_tmp", [P, CW])
        VB = alloc(m, ctx, "v_bonus", [P, 2, CW])
        GT = alloc(m, ctx, "gate", [P, CW])
        LNX = alloc(m, ctx, "lnx_rows", [P, 2, CW])
        st = alloc(m, ctx, "stats", [P, 4, RH])
        s = phase(m, "rows_in pe order act dve pool eps chain achain init squared y_ready y_out mean_ready")
        block = ctx.enter_context(nc.Block())

        inner = [("TRa", "act"), ("TRb", "act"), ("PBa", "dve"), ("PBb", "dve"), ("N", "dve"), ("PGa", "dve"),
                 ("PGb", "dve"), ("SQ1a", "dve"), ("SQ1b", "act"), ("AP1", "dve"), ("SQ2a", "dve"),
                 ("SQ2b", "act"), ("AP2", "dve"), ("SQ3", "act"), ("GV", "act"), ("AP3", "dve"), ("FR", "act"),
                 ("Z", "act"), ("H1", "dve"), ("H2", "dve"), ("H3", "dve"), ("MT", "dve"), ("ZT", "dve")]
        plan = []
        for k in range(TT):
            for n, (name, eng) in enumerate(inner):
                plan += [(k, g, name, eng, 3 * g + n % 3) for g in range(2)]
                if name == "GV" and k:
                    plan.append((k - 1, 0, "YT", "act", 3 * 0 + (n + 1) % 3))
            plan += [(k, 0, "S0", "dve", 7), (k, 0, "S1", "dve", 7), (k, 0, "Y", "dve", 6), (k, 0, "GT", "act", 0)]
        plan.append((TT - 1, 0, "YT", "act", 1))
        count, filled, emptied, before, last_in = {"act": 0, "dve": 0}, {}, {}, {}, {}
        for n, (k, g, name, eng, bank) in enumerate(plan):
            count[eng] += 1
            key = (k, g, name)
            filled[key], emptied[key], before[key] = n + 1, (eng, count[eng]), last_in.get(bank)
            last_in[bank] = key
        banks = {(k, g, name): bank for k, g, name, _, bank in plan}

        def empty(eng, key):
            who, n = emptied[key]
            eng.wait_ge(s.act if who == "act" else s.dve, n)

        ftile = lambda g, h: 2 * g + h // 2
        hb = lambda h: HD * (h % 2)
        MIX_Y = RKVQ[:, 2 * CT:3 * CT]

        @block.sync
        def _(sp):
            sp.dma_start(LNX[:, 0], t.lnx_g.to_broadcast([P, CW])).then_inc(s.rows_in, 16)
            sp.dma_start(LNX[:, 1], t.lnx_b.to_broadcast([P, CW])).then_inc(s.rows_in, 16)

        @block.tensor
        def _(pe):
            pe.wait_ge(s.init, 1)
            fences = [0]

            def fence(ins):
                fences[0] += 1
                ins.then_inc(s.order, 1)
                pe.wait_ge(s.order, fences[0])

            for k, g, name, eng, bank in plan:
                key = (k, g, name)
                if before[key] is not None:
                    empty(pe, before[key])
                B = PS[:, bank, :]
                B4 = B.rearrange("p (h c) -> p h c", h=HB)
                cols = slice(k * P, (k + 1) * P)
                v, nb, kn, q = (tok[:, g, i] for i in range(4))
                if name in ("TRa", "TRb"):
                    if k and name == "TRa":
                        pe.wait_ge(s.pool, k * 2)
                    for i in range(2):
                        for f in range(2):
                            src = (RKVQ[:, 2 * CT + 2 * g + f], A[:, 2 * g + f], RKVQ[:, CT + 2 * g + f],
                                   RKVQ[:, 3 * CT + 2 * g + f])[2 * (name == "TRb") + i]
                            last = pe.transpose(B[:, (2 * i + f) * P:(2 * i + f + 1) * P], src[:, cols],
                                                m.const("ident"))
                elif name in ("PBa", "PBb", "PGa", "PGb"):
                    for i in range(2):
                        h = 2 * i + (name[2] == "b")
                        f, b = ftile(g, h), hb(h)
                        left = A[b:b + HD, f, cols] if name[1] == "B" else RKVQ[b:b + HD, CT + f, cols]
                        last = pe.matmul(B[:, i * 2 * P:(i + 1) * 2 * P].rearrange("p (a c) -> p a c", a=2), left,
                                         RKVQ[b:b + HD, f:f + 3 * CT + 1:3 * CT, cols], start=True, stop=True)
                elif name == "N":
                    for h in (0, 2, 1, 3):
                        if h == 1:
                            fence(last)
                        f, b = ftile(g, h), hb(h)
                        last = pe.matmul(B4[:, h], RKVQ[b:b + HD, 3 * CT + f, cols], A[b:b + HD, f, cols],
                                         start=True, stop=True)
                elif name in ("SQ1a", "SQ1b", "AP1", "SQ2a", "SQ2b", "AP2", "SQ3", "AP3", "FR", "Z", "H1", "H2",
                              "H3"):
                    needs = {"SQ1a": ("N", "PBb"), "SQ1b": (), "AP1": ("SQ1a",), "SQ2a": ("SQ1b",), "SQ2b": (),
                             "AP2": ("SQ2a", "AP1"), "SQ3": ("SQ2b",), "AP3": ("SQ3", "AP2"), "FR": ("AP3",),
                             "Z": ("GV",), "H1": ("FR", "Z"), "H2": ("H1",), "H3": ("H2",)}[name]
                    for need in needs:
                        empty(pe, (k, g, need))
                    for h in range(HB):
                        left, right = {
                            "SQ1a": (BR[:, g, h, 1], ND[:, g, h]), "SQ1b": (ND[:, g, h], BR[:, g, h, 1]),
                            "AP1": (P2[:, g, 0, h], IB[:, g, h]),
                            "SQ2a": (P2[:, g, 1, h], P2[:, g, 0, h]), "SQ2b": (P2[:, g, 0, h], P2[:, g, 1, h]),
                            "AP2": (P4[:, g, 0, h], IB[:, g, h]), "SQ3": (P4[:, g, 1, h], P4[:, g, 0, h]),
                            "AP3": (P8[:, g, h], IB[:, g, h]), "FR": (NE[:, g, h], IB[:, g, h]),
                            "Z": (IB[:, g, h], XR[:, g, h]), "H1": (FR[:, g, h], ZZ[:, g, h]),
                            "H2": (FR[:, g, h], WU[:, g, h]), "H3": (FR[:, g, h], WU[:, g, h]),
                        }[name]
                        last = pe.matmul(B4[:, h], left, right, start=True, stop=True)
                elif name == "GV":
                    empty(pe, (k, g, "PGb"))
                    empty(pe, (k, g, "TRa"))
                    for h in range(HB):
                        last = pe.matmul(B[:, h * HD:(h + 1) * HD], GR[:, g, h, 1], v[:, h * HD:(h + 1) * HD],
                                         start=True, stop=True)
                elif name == "MT":
                    empty(pe, (k, g, "H3"))
                    for c in range(2):
                        if c:
                            fence(last)
                        for h in range(HB):
                            rows, b = slice(c * CH, (c + 1) * CH), hb(h)
                            last = pe.matmul(B[b:b + HD, (2 * (h // 2) + c) * HD:(2 * (h // 2) + c + 1) * HD],
                                             WU[rows, g, h, 0:HD], nb[rows, h * HD:(h + 1) * HD],
                                             start=True, stop=True)
                elif name == "ZT":
                    for h in range(HB):
                        b = hb(h)
                        last = pe.matmul(B[b:b + HD, (h // 2) * P:(h // 2 + 1) * P], WU[:, g, h, 0:HD],
                                         BR[:, g, h, 0], start=True, stop=True)
                elif name in ("S0", "S1"):
                    c = int(name[1])
                    if c == 0:
                        for gg in range(2):
                            empty(pe, (k, gg, "MT"))
                            empty(pe, (k, gg, "ZT"))
                    else:
                        empty(pe, (k, 0, "S0"))
                    if c == 0:
                        if before[(k, 0, "Y")] is not None:
                            empty(pe, before[(k, 0, "Y")])
                    rows = slice(c * CH, (c + 1) * CH)
                    every = [(gg, h) for gg in range(2) for h in range(HB)]
                    out = lambda gg, h: B[hb(h):hb(h) + HD, ftile(gg, h) * HD:(ftile(gg, h) + 1) * HD]
                    y_at = lambda gg, h: slice((4 * gg + h) * HD, (4 * gg + h + 1) * HD)
                    for gg, h in every:
                        hs = slice(h * HD, (h + 1) * HD)
                        pe.matmul(out(gg, h), tok[rows, gg, 2, hs], tok[rows, gg, 0, hs],
                                  start=gg == 0 and h < 2, stop=False, skip_group_check=True)
                        last = pe.matmul(out(gg, h), tok[rows, gg, 1, hs], WU[rows, gg, h, HD:P], start=False,
                                         stop=False, skip_group_check=True)
                    if c == 0:
                        for gg, h in every:
                            pe.matmul(PS[:, 6, y_at(gg, h)], GR[:, gg, h, 0], tok[:, gg, 0, h * HD:(h + 1) * HD],
                                      start=gg == 0 and h == 0, stop=False, skip_group_check=True)
                            last = pe.matmul(PS[:, 6, y_at(gg, h)], BR[:, gg, h, 0], WU[:, gg, h, HD:P],
                                             start=False, stop=False, skip_group_check=True)
                    for odd in range(2):
                        fence(last)
                        for gg, h in every:
                            if h % 2 == odd:
                                f, b = ftile(gg, h), hb(h)
                                pe.matmul(out(gg, h), MT[b:b + HD, gg, h // 2, c], S[b:b + HD, f], start=False,
                                          stop=True, skip_group_check=True)
                                last = pe.matmul(PS[rows, 6, y_at(gg, h)], ZT[b:b + HD, f, rows], S[b:b + HD, f],
                                                 start=False, stop=True, skip_group_check=True)
                elif name == "Y":
                    pe.sem_inc(s.pe, 1)
                    continue
                elif name == "GT":
                    if k:
                        pe.wait_ge(s.y_ready, k)
                    pe.matmul(B, LO[:, 1, cols], G2[:, 0], start=True, stop=False)
                    last = pe.matmul(B, LO[0:GLORA - P, 2, cols], G2[0:GLORA - P, 1], start=False, stop=True)
                elif name == "YT":
                    pe.wait_ge(s.y_ready, k + 1)
                    for q_ in range(CT):
                        last = pe.transpose(B[:, q_ * P:(q_ + 1) * P], Y[:, q_ * P:(q_ + 1) * P], m.const("ident"))
                last.then_inc(s.pe, 1)
                if name == "S1":
                    pe.wait_ge(s.pe, filled[key])

        @block.scalar
        def _(act):
            for k, g, name, eng, bank in plan:
                if eng != "act":
                    continue
                key = (k, g, name)
                act.wait_ge(s.pe, filled[key])
                B = PS[:, bank, :]
                ins = None
                if name == "TRa":
                    ins = nc.scalar.copy(tok[:, g, 0:2].rearrange("p a c -> p (a c)"), B)
                elif name == "TRb":
                    ins = nc.scalar.copy(tok[:, g, 2:4].rearrange("p a c -> p (a c)"), B)
                elif name == "GV":
                    act.wait_ge(s.act, emptied[(k, g, "TRb")][1])
                    nc.scalar.copy(XR[:, g, :, 0:HD], tok[:, g, 3].rearrange("p (h c) -> p h c", h=HB))
                    ins = nc.scalar.copy(XR[:, g, :, HD:P], B[:, 0:HB * HD].rearrange("p (h c) -> p h c", h=HB))
                elif name == "GT":
                    ins = nc.scalar.copy(GT[:], B)
                elif name == "YT":
                    ins = nc.scalar.copy(MIX_Y[:, :, k * P:(k + 1) * P], B.rearrange("p (q c) -> p q c", q=CT))
                else:
                    out = {"SQ1b": P2[:, g, 1], "SQ2b": P4[:, g, 1], "SQ3": P8[:, g], "FR": FR[:, g],
                           "Z": ZZ[:, g]}[name]
                    ins = nc.scalar.copy(flat(out), B)
                ins.then_inc(s.act, 1)
                if name == "GT":
                    act.wait_ge(s.squared, 2 * k + 1)
                    nc.scalar.activation(Y2[:], Y[:], ACT.Square).then_inc(s.achain, 1)
                    act.wait_ge(s.squared, 2 * k + 2)
                    nc.scalar.activation(st[:, 1], st[:, 1], ACT.Sqrt, scale=1.0 / HD, bias=m.small[:, 0:1]
                                         ).then_inc(s.achain, 1)

        @block.gpsimd
        def _(pool):
            for k in range(TT):
                if k >= 2:
                    pool.wait_ge(s.y_ready, k - 1)
                for g in range(2):
                    empty(pool, (k, g, "TRa"))
                    nc.gpsimd.tensor_tensor(
                        VB[:, k % 2, g * 2 * P:(g + 1) * 2 * P].rearrange("p (h c) -> p h c", h=HB),
                        tok[:, g, 0].rearrange("p (h c) -> p h c", h=HB),
                        bonus[:, k * RH + g * HB:k * RH + (g + 1) * HB].unsqueeze(2).to_broadcast([P, HB, HD]),
                        ALU.mult).then_inc(s.pool, 1)

        @block.vector
        def _(dve):
            do = Chain(dve, s.chain)
            v = nc.vector
            v.memset(m.small[:, 0:1], LNX_EPS).then_inc(s.eps, 1)
            v.memset(S[:], 0.0).then_inc(s.init, 1)
            dve.wait_ge(s.rows_in, 32)
            heads = lambda ap: ap.rearrange("p (h c) -> p h c", h=RH)
            wide = lambda ap: ap.unsqueeze(2).to_broadcast([P, RH, HD])

            def mask(name, n=1):
                at = CONSTS[name][0]
                return m.consts[:, at:at + n * P].unsqueeze(1).to_broadcast([P, HB // n, n * P])

            for k, g, name, eng, bank in plan:
                if eng != "dve":
                    continue
                key = (k, g, name)
                dve.wait_ge(s.pe, filled[key])
                B = PS[:, bank, :]
                B4 = B.rearrange("p (h c) -> p h c", h=HB)
                B2 = B.rearrange("p (h c) -> p h c", h=2)
                cols = slice(k * P, (k + 1) * P)
                if name in ("PBa", "PBb"):
                    h = int(name[2] == "b")
                    ins = v.tensor_tensor(BR[:, g, h:HB:2].rearrange("p h a c -> p h (a c)"), B2,
                                          mask("mask_incl_up", 2), ALU.mult)
                elif name in ("PGa", "PGb"):
                    h = int(name[2] == "b")
                    ins = v.tensor_tensor(GR[:, g, h:HB:2].rearrange("p h a c -> p h (a c)"), B2,
                                          mask("mask_incl_up_2", 2), ALU.mult)
                elif name == "N":
                    dve.wait_ge(s.dve, emptied[(k, g, "PBb")][1])
                    v.tensor_tensor(IB[:, g], BR[:, g, :, 1], mask("ident"), ALU.add)
                    v.tensor_tensor(ND[:, g], B4, mask("mask_diag_low"), ALU.mult)
                    ins = v.tensor_tensor(NE[:, g], B4, mask("mask_off_low"), ALU.mult)
                elif name in ("SQ1a", "SQ2a"):
                    ins = v.tensor_copy(flat((P2 if name == "SQ1a" else P4)[:, g, 0]), B)
                elif name in ("AP1", "AP2", "AP3"):
                    ins = v.tensor_tensor(flat(IB[:, g]), flat(IB[:, g]), B, ALU.add)
                elif name in ("H1", "H2", "H3"):
                    ins = v.tensor_tensor(flat(WU[:, g]), flat(ZZ[:, g]), B, ALU.add)
                elif name == "MT":
                    at = CONSTS["ident_heads"][0]
                    ident = m.consts[:, at:at + HD].unsqueeze(1).to_broadcast([P, 4, HD])
                    ins = v.tensor_tensor(MT[:, g].rearrange("p f c j -> p (f c) j"),
                                          B[:, 0:4 * HD].rearrange("p (f j) -> p f j", f=4), ident, ALU.add)
                elif name == "ZT":
                    ins = v.tensor_tensor(ZT[:, 2 * g:2 * g + 2], B[:, 0:2 * P].rearrange("p (f c) -> p f c", f=2),
                                          RKVQ[:, 2 * g:2 * g + 2, cols], ALU.add)
                elif name in ("S0", "S1"):
                    c = int(name[1])
                    ins = v.tensor_tensor(S[:], B[:, 0:CT * HD].rearrange("p (f i) -> p f i", f=CT),
                                          PC[:, :, 2 * k + c].unsqueeze(2).to_broadcast([P, CT, HD]), ALU.mult)
                elif name == "Y":
                    if k:
                        dve.wait_ge(s.pe, filled[(k - 1, 0, "YT")])
                    do(v.tensor_reduce(st[:, 0], heads(B), AX, ALU.add))
                    do(v.tensor_scalar(st[:, 0], st[:, 0], 1.0 / HD, None, ALU.mult))
                    ins = v.tensor_tensor(heads(Y[:]), heads(B), wide(st[:, 0]), ALU.subtract)
                ins.then_inc(s.dve, 1)
                if name == "Y":
                    dve.wait_ge(s.dve, emptied[key][1])
                    v.sem_inc(s.squared, 1)
                    dve.wait_ge(s.achain, 2 * k + 1)
                    v.tensor_reduce(st[:, 1], heads(Y2[:]), AX, ALU.add).then_inc(s.squared, 1)
                    dve.wait_ge(s.achain, 2 * k + 2)
                    do(v.reciprocal(st[:, 2], st[:, 1]))
                    do(v.tensor_tensor(heads(Y[:]), heads(Y[:]), wide(st[:, 2]), ALU.mult))
                    do(v.tensor_tensor(Y[:], Y[:], LNX[:, 0], ALU.mult))
                    do(v.tensor_tensor(Y[:], Y[:], LNX[:, 1], ALU.add))
                    dve.wait_ge(s.pool, 2 * k + 2)
                    do(v.tensor_tensor(Y[:], Y[:], VB[:, k % 2], ALU.add))
                    empty(dve, (k, 0, "GT"))
                    v.tensor_tensor(Y[:], Y[:], GT[:], ALU.mult).then_inc(s.y_ready, 1)


def out_projection(m, tiles, w, GM, X):
    nc, t, PS = m.nc, m.t, m.PS
    with ExitStack() as ctx:
        W = alloc(m, ctx, "w_out", [P, KT, D])
        tmp = alloc(m, ctx, "scaled", [P, 2, D])
        junk = alloc(m, ctx, "junk", [P, D])
        s = phase(m, "w_in x_in eps prod rooted ps_free chain done")
        block = ctx.enter_context(nc.Block())
        ss, rstd, eps = m.small[:, 0:TT], m.small[:, TT:2 * TT], m.small[:, 2 * TT:2 * TT + 1]

        @block.sync
        def _(sp):
            sp.dma_start(W[:], w.rearrange("(k p) n -> p k n", p=P)).then_inc(s.w_in, 16)
            sp.dma_start(X[:], t.x.rearrange("(k p) n -> p k n", p=P)).then_inc(s.x_in, 16)

        @block.tensor
        def _(pe):
            pe.wait_ge(s.w_in, 16)
            for k in range(TT):
                if k >= 4:
                    pe.wait_ge(s.ps_free, k - 3)
                for half in range(2):
                    for q in range(KT):
                        last = pe.matmul(PS[:, 2 * (k % 4) + half, :], tiles[q][:, k * P:(k + 1) * P],
                                         W[:, q, half * NH:(half + 1) * NH], start=q == 0, stop=q == KT - 1)
                last.then_inc(s.prod, 1)

        @block.scalar
        def _(act):
            act.wait_ge(s.eps, 1)
            for k in range(TT):
                act.wait_ge(s.prod, k + 1)
                nc.scalar.activation(junk[:], bank2(m, k % 4), ACT.Square, accum_out=ss[:, k:k + 1]
                                     ).then_inc(s.chain, 1)
                act.wait_ge(s.chain, k + 1)
                nc.scalar.activation(rstd[:, k:k + 1], ss[:, k:k + 1], ACT.Sqrt, scale=1.0 / D, bias=eps
                                     ).then_inc(s.rooted, 1)

        @block.vector
        def _(dve):
            v = nc.vector
            v.memset(eps, RMS_EPS).then_inc(s.eps, 1)
            dve.wait_ge(s.x_in, 16)
            for k in range(TT):
                dve.wait_ge(s.rooted, k + 1)
                v.reciprocal(rstd[:, k:k + 1], rstd[:, k:k + 1]).then_inc(s.done, 1)
                dve.wait_ge(s.done, 2 * k + 1)
                v.scalar_tensor_tensor(out=tmp[:, k % 2], in0=bank2(m, k % 4), scalar=rstd[:, k:k + 1],
                                       in1=GM, op0=ALU.mult, op1=ALU.mult).then_inc(s.ps_free, 1)
                dve.wait_ge(s.ps_free, k + 1)
                v.tensor_tensor(X[:, k], X[:, k], tmp[:, k % 2], ALU.add).then_inc(s.done, 1)


def up_projection(m, MID):
    nc, t, PS = m.nc, m.t, m.PS
    with ExitStack() as ctx:
        W = alloc(m, ctx, "up_slots", [P, 2, KT, 2 * P])
        Z = alloc(m, ctx, "z", [P, 2, 2, T])
        s = phase(m, "w_in0 w_in1 slot_free tile_done ps_free tap2 chain silu mid")
        w_in = [s.w_in0, s.w_in1]
        block = ctx.enter_context(nc.Block())
        col = lambda name, at: m.cols[:, bass.ds(at + COLS[name][0], 1)]

        @block.sync
        def _(sp):
            with sp.Fori(0, FT // 2) as i:
                at = [[sp.snap(i * 2 * P + j * P + c * D_FF) for c in range(2)] for j in range(2)]
                for j in range(2):
                    sp.wait_ge(s.slot_free, i * 2 + j + 1)
                    for c in range(2):
                        sp.dma_start(W[:, j, :, c * P:(c + 1) * P],
                                     t.w_up[:, bass.ds(at[j][c], P)].rearrange("(k p) n -> p k n", p=P)
                                     ).then_inc(w_in[j], 16)

        @block.tensor
        def _(pe):
            pe.sem_inc(s.slot_free, 2)
            with pe.Fori(0, FT // 2) as i:
                for j in range(2):
                    pe.wait_ge(w_in[j], (i + 1) * 32)
                    for c in range(2):
                        pe.wait_ge(s.ps_free, i * 4 + 2 * j + c + 1)
                        tile_product(m, pe, W, j, c, 2 * j + c).then_inc(s.tile_done, 1)
                    pe.wait_ge(s.tile_done, i * 4 + 2 * j + 2)
                    pe.sem_inc(s.slot_free, 1)

        @block.scalar
        def _(act):
            with act.Fori(0, FT // 2) as i:
                for j in range(2):
                    act.wait_ge(s.mid, i * 2 + j + 1)
                    for c in range(2):
                        ch = i * 2 + (j + c * FT)
                        act.wait_ge(s.tile_done, i * 4 + 2 * j + c + 1)
                        nc.scalar.activation(Z[:, j, c], bank2(m, 2 * j + c), ACT.Identity,
                                             scale=col("ffn_w", i * 6 + (j + c * FT) * 3 + 2), bias=col("ffn_b", ch)
                                             ).then_inc(s.tap2, 1)
                    act.wait_ge(s.ps_free, i * 4 + 2 * j + 1 + 4)
                    nc.scalar.activation(Z[:, j, 0], Z[:, j, 0], ACT.Silu).then_inc(s.silu, 1)

        @block.vector
        def _(dve):
            v = nc.vector
            dve.sem_inc(s.ps_free, 4)
            dve.sem_inc(s.mid, 2)
            with dve.Fori(0, FT // 2) as i:
                for j in range(2):
                    for c in range(2):
                        n = 2 * j + c
                        dve.wait_ge(s.tap2, i * 4 + n + 1)
                        for tap in (1, 2):
                            z = Z[:, j, c, tap:T]
                            ins = v.scalar_tensor_tensor(out=z, in0=bank2(m, n)[:, 0:T - tap],
                                                         scalar=col("ffn_w", i * 6 + (j + c * FT) * 3 + 2 - tap),
                                                         in1=z, op0=ALU.mult, op1=ALU.add)
                            if tap == 1:
                                ins.then_inc(s.chain, 1)
                                dve.wait_ge(s.chain, i * 4 + n + 1)
                        ins.then_inc(s.ps_free, 1)
                    dve.wait_ge(s.silu, i * 2 + j + 1)
                    dve.wait_ge(s.ps_free, i * 4 + 2 * j + 2 + 4)
                    v.tensor_tensor(MID[:, bass.ds(i * 2 + j, 1), :].rearrange("p a b -> p (a b)"), Z[:, j, 0],
                                    Z[:, j, 1], ALU.mult).then_inc(s.mid, 1)


def down_projection(m, MID, GM, X, dst):
    nc, t, PS = m.nc, m.t, m.PS
    QW, KC = D // 4, FT // 2
    F = m.HT
    with ExitStack() as ctx:
        W = alloc(m, ctx, "down_slots", [P, 2, KC, QW])
        s = phase(m, "w_in0 w_in1 slot_free prod ps_free moved eps sq rooted chain out stored")
        w_in = [s.w_in0, s.w_in1]
        block = ctx.enter_context(nc.Block())
        ss, rstd, eps = m.small[:, 0:TT], m.small[:, TT:2 * TT], m.small[:, 2 * TT:2 * TT + 1]

        @block.sync
        def _(sp):
            with sp.Fori(0, 4) as i:
                at = sp.snap(i * QW)
                for c in range(2):
                    sp.wait_ge(s.slot_free, i * 2 + c + 1)
                    sp.dma_start(W[:, c], t.w_down[c * KC * P:(c + 1) * KC * P, bass.ds(at, QW)]
                                 .rearrange("(k p) n -> p k n", p=P)).then_inc(w_in[c], 16)
            for k in range(TT):
                sp.wait_ge(s.out, TT + k + 1)
                sp.dma_start(dst[k * P:(k + 1) * P], X[:, k]).then_inc(s.stored, 16)
            sp.wait_ge(s.stored, 16 * TT)

        @block.tensor
        def _(pe):
            pe.sem_inc(s.slot_free, 2)
            with pe.Fori(0, 2) as i:
                for r in range(2):
                    for c in range(2):
                        pe.wait_ge(w_in[c], (i * 2 + r + 1) * 16)
                        for k in range(TT):
                            if c == 0 and k % 2 == 0:
                                pe.wait_ge(s.ps_free, i * 8 + 4 * r + k // 2 + 1)
                            for q in range(KC):
                                last = pe.matmul(PS[:, 4 * r + k // 2, (k % 2) * QW:(k % 2 + 1) * QW],
                                                 MID[:, c * KC + q, k * P:(k + 1) * P], W[:, c, q],
                                                 start=c == 0 and q == 0 and k % 2 == 0,
                                                 stop=c == 1 and q == KC - 1, skip_group_check=True)
                            if c == 1 and k % 2 == 1:
                                last.then_inc(s.prod, 1)
                            elif c == 0 and k == TT - 1:
                                last.then_inc(s.slot_free, 1)
                        if c == 1:
                            pe.wait_ge(s.prod, i * 8 + 4 * r + 4)
                            pe.sem_inc(s.slot_free, 1)

        @block.scalar
        def _(act):
            act.sem_inc(s.ps_free, 8)
            with act.Fori(0, 2) as i:
                for r in range(2):
                    for b in range(4):
                        act.wait_ge(s.prod, i * 8 + 4 * r + b + 1)
                        nc.scalar.copy(F[:, 2 * b:2 * b + 2, bass.ds(i * 2 * QW + r * QW, QW)],
                                       PS[:, 4 * r + b, :].rearrange("p (k n) -> p k n", k=2)).then_inc(s.ps_free, 1)
            act.wait_ge(s.ps_free, 24)
            act.wait_ge(s.eps, 1)
            for k in range(TT):
                if k:
                    act.wait_ge(s.sq, k)
                nc.scalar.activation(flat(W[:, 0, 0:4]), F[:, k], ACT.Square, accum_out=ss[:, k:k + 1]
                                     ).then_inc(s.sq, 1)
            act.wait_ge(s.sq, TT)
            nc.scalar.activation(rstd, ss, ACT.Sqrt, scale=1.0 / D, bias=eps).then_inc(s.rooted, 1)

        @block.vector
        def _(dve):
            do = Chain(dve, s.chain)
            v = nc.vector
            v.memset(eps, RMS_EPS).then_inc(s.eps, 1)
            dve.wait_ge(s.rooted, 1)
            do(v.reciprocal(rstd, rstd))
            for k in range(TT):
                v.scalar_tensor_tensor(out=F[:, k], in0=F[:, k], scalar=rstd[:, k:k + 1], in1=GM,
                                       op0=ALU.mult, op1=ALU.mult).then_inc(s.out, 1)
            dve.wait_ge(s.out, TT)
            for k in range(TT):
                v.tensor_tensor(X[:, k], X[:, k], F[:, k], ALU.add).then_inc(s.out, 1)




def turned_in(m, src, HH, HL):
    nc, PS = m.nc, m.PS
    X = m.HT
    s = phase(m, "in0 in1 in2 in3 in4 in5 in6 in7 turned high low")
    x_in = [s.in0, s.in1, s.in2, s.in3, s.in4, s.in5, s.in6, s.in7]
    at = lambda n: (slice(None), n % KT, slice(n // KT * NH, (n // KT + 1) * NH))
    with nc.Block() as block:
        @block.sync
        def _(sp):
            for k in range(TT):
                sp.dma_start(X[:, k], src[k * P:(k + 1) * P]).then_inc(x_in[k], 16)

        @block.tensor
        def _(pe):
            for n in range(2 * KT):
                half, k = n // KT, n % KT
                if k == 0:
                    for j in range(4):
                        pe.wait_ge(x_in[4 * half + j], 16)
                if half:
                    pe.wait_ge(s.low, k + 1)
                for j in range(4):
                    last = pe.transpose(PS[:, k, j * P:(j + 1) * P], X[:, 4 * half + j, k * P:(k + 1) * P],
                                        m.const("ident"))
                last.then_inc(s.turned, 1)

        @block.scalar
        def _(act):
            for n in range(2 * KT):
                act.wait_ge(s.turned, n + 1)
                nc.scalar.copy(HH[at(n)], PS[:, n % KT, :]).then_inc(s.high, 1)

        @block.vector
        def _(dve):
            for n in range(2 * KT):
                dve.wait_ge(s.high, n + 1)
                nc.vector.tensor_tensor(HL[at(n)], PS[:, n % KT, :], HH[at(n)], ALU.subtract).then_inc(s.low, 1)


def projections_and_attention(m, layer, w, sinks, HH, HL, DT, attn_d, xbc_d, gate_d):
    nc, t, PS = m.nc, m.t, m.PS
    G4 = 4
    with ExitStack() as ctx:
        KH = alloc(m, ctx, "k", [P, 4, T])
        V = alloc(m, ctx, "v", [P, TT, KVW])
        RAW = alloc(m, ctx, "w_raw", [P, 3, KT, P])
        WH = alloc(m, ctx, "w_high", [P, 2, KT, P], F32R)
        WL = alloc(m, ctx, "w_low", [P, 2, KT, P], F32R)
        ST = alloc(m, ctx, "staged", [P, 2, T])
        BIAS = alloc(m, ctx, "alibi", [P, 2, G4, 2 * P])
        SC = alloc(m, ctx, "scores", [P, 2, G4, 2 * P])
        PT = alloc(m, ctx, "probs_turned", [P, 2, 2, G4 * P])
        SK = alloc(m, ctx, "sinks", [P, QH])
        MX, NM, DN, ES, RD = (alloc(m, ctx, n, [P, 2, G4]) for n in (
            "maxima", "minus_max", "sums", "sink_terms", "inverse_sums"))
        QT = m.HT[:, 0:4]
        AT = m.HT[:, 4:8]
        s = phase(m, "raw0 raw1 raw2 split wchain tile act_free dve_free tap silu stage0 stage1 bias0 bias1 sink_in "
                     "swapped scored biased neg exps rden chain probs turned moved0 moved1 outed gated "
                     "stored small small_free")
        raw_in, stage, bias_in = [s.raw0, s.raw1, s.raw2], [s.stage0, s.stage1], [s.bias0, s.bias1]
        block = ctx.enter_context(nc.Block())

        units = [(g, nb) for g in range(KVH) for nb in range(TT)]
        N = len(units)
        lo = lambda nb: P if nb == 0 else 0

        first = [("k", 0), ("k", 1), ("v", 0), ("v", 1), ("dt", 0), ("q", 0), ("q", 1), ("za", 0), ("za", 1)]
        rest = [("xbc", i) for i in range(XT)] + [("zs", i) for i in range(KT)]
        beside = []
        for g in range(KVH):
            ahead = [] if g == KVH - 1 else [("q", 2 * g + 2), ("q", 2 * g + 3), ("za", 2 * g + 2), ("za", 2 * g + 3)]
            beside += ahead + rest[:TT - len(ahead)]
            rest = rest[TT - len(ahead):]
        jobs = first + beside
        F = len(first)
        where = {job: n for n, job in enumerate(jobs)}
        column = {"q": O_Q, "k": O_K, "v": O_V, "za": O_ZA, "zs": O_ZS, "xbc": O_XBC, "dt": IN_W - P}
        staged = [job for job in jobs if job[0] in ("v", "dt", "xbc", "zs")]
        slot = {job: j % 2 for j, job in enumerate(staged)}
        before = {job: sum(o[0] in ("xbc", "zs") for o in staged[:j] if slot[o] == slot[job])
                  for j, job in enumerate(staged)}
        dve_jobs = [job for job in jobs if job[0] == "xbc"]
        act_jobs = [job for job in jobs if job[0] != "xbc"]

        def free(eng, n):
            if jobs[n][0] == "xbc":
                eng.wait_ge(s.dve_free, dve_jobs.index(jobs[n]) + 1)
            else:
                eng.wait_ge(s.act_free, act_jobs.index(jobs[n]) + 1)

        pair = lambda n: 2 + n % 2

        @block.sync
        def _(sp):
            sp.dma_start(SK[:], sinks.to_broadcast([P, QH])).then_inc(s.sink_in, 16)
            for n, (kind, i) in enumerate(jobs):
                if n >= 3:
                    sp.wait_ge(s.split, n - 2)
                at = column[kind] + i * P
                sp.dma_start(RAW[:, n % 3], w[:, at:at + P].rearrange("(k p) n -> p k n", p=P)
                             ).then_inc(raw_in[n % 3], 16)
                if n == 4:
                    free(sp, where["k", 1])
                    sp.dma_start(KH[0:HD, 2:4], KH[HD:P, 0:2]).then_inc(s.swapped, 16)
                    sp.dma_start(KH[HD:P, 2:4], KH[0:HD, 0:2]).then_inc(s.swapped, 16)
                if n >= 5 and (n - 5) % TT == 0 and (n - 5) // TT < KVH:
                    g = (n - 5) // TT
                    if g >= 2:
                        sp.wait_ge(s.biased, TT * (g - 1))
                    sp.dma_start(BIAS[:, g % 2], t.alibi[:, G4 * g:G4 * g + G4]).then_inc(bias_in[g % 2], 16)

        @block.tensor
        def _(pe):
            def half_tile(n, half):
                if half == 0:
                    pe.wait_ge(s.split, n + 1)
                    if n >= 2:
                        free(pe, n - 2)
                bank = 2 * pair(n) + half
                cols = slice(half * NH, (half + 1) * NH)
                for k in range(KT):
                    for a, b in ((WH, HH), (WH, HL), (WL, HH)):
                        last = pe.matmul(PS[:, bank, :], a[:, n % 2, k], b[:, k, cols],
                                         start=k == 0 and a is WH and b is HH, stop=k == KT - 1 and a is WL)
                if half:
                    last.then_inc(s.tile, 1)

            def scores(u):
                g, nb = units[u]
                if u >= 2:
                    pe.wait_ge(s.gated, u - 1)
                if nb == 0:
                    free(pe, where["q", 2 * g + 1])
                for i in range(G4):
                    at, b = (i // 2) * 2 * P, HD * (i % 2)
                    last = pe.matmul(PS[:, 2 * (u % 2) + i % 2, at + lo(nb):at + 2 * P],
                                     QT[b:b + HD, 2 * (g % 2) + i // 2, nb * P:(nb + 1) * P],
                                     KH[b:b + HD, g // 2 + (2 if i % 2 != g % 2 else 0),
                                        (nb - 1) * P + lo(nb):(nb + 1) * P], start=True, stop=True)
                last.then_inc(s.scored, 1)

            def turn(u):
                g, nb = units[u]
                pe.wait_ge(s.probs, u + 1)
                for a in range(2):
                    if a == 0 and nb == 0:
                        pe.sem_inc(s.turned, 1)
                        continue
                    for i in range(G4):
                        at = ((i % 2) * 2 + i // 2) * P
                        last = pe.transpose(PS[:, 2 * (u % 2) + a, at:at + P], SC[:, u % 2, i, a * P:(a + 1) * P],
                                            m.const("ident"))
                    last.then_inc(s.turned, 1)

            def out(u):
                g, nb = units[u]
                pe.wait_ge(s.moved0, u + 1)
                pe.wait_ge(s.moved1, u + 1)
                for odd in range(2):
                    for a in range(1 if nb == 0 else 0, 2):
                        last = pe.matmul(PS[odd * HD:(odd + 1) * HD, 2 * (u % 2), 0:2 * P],
                                         V[:, nb - 1 + a, g * HD:(g + 1) * HD],
                                         PT[:, u % 2, a, odd * 2 * P:(odd + 1) * 2 * P],
                                         start=a == 0 or nb == 0, stop=a == 1)
                last.then_inc(s.outed, 1)

            for n, job in enumerate(first):
                half_tile(n, 0)
                half_tile(n, 1)
                if job[0] == "dt":
                    free(pe, where["v", 1])
                    for l in range(TT):
                        for c in range(2):
                            last = pe.transpose(PS[:, l // 2, (l % 2) * KVW + c * P:(l % 2) * KVW + (c + 1) * P],
                                                ST[:, slot["v", c], l * P:(l + 1) * P], m.const("ident"))
                    last.then_inc(s.small, 1)
                if job == ("q", 0):
                    free(pe, where["dt", 0])
                    pe.wait_ge(s.small_free, 1)
                    for l in range(TT):
                        last = pe.transpose(PS[:, l // 4, (l % 4) * P:(l % 4 + 1) * P],
                                            ST[:, slot["dt", 0], l * P:(l + 1) * P], m.const("ident"))
                    last.then_inc(s.small, 1)
            pe.wait_ge(s.small_free, 2)
            pe.wait_ge(s.swapped, 32)
            scores(0)
            for u in range(N):
                if u:
                    turn(u - 1)
                half_tile(F + u, 0)
                if u:
                    out(u - 1)
                half_tile(F + u, 1)
                if u + 1 < N:
                    scores(u + 1)
            turn(N - 1)
            out(N - 1)

        @block.gpsimd
        def _(pool):
            def split(n):
                pool.wait_ge(raw_in[n % 3], 16 * (n // 3 + 1))
                if n >= 2:
                    pool.wait_ge(s.tile, n - 1)
                nc.gpsimd.tensor_copy(WH[:, n % 2], RAW[:, n % 3]).then_inc(s.wchain, 1)
                pool.wait_ge(s.wchain, n + 1)
                nc.gpsimd.tensor_tensor(WL[:, n % 2], RAW[:, n % 3], WH[:, n % 2], ALU.subtract).then_inc(s.split, 1)

            for n in range(F + 1):
                split(n)
            for u in range(N):
                g, nb = units[u]
                if F + u + 1 < len(jobs):
                    split(F + u + 1)
                pool.wait_ge(s.rden, u + 1)
                p = SC[:, u % 2, :, lo(nb):2 * P]
                nc.gpsimd.tensor_tensor(p, p, RD[:, u % 2].unsqueeze(2).to_broadcast([P, G4, 2 * P - lo(nb)]),
                                        ALU.mult).then_inc(s.probs, 1)

        @block.scalar
        def _(act):
            def store(job):
                dst = (xbc_d if job[0] == "xbc" else gate_d)[job[1]]
                act.dma_start(dst, ST[:, slot[job]]).then_inc(stage[slot[job]], 16)

            def store_attention(g):
                act.wait_ge(s.gated, TT * (g + 1))
                act.dma_start(attn_d[2 * g:2 * g + 2].rearrange("k p t -> p k t"),
                              AT[:, 2 * (g % 2):2 * (g % 2) + 2]).then_inc(s.stored, 16)

            silus = [0]

            def evacuate(n):
                kind, i = jobs[n]
                act.wait_ge(s.tile, n + 1)
                src = bank2(m, pair(n))
                if kind in ("v", "dt", "xbc", "zs"):
                    st = ST[:, slot[kind, i]]
                    if before[kind, i]:
                        act.wait_ge(stage[slot[kind, i]], 16 * before[kind, i])
                    elif kind in ("dt", "xbc", "zs"):
                        act.wait_ge(s.small, 1 if kind == "dt" else 2)
                if kind == "k":
                    nc.scalar.copy(KH[:, i], src).then_inc(s.act_free, 1)
                elif kind == "q":
                    g = i // 2
                    if g >= 2:
                        act.wait_ge(s.scored, TT * (g - 1))
                    nc.scalar.copy(QT[:, i % 4], src).then_inc(s.act_free, 1)
                elif kind == "za":
                    g = i // 2
                    if g >= 2:
                        act.wait_ge(s.stored, 16 * (g - 1))
                    nc.scalar.activation(AT[:, i % 4], src, ACT.Silu).then_inc(s.act_free, 1)
                elif kind in ("v", "dt"):
                    nc.scalar.copy(st, src).then_inc(s.act_free, 1)
                elif kind == "zs":
                    nc.scalar.activation(st, src, ACT.Silu).then_inc(s.act_free, 1)
                    act.wait_ge(s.act_free, act_jobs.index((kind, i)) + 1)
                    store((kind, i))
                else:
                    ch = layer * XT + i
                    nc.scalar.activation(st, src, ACT.Identity, bias=m.col("conv_b_2", ch),
                                         scale=m.col("conv_w_2", ch * CK2 + CK2 - 1)).then_inc(s.tap, 1)

            def finish(n):
                job = jobs[n]
                if job[0] == "xbc":
                    act.wait_ge(s.dve_free, dve_jobs.index(job) + 1)
                    nc.scalar.activation(ST[:, slot[job]], ST[:, slot[job]], ACT.Silu).then_inc(s.silu, 1)
                    silus[0] += 1
                    act.wait_ge(s.silu, silus[0])
                    store(job)

            def exps(u):
                g, nb = units[u]
                act.wait_ge(s.neg, u + 1)
                nc.scalar.activation(ES[:, u % 2], ES[:, u % 2], ACT.Exp).then_inc(s.exps, 1)
                for i in range(G4):
                    p = SC[:, u % 2, i, lo(nb):2 * P]
                    nc.scalar.activation(p, p, ACT.Exp, bias=NM[:, u % 2, i:i + 1],
                                         accum_out=DN[:, u % 2, i:i + 1]).then_inc(s.exps, 1)

            def move0(u):
                if units[u][1] == 0:
                    act.sem_inc(s.moved0, 1)
                    return
                act.wait_ge(s.turned, 2 * u + 1)
                if u >= 2:
                    act.wait_ge(s.outed, u - 1)
                nc.scalar.copy(PT[:, u % 2, 0], PS[:, 2 * (u % 2), :]).then_inc(s.moved0, 1)

            for n in range(F - 1):
                evacuate(n)
                if jobs[n] == ("dt", 0):
                    act.wait_ge(s.small, 1)
                    nc.scalar.copy(V[:], PS[:, 0:4, :].rearrange("p a b -> p (a b)").rearrange(
                        "p (l c) -> p l c", l=TT)).then_inc(s.small_free, 1)
                if jobs[n] == ("q", 0):
                    act.wait_ge(s.small, 2)
                    nc.scalar.copy(DT[:].rearrange("p (l h) -> p l h", l=TT), PS[:, 0:2, :].rearrange(
                        "p a (b c) -> p (a b) c", b=4)[:, :, P - SH:P]).then_inc(s.small_free, 1)
            for u in range(N + 1):
                if u:
                    move0(u - 1)
                if u < N:
                    exps(u)
                evacuate(F + u - 1)
                if u:
                    finish(F + u - 2)
                if u > 1 and u % TT == 1:
                    store_attention(u // TT - 1)
            store_attention(KVH - 1)
            act.wait_ge(s.stored, 16 * KVH)
            act.wait_ge(stage[0], 16 * sum(slot[j] == 0 for j in staged if j[0] in ("xbc", "zs")))
            act.wait_ge(stage[1], 16 * sum(slot[j] == 1 for j in staged if j[0] in ("xbc", "zs")))

        @block.vector
        def _(dve):
            do = Chain(dve, s.chain)
            v = nc.vector

            def bias(u):
                g, nb = units[u]
                dve.wait_ge(s.scored, u + 1)
                if nb == 0:
                    dve.wait_ge(bias_in[g % 2], 16 * (g // 2 + 1))
                if u >= 2:
                    dve.wait_ge(s.turned, 2 * (u - 1))
                for i in range(G4):
                    h, at = G4 * g + i, (i // 2) * 2 * P
                    ins = v.tensor_tensor_reduce(
                        SC[:, u % 2, i, lo(nb):2 * P], PS[:, 2 * (u % 2) + i % 2, at + lo(nb):at + 2 * P],
                        BIAS[:, g % 2, i, lo(nb):2 * P], HD ** -0.5, SK[:, h:h + 1], ALU.add, ALU.max,
                        MX[:, u % 2, i:i + 1])
                ins.then_inc(s.biased, 1)
                dve.wait_ge(s.biased, u + 1)
                do(v.tensor_tensor(ES[:, u % 2], SK[:, G4 * g:G4 * g + G4], MX[:, u % 2], ALU.subtract))
                v.tensor_scalar(NM[:, u % 2], MX[:, u % 2], -1.0, None, ALU.mult).then_inc(s.neg, 1)

            def move1(u):
                dve.wait_ge(s.turned, 2 * u + 2)
                if u >= 2:
                    dve.wait_ge(s.outed, u - 1)
                v.tensor_copy(PT[:, u % 2, 1], PS[:, 2 * (u % 2) + 1, :]).then_inc(s.moved1, 1)

            def inverse(u):
                dve.wait_ge(s.exps, 5 * u + 5)
                do(v.tensor_tensor(DN[:, u % 2], DN[:, u % 2], ES[:, u % 2], ALU.add))
                v.reciprocal(RD[:, u % 2], DN[:, u % 2]).then_inc(s.rden, 1)

            def taps(n):
                kind, i = jobs[n]
                if kind != "xbc":
                    return
                dve.wait_ge(s.tap, dve_jobs.index((kind, i)) + 1)
                ch, st = layer * XT + i, ST[:, slot[kind, i]]
                for tap in range(1, CK2):
                    ins = v.scalar_tensor_tensor(out=st[:, tap:T], in0=bank2(m, pair(n))[:, 0:T - tap],
                                                 scalar=m.col("conv_w_2", ch * CK2 + CK2 - 1 - tap),
                                                 in1=st[:, tap:T], op0=ALU.mult, op1=ALU.add)
                    if tap < CK2 - 1:
                        do(ins)
                ins.then_inc(s.dve_free, 1)

            def gate(u):
                g, nb = units[u]
                dve.wait_ge(s.outed, u + 1)
                if nb == 0:
                    free(dve, where["za", 2 * g + 1])
                a = AT[:, 2 * (g % 2):2 * (g % 2) + 2, nb * P:(nb + 1) * P]
                v.tensor_tensor(a, PS[:, 2 * (u % 2), 0:2 * P].rearrange("p (i q) -> p i q", i=2), a, ALU.mult
                                ).then_inc(s.gated, 1)

            dve.wait_ge(s.sink_in, 16)
            for u in range(N + 1):
                if u < N:
                    bias(u)
                if u:
                    move1(u - 1)
                if u < N:
                    inverse(u)
                if u:
                    taps(F + u - 1)
                    gate(u - 1)


def step_sizes(m, dt_bias, a_log, DT, NA, EI, DE, CD, DA):
    nc, t, PS = m.nc, m.t, m.PS
    C = TT * SH
    with ExitStack() as ctx:
        rows = alloc(m, ctx, "dt_rows", [P, 2, SH])
        tmp = alloc(m, ctx, "dt_tmp", [P, 5, C])
        s = phase(m, "par_in ab e chain sums acs last ex")
        block = ctx.enter_context(nc.Block())
        ax, e, sv, z, poly = (tmp[:, i] for i in range(5))
        by_head = lambda ap: ap.rearrange("p (c h) -> p c h", h=SH)

        @block.sync
        def _(sp):
            sp.dma_start(rows[:, 0], dt_bias.to_broadcast([P, SH])).then_inc(s.par_in, 16)
            sp.dma_start(rows[:, 1], a_log.to_broadcast([P, SH])).then_inc(s.par_in, 16)

        @block.scalar
        def _(act):
            act.wait_ge(s.par_in, 32)
            nc.scalar.activation(rows[:, 1], rows[:, 1], ACT.Exp).then_inc(s.e, 1)
            act.wait_ge(s.ab, 1)
            nc.scalar.activation(ax, DT[:], ACT.Abs).then_inc(s.e, 1)
            act.wait_ge(s.e, 2)
            nc.scalar.activation(e, ax, ACT.Exp, scale=-1.0).then_inc(s.e, 1)
            act.wait_ge(s.sums, 1)
            nc.scalar.activation(EI[:], PS[:, 0, 0:C], ACT.Exp).then_inc(s.ex, 1)
            nc.scalar.mul(NA[:], PS[:, 0, 0:C], -1.0).then_inc(s.acs, 1)
            act.wait_ge(s.last, 1)
            nc.scalar.activation(CD[:], PS[:, 1, 0:C], ACT.Exp).then_inc(s.ex, 1)
            act.wait_ge(s.ex, 3)
            nc.scalar.activation(DE[:], DE[:], ACT.Exp)

        @block.vector
        def _(dve):
            v = nc.vector
            do = Chain(dve, s.chain)
            dve.wait_ge(s.par_in, 32)
            v.tensor_tensor(by_head(DT[:]), by_head(DT[:]), rows[:, 0].unsqueeze(1).to_broadcast([P, TT, SH]),
                            ALU.add).then_inc(s.ab, 1)
            dve.wait_ge(s.e, 3)
            do(v.tensor_scalar(sv, e, 2.0, None, ALU.add))
            do(v.reciprocal(sv, sv))
            do(v.tensor_tensor(sv, sv, e, ALU.mult))
            do(v.tensor_tensor(z, sv, sv, ALU.mult))
            do(v.tensor_scalar(poly, z, 2.0 / 17, 2.0 / 15, ALU.mult, ALU.add))
            for n in range(13, 0, -2):
                do(v.tensor_tensor(poly, poly, z, ALU.mult))
                do(v.tensor_scalar(poly, poly, 2.0 / n, None, ALU.add))
            do(v.tensor_tensor(poly, poly, sv, ALU.mult))
            do(v.scalar_tensor_tensor(out=DT[:], in0=DT[:], scalar=0.0, in1=poly, op0=ALU.max, op1=ALU.add))
            do(v.scalar_tensor_tensor(out=by_head(DA[:]), in0=by_head(DT[:]), scalar=-1.0,
                                      in1=rows[:, 1].unsqueeze(1).to_broadcast([P, TT, SH]), op0=ALU.mult,
                                      op1=ALU.mult))
            dve.wait_ge(s.acs, 1)
            dve.wait_ge(s.last, 1)
            dve.wait_ge(s.ex, 2)
            v.tensor_tensor(DE[:], PS[:, 1, 0:C], NA[:], ALU.add).then_inc(s.ex, 1)

        @block.tensor
        def _(pe):
            pe.wait_ge(s.chain, 5 + 2 * 7 + 3)
            pe.matmul(PS[:, 0, 0:C], m.const("tri"), DA[:], start=True, stop=True).then_inc(s.sums, 1)
            pe.wait_ge(s.acs, 1)
            pe.matmul(PS[:, 1, 0:C], m.const("minus_last"), NA[:], start=True, stop=True).then_inc(s.last, 1)


def state_space(m, d_skip, xbc_d, gate_d, DT, DA, NA, EI, DE, CD):
    nc, t, PS, HT = m.nc, m.t, m.PS, m.HT
    BF16 = mybir.dt.bfloat16
    GW = DI // SG
    with ExitStack() as ctx:
        XB = alloc(m, ctx, "xbc", [P, XT, T])
        ZS = alloc(m, ctx, "z_gate", [P, KT, T])
        SQ = alloc(m, ctx, "gated_squares", [P, KT, P])
        RS = alloc(m, ctx, "inverse_rms", [P, 2, SG, P])
        E = alloc(m, ctx, "decays", [P, SH, P])
        XS = alloc(m, ctx, "x_by_token", [P, DI])
        XDT = alloc(m, ctx, "x_dt", [P, DI])
        XDE = alloc(m, ctx, "x_dt_decayed", [P, DI])
        Y = alloc(m, ctx, "y", [P, 2, DI])
        tmp = alloc(m, ctx, "y_tmp", [P, DI])
        BC = alloc(m, ctx, "b_and_cb", [P, 512])
        S = alloc(m, ctx, "state", [P, DI])
        DS = alloc(m, ctx, "skip_rows", [P, SH])
        eps = m.small[:, 0:1]
        identb = ctx.enter_context(nc.sbuf_tensor(f"ident_bf16_{m.phases}", [P, P], BF16))
        negb = ctx.enter_context(nc.sbuf_tensor(f"neg_bf16_{m.phases}", [P, 4, P], BF16))
        s = phase(m, "rows_in x_in z_in pe act dve pool masks m_ready chain y_sum squared inverse normed")
        block = ctx.enter_context(nc.Block())

        order = [("X", "act", 0, 2), ("B", "act", 7, 1), ("R0", "act", 4, 1), ("R1", "act", 5, 1),
                 ("R2", "act", 4, 1), ("R3", "act", 5, 1), ("G", "dve", 0, 2),
                 ("YO", "dve", 2, 2), ("ST", "dve", 6, 2), ("SS", "act", 4, 1), ("YD", "dve", 0, 2)]
        plan = [(c - (name in ("G", "SS")), name, eng, bank, n) for c in range(TT) for name, eng, bank, n in order
                if name not in ("G", "SS") or c]
        plan += [(TT - 1, "G", "dve", 0, 2), (TT - 1, "SS", "act", 4, 1)]
        count, filled, emptied, before, last_in = {"act": 0, "dve": 0}, {}, {}, {}, {}
        for i, (c, name, eng, bank, n) in enumerate(plan):
            count[eng] += 1
            filled[c, name], emptied[c, name] = i + 1, (eng, count[eng])
            before[c, name] = sorted({last_in[b] for b in range(bank, bank + n) if b in last_in})
            for b in range(bank, bank + n):
                last_in[b] = (c, name)

        def empty(eng, key):
            who, n = emptied[key]
            eng.wait_ge(s.act if who == "act" else s.dve, n)

        by_head = lambda ap: ap.rearrange("p (h c) -> p h c", h=SH)
        wide = lambda ap, c: ap[:, c * SH:(c + 1) * SH].unsqueeze(2).to_broadcast([P, SH, HD])

        @block.sync
        def _(sp):
            sp.dma_start(XB[:], xbc_d.rearrange("k p t -> p k t")).then_inc(s.x_in, 16)
            sp.dma_start(DS[:], d_skip.to_broadcast([P, SH])).then_inc(s.rows_in, 16)
            sp.dma_start(ZS[:], gate_d.rearrange("k p t -> p k t")).then_inc(s.z_in, 16)

        @block.tensor
        def _(pe):
            pe.wait_ge(s.masks, 3)
            pe.wait_ge(s.x_in, 16)
            for c, name, eng, bank, n in plan:
                for key in before[c, name]:
                    empty(pe, key)
                B = PS[:, bank, :]
                cols = slice(c * P, (c + 1) * P)
                if name == "X":
                    for q in range(KT):
                        last = pe.transpose(PS[:, bank + q // 4, (q % 4) * P:(q % 4 + 1) * P], XB[:, q, cols],
                                            m.const("ident"))
                elif name == "B":
                    for g in range(SG):
                        pe.transpose(B[:, g * P:(g + 1) * P], XB[:, KT + g, cols], m.const("ident"))
                    for g in range(SG):
                        last = pe.matmul(B[:, (2 + g) * P:(3 + g) * P], XB[:, KT + g, cols],
                                         XB[:, KT + SG + g, cols], start=True, stop=True)
                elif name[0] == "R":
                    r = int(name[1])
                    pe.matmul(B, identb[:], negb[:].rearrange("p a b -> p (a b)"), start=True, stop=False,
                              skip_group_check=True)
                    for i in range(4):
                        at = c * SH + 4 * r + i
                        last = pe.matmul(B[:, i * P:(i + 1) * P], DA[:, at:at + 1].to_broadcast([P, P]),
                                         m.const("tri"), start=False, stop=i == 3, skip_group_check=True)
                elif name == "G":
                    pe.wait_ge(s.y_sum, c + 1)
                    for q in range(KT):
                        last = pe.transpose(PS[:, bank + q // 4, (q % 4) * P:(q % 4 + 1) * P],
                                            Y[:, c % 2, q * P:(q + 1) * P], m.const("ident"))
                elif name == "SS":
                    pe.wait_ge(s.squared, c + 1)
                    for g in range(SG):
                        for q in range(KT // SG):
                            last = pe.matmul(B[:, g * P:(g + 1) * P], m.const("ones"), SQ[:, g * (KT // SG) + q],
                                             start=q == 0, stop=q == KT // SG - 1)
                elif name == "YO":
                    if c:
                        empty(pe, (c - 1, "ST"))
                    for g in range(SG):
                        last = pe.matmul(PS[:, bank + g, :], XB[:, KT + SG + g, cols], S[:, g * GW:(g + 1) * GW],
                                         start=True, stop=True)
                elif name == "ST":
                    empty(pe, (c, "B"))
                    pe.wait_ge(s.pool, 3 * c + 3)
                    for g in range(SG):
                        last = pe.matmul(PS[:, bank + g, :], BC[:, g * P:(g + 1) * P], XDE[:, g * GW:(g + 1) * GW],
                                         start=True, stop=True)
                elif name == "YD":
                    pe.wait_ge(s.m_ready, 4 * c + 4)
                    for h in range(SH):
                        last = pe.matmul(PS[:, bank + h // 8, (h % 8) * HD:(h % 8 + 1) * HD], E[:, h],
                                         XDT[:, h * HD:(h + 1) * HD], start=True, stop=True)
                last.then_inc(s.pe, 1)

        @block.scalar
        def _(act):
            def squares(c):
                empty(act, (c, "G"))
                if c:
                    act.wait_ge(s.pe, filled[c - 1, "SS"])
                nc.scalar.activation(SQ[:], HT[:, :, c * P:(c + 1) * P], ACT.Square).then_inc(s.squared, 1)

            for c, name, eng, bank, n in plan:
                if eng != "act":
                    continue
                if name == "SS":
                    squares(c)
                act.wait_ge(s.pe, filled[c, name])
                B = PS[:, bank, :]
                both = bank2(m, bank // 2)
                if name == "X":
                    if c:
                        act.wait_ge(s.pool, 3 * c)
                    ins = nc.scalar.copy(XS[:], both)
                elif name == "B":
                    ins = nc.scalar.copy(BC[:], B)
                elif name[0] == "R":
                    for i in range(4):
                        h = 4 * int(name[1]) + i
                        ins = nc.scalar.activation(E[:, h], B[:, i * P:(i + 1) * P], ACT.Exp,
                                                   bias=NA[:, c * SH + h:c * SH + h + 1])
                elif name == "SS":
                    if c >= 2:
                        act.wait_ge(s.normed, c - 1)
                    ins = nc.scalar.activation(RS[:, c % 2], B[:, 0:SG * P].rearrange("p (g n) -> p g n", g=SG),
                                               ACT.Sqrt, scale=1.0 / GW, bias=eps)
                ins.then_inc(s.act, 1)

        @block.gpsimd
        def _(pool):
            pool.wait_ge(s.rows_in, 16)
            v = nc.gpsimd
            for c in range(TT):
                empty(pool, (c, "X"))
                if c:
                    pool.wait_ge(s.pe, filled[c - 1, "YD"])
                v.tensor_tensor(by_head(XDT[:]), by_head(XS[:]), wide(DT, c), ALU.mult).then_inc(s.pool, 1)
                if c >= 2:
                    pool.wait_ge(s.pe, filled[c - 2, "G"])
                v.tensor_tensor(by_head(Y[:, c % 2]), by_head(XS[:]), DS[:].unsqueeze(2).to_broadcast([P, SH, HD]),
                                ALU.mult).then_inc(s.pool, 1)
                pool.wait_ge(s.pool, 3 * c + 1)
                v.tensor_tensor(by_head(XDE[:]), by_head(XDT[:]), wide(DE, c), ALU.mult).then_inc(s.pool, 1)

        @block.vector
        def _(dve):
            v = nc.vector
            do = Chain(dve, s.chain)
            v.tensor_copy(identb[:], m.const("ident")).then_inc(s.masks, 1)
            v.tensor_copy(negb[:], m.const("neg_up").unsqueeze(1).to_broadcast([P, 4, P])).then_inc(s.masks, 1)
            v.memset(eps, RMS_EPS_2)
            v.memset(S[:], 0.0).then_inc(s.masks, 1)
            dve.wait_ge(s.rows_in, 16)

            dve.wait_ge(s.z_in, 16)

            def gate(c):
                dve.wait_ge(s.pe, filled[c, "G"])
                v.tensor_tensor(HT[:, :, c * P:(c + 1) * P],
                                PS[:, 0:2, :].rearrange("p a (b c) -> p (a b) c", b=4),
                                ZS[:, :, c * P:(c + 1) * P], ALU.mult).then_inc(s.dve, 1)

            def normalise(c):
                empty(dve, (c, "SS"))
                v.reciprocal(RS[:, c % 2], RS[:, c % 2]).then_inc(s.inverse, 1)
                dve.wait_ge(s.inverse, c + 1)
                h = HT[:, :, c * P:(c + 1) * P].rearrange("p (g k) n -> p g k n", g=SG)
                v.tensor_tensor(h, h, RS[:, c % 2].unsqueeze(2).to_broadcast([P, SG, KT // SG, P]), ALU.mult
                                ).then_inc(s.normed, 1)

            for c in range(TT):
                for r in range(4):
                    empty(dve, (c, "B"))
                    empty(dve, (c, f"R{r}"))
                    cb = BC[:, (2 + r // 2) * P:(3 + r // 2) * P].unsqueeze(1).to_broadcast([P, 4, P])
                    v.tensor_tensor(E[:, 4 * r:4 * r + 4], E[:, 4 * r:4 * r + 4], cb, ALU.mult).then_inc(s.m_ready, 1)
                if c:
                    gate(c - 1)
                pair = lambda b: PS[:, b:b + 2, :].rearrange("p a (h c) -> p (a h) c", c=HD)
                y = by_head(Y[:, c % 2])
                dve.wait_ge(s.pe, filled[c, "YO"])
                v.tensor_tensor(by_head(tmp[:]), pair(2), wide(EI, c), ALU.mult).then_inc(s.dve, 1)
                do(v.tensor_tensor(by_head(S[:]), by_head(S[:]), wide(CD, c), ALU.mult))
                dve.wait_ge(s.dve, emptied[c, "YO"][1])
                dve.wait_ge(s.pool, 3 * c + 2)
                do(v.tensor_tensor(Y[:, c % 2], Y[:, c % 2], tmp[:], ALU.add))
                dve.wait_ge(s.pe, filled[c, "ST"])
                v.tensor_tensor(S[:], S[:], PS[:, 6:8, :].rearrange("p a b -> p (a b)"), ALU.add).then_inc(s.dve, 1)
                dve.wait_ge(s.pe, filled[c, "YD"])
                v.tensor_tensor(y, y, pair(0), ALU.add).then_inc(s.dve, 1)
                dve.wait_ge(s.dve, emptied[c, "YD"][1])
                v.sem_inc(s.y_sum, 1)
                if c:
                    normalise(c - 1)
            gate(TT - 1)
            normalise(TT - 1)


def mix_and_norm(m, layer, w, ln_g, ln_b, attn_d, src, dst):
    nc, t, PS, HT = m.nc, m.t, m.PS, m.HT
    Q = 2 * KT
    with ExitStack() as ctx:
        AR = alloc(m, ctx, "attn_raw", [P, 2, T])
        AH = alloc(m, ctx, "mixed_high", [P, Q, T], F32R)
        AL = alloc(m, ctx, "mixed_low", [P, Q, T], F32R)
        RAW = alloc(m, ctx, "w_raw", [P, 3, NH])
        WH = alloc(m, ctx, "w_high", [P, 2, NH], F32R)
        WL = alloc(m, ctx, "w_low", [P, 2, NH], F32R)
        LN = alloc(m, ctx, "ln_rows", [P, 2, D])
        s = phase(m, "a_in0 a_in1 raw0 raw1 raw2 x_in rows_in high low split wchain used prod added eps summed "
                     "centred squared root chain out stored")
        a_in, raw_in = [s.a_in0, s.a_in1], [s.raw0, s.raw1, s.raw2]
        block = ctx.enter_context(nc.Block())
        sums, mean, rstd, eps = (m.small[:, i * TT:(i + 1) * TT] for i in range(4))
        eps = eps[:, 0:1]
        X = HT
        tiles = list(range(KT, Q)) + list(range(KT))

        @block.sync
        def _(sp):
            for i in range(2 * Q):
                half, q = i // Q, tiles[i % Q]
                if i >= 3:
                    sp.wait_ge(s.split, i - 2)
                sp.dma_start(RAW[:, i % 3], w[q * P:(q + 1) * P, half * NH:(half + 1) * NH]
                             ).then_inc(raw_in[i % 3], 16)
                if i == KT:
                    sp.wait_ge(s.low, KT)
                    sp.dma_start(X[:], src.rearrange("(k p) n -> p k n", p=P)).then_inc(s.x_in, 16)
            for k in range(TT):
                sp.wait_ge(s.out, k + 1)
                sp.dma_start(dst[k * P:(k + 1) * P], X[:, k]).then_inc(s.stored, 16)
            sp.wait_ge(s.stored, 16 * TT)

        @block.tensor
        def _(pe):
            for i in range(2 * Q):
                half, q = i // Q, tiles[i % Q]
                pe.wait_ge(s.split, i + 1)
                if not half:
                    pe.wait_ge(s.low, i + 1)
                for k in range(TT):
                    if i == Q:
                        pe.wait_ge(s.added, k + 1)
                    cols = slice(k * P, (k + 1) * P)
                    for a, b in ((AH, WH), (AH, WL), (AL, WH)):
                        last = pe.matmul(PS[:, k, :], a[:, q, cols], b[:, i % 2],
                                         start=i % Q == 0 and a is AH and b is WH, stop=i % Q == Q - 1 and a is AL)
                    if i % Q == Q - 1:
                        last.then_inc(s.prod, 1)
                pe_done = last if i % Q < Q - 1 else None
                if pe_done is not None:
                    pe_done.then_inc(s.used, 1)
                else:
                    pe.wait_ge(s.prod, TT * (half + 1))
                    pe.sem_inc(s.used, 1)

        @block.gpsimd
        def _(pool):
            pool.dma_start(LN[:, 0], ln_g.to_broadcast([P, D])).then_inc(s.rows_in, 16)
            pool.dma_start(LN[:, 1], ln_b.to_broadcast([P, D])).then_inc(s.rows_in, 16)
            for i in range(2 * Q):
                pool.wait_ge(raw_in[i % 3], 16 * (i // 3 + 1))
                if i >= 2:
                    pool.wait_ge(s.used, i - 1)
                nc.gpsimd.tensor_copy(WH[:, i % 2], RAW[:, i % 3]).then_inc(s.wchain, 1)
                pool.wait_ge(s.wchain, i + 1)
                nc.gpsimd.tensor_tensor(WL[:, i % 2], RAW[:, i % 3], WH[:, i % 2], ALU.subtract).then_inc(s.split, 1)

        @block.scalar
        def _(act):
            for i in range(Q):
                q = tiles[i]
                if q >= KT:
                    nc.scalar.mul(AH[:, q], HT[:, q - KT], m.col("norm_w_2", layer * KT + q - KT)).then_inc(s.high, 1)
                else:
                    if q >= 2:
                        act.wait_ge(s.low, KT + q - 1)
                    act.dma_start(AR[:, q % 2], attn_d[q]).then_inc(a_in[q % 2], 16)
                    act.wait_ge(a_in[q % 2], 16 * (q // 2 + 1))
                    nc.scalar.copy(AH[:, q], AR[:, q % 2]).then_inc(s.high, 1)
            act.wait_ge(s.eps, 1)
            for k in range(TT):
                act.wait_ge(s.added, TT + k + 1)
                if k:
                    act.wait_ge(s.squared, k)
                nc.scalar.activation(AR[:, 0], X[:, k], ACT.Identity, accum_out=sums[:, k:k + 1]).then_inc(s.summed, 1)
                act.wait_ge(s.centred, k + 1)
                act.wait_ge(s.summed, k + 1)
                nc.scalar.activation(AR[:, 0], X[:, k], ACT.Square, accum_out=sums[:, k:k + 1]).then_inc(s.squared, 1)
                act.wait_ge(s.squared, k + 1)
                nc.scalar.activation(rstd[:, k:k + 1], sums[:, k:k + 1], ACT.Sqrt, scale=1.0 / D, bias=eps
                                     ).then_inc(s.root, 1)

        @block.vector
        def _(dve):
            v = nc.vector
            do = Chain(dve, s.chain)
            v.memset(eps, LN_EPS).then_inc(s.eps, 1)
            for i in range(Q):
                q = tiles[i]
                dve.wait_ge(s.high, i + 1)
                if q >= KT:
                    v.scalar_tensor_tensor(out=AL[:, q], in0=HT[:, q - KT],
                                           scalar=m.col("norm_w_2", layer * KT + q - KT), in1=AH[:, q],
                                           op0=ALU.mult, op1=ALU.subtract).then_inc(s.low, 1)
                else:
                    v.tensor_tensor(AL[:, q], AR[:, q % 2], AH[:, q], ALU.subtract).then_inc(s.low, 1)
            dve.wait_ge(s.x_in, 16)
            dve.wait_ge(s.rows_in, 32)
            for half in range(2):
                for k in range(TT):
                    x = X[:, k, half * NH:(half + 1) * NH]
                    dve.wait_ge(s.prod, half * TT + k + 1)
                    v.scalar_tensor_tensor(out=x, in0=x, scalar=ALPHA, in1=PS[:, k, :], op0=ALU.mult, op1=ALU.add
                                           ).then_inc(s.added, 1)
                    if half:
                        dve.wait_ge(s.summed, k + 1)
                        do(v.tensor_scalar(mean[:, k:k + 1], sums[:, k:k + 1], 1.0 / D, None, ALU.mult))
                        v.tensor_scalar(X[:, k], X[:, k], mean[:, k:k + 1], None, ALU.subtract).then_inc(s.centred, 1)
                        dve.wait_ge(s.root, k + 1)
                        do(v.reciprocal(rstd[:, k:k + 1], rstd[:, k:k + 1]))
                        do(v.scalar_tensor_tensor(out=X[:, k], in0=X[:, k], scalar=rstd[:, k:k + 1], in1=LN[:, 0],
                                                  op0=ALU.mult, op1=ALU.mult))
                        v.tensor_tensor(X[:, k], X[:, k], LN[:, 1], ALU.add).then_inc(s.out, 1)


def move(m, src, dst):
    nc = m.nc
    with nc.Block() as block:
        @block.vector
        def _(dve):
            for k in range(0, TT, 2):
                nc.vector.tensor_copy(dst[:, k], src[:, k])

        @block.scalar
        def _(act):
            for k in range(1, TT, 2):
                nc.scalar.copy(dst[:, k], src[:, k])


def first_block(m, dst):
    nc, t = m.nc, m.t
    with ExitStack() as whole:
        GM = alloc(m, whole, "gates", [P, 2, D])
        with ExitStack() as ctx:
            X = alloc(m, ctx, "x", [P, TT, D])
            modulation(m, X, GM)
            to_channels(m, X, 0)
        with ExitStack() as ctx:
            MIX = alloc(m, ctx, "mix", [P, CT, T])
            RKVQ = alloc(m, ctx, "rkvq", [P, 4 * CT, T])
            LO = alloc(m, ctx, "lora", [P, 3, T])
            with ExitStack() as slots:
                W = alloc(m, slots, "w_in_slots", [P, 2, KT, 2 * P])
                in_projection(m, MIX, RKVQ, LO, W)
            conv_branch(m, MIX)
            with ExitStack() as inner:
                G2 = alloc(m, inner, "g2", [P, 2, CW])
                PC = alloc(m, inner, "chunk_decay", [P, CT, T // CH])
                bonus = alloc(m, inner, "bonus", [P, TT * RH])
                rwkv_operands(m, RKVQ, LO, G2, m.HT[:, 0:CT], m.HT[:, CT:2 * CT], PC, bonus)
                rwkv_recurrence(m, RKVQ, m.HT[:, 0:CT], PC, LO, G2, bonus)
            tiles = [MIX[:, q] for q in range(CT)] + [RKVQ[:, 2 * CT + q] for q in range(CT)]
            out_projection(m, tiles, t.w_out, GM[:, 0], m.HT)
        X = alloc(m, whole, "x_mixed", [P, TT, D])
        move(m, m.HT, X)
        to_channels(m, X, 1)
        with ExitStack() as ctx:
            MID = alloc(m, ctx, "mid", [P, FT, T])
            up_projection(m, MID)
            down_projection(m, MID, GM[:, 1], X, dst)


def second_layer(m, i, src, dst):
    t = m.t
    row = lambda ap: ap[i:i + 1]
    scratch = lambda name, tiles: m.nc.dram_tensor(f"{name}_{i}", (tiles, P, T), F32, kind="Internal").ap()
    attn_d, xbc_d, gate_d = scratch("attn", KT), scratch("xbc", XT), scratch("gate", KT)
    with ExitStack() as whole:
        DT, DA, NA, EI, DE, CD = (alloc(m, whole, n, [P, TT * SH]) for n in ("dt", "dta", "na", "ei", "de", "cd"))
        with ExitStack() as ctx:
            HH, HL = (alloc(m, ctx, n, [P, KT, T], F32R) for n in ("x_high", "x_low"))
            turned_in(m, src, HH, HL)
            projections_and_attention(m, i, t.w_in_2[i], row(t.sinks_2), HH, HL, DT, attn_d, xbc_d, gate_d)
        step_sizes(m, row(t.dt_bias_2), row(t.a_log_2), DT, NA, EI, DE, CD, DA)
        state_space(m, row(t.d_skip_2), xbc_d, gate_d, DT, DA, NA, EI, DE, CD)
    mix_and_norm(m, i, t.w_out_2[i], row(t.ln_g_2), row(t.ln_b_2), attn_d, src, dst)


def hybrid_kernel(nc, t):
    m = make(nc, t)
    x1 = nc.dram_tensor("after_first_block", (T, D), F32, kind="Internal").ap()
    x2 = nc.dram_tensor("after_first_layer", (T, D), F32, kind="Internal").ap()
    first_block(m, x1)
    recycle(m)
    second_layer(m, 0, x1, x2)
    recycle(m)
    second_layer(m, 1, x2, t.out)
    m.ctx.close()


def laid_out(inputs):
    import numpy as _np

    a = {k: _np.ascontiguousarray(v) for k, v in inputs.items()}
    column = lambda v: v.reshape(-1, P).T
    taps = lambda w: _np.transpose(w.reshape(w.shape[0], -1, P), (2, 1, 0)).reshape(P, -1)
    mu = _np.zeros((15 * P,), a["rwkv_mu"].dtype)
    mu[:a["rwkv_mu"].shape[1]] = a["rwkv_mu"][0]
    ada = a["ada_b"][0].reshape(6, D)
    parts = {
        "c": column(a["c"][0]), "ada_b": _np.concatenate([column(ada[i]) for i in (0, 1, 3, 4)], axis=1),
        "pre_g": _np.concatenate([column(a["mix_pre_g"][0]), column(a["ffn_pre_g"][0])], axis=1),
        "mu": column(mu), "conv_b": column(a["conv_dw_b"][0]), "conv_ln_g": column(a["conv_ln_g"][0]),
        "conv_ln_b": column(a["conv_ln_b"][0]), "w0": column(a["w0"][0]), "a0": column(a["a0"][0]),
        "k_k": column(a["k_k"][0]), "k_a": column(a["k_a"][0]), "r_k": column(a["r_k"][0].reshape(-1)),
        "conv_w": taps(a["conv_dw_w"][0]), "ffn_b": column(a["ffn_dw_b"][0]), "ffn_w": taps(a["ffn_dw_w"][0]),
        "conv_b_2": _np.concatenate([column(a["conv_b_2"][i]) for i in range(LAYERS)], axis=1),
        "norm_w_2": _np.concatenate([column(a["ssm_norm_w_2"][i]) for i in range(LAYERS)], axis=1),
        "conv_w_2": _np.concatenate([taps(a["conv_w_2"][i]) for i in range(LAYERS)], axis=1),
    }
    consts, alibi = shape_constants()
    arrays = {
        "cols": _np.ascontiguousarray(_np.concatenate([parts[n] for n in COLS], axis=1)),
        "consts": consts, "alibi": alibi, "x": a["x"][0],
    }
    for name in ("ada_w", "w_in", "w_out", "w_up", "w_down", "w2", "a2", "g2"):
        arrays[name] = a[name][0]
    for name in ("ada_b", "mix_post_g", "ffn_post_g", "lnx_g", "lnx_b"):
        arrays[name] = a[name]
    for name in ("w_in_2", "w_out_2"):
        arrays[name] = a[name]
    for name in ("dt_bias_2", "a_log_2", "d_skip_2", "sinks_2", "ln_g_2", "ln_b_2"):
        arrays[name] = a[name]
    return {k: _np.ascontiguousarray(v) for k, v in arrays.items()}


def kernel(**inputs):
    from collections import namedtuple as _namedtuple

    import concourse.bacc as _bacc
    from concourse import mybir as _mybir
    from concourse.bass_utils import run_bass_kernel_spmd as _run

    nc = _bacc.Bacc("TRN2", target_bir_lowering=False, num_devices=1)
    arrays = laid_out(inputs)
    tensors = {
        n: nc.dram_tensor(n, a.shape, _mybir.dt.from_np(a.dtype), kind="ExternalInput").ap()
        for n, a in arrays.items()
    }
    tensors["out"] = nc.dram_tensor("out", (T, D), F32, kind="ExternalOutput").ap()
    t = _namedtuple("Tensors", list(tensors))(*tensors.values())
    hybrid_kernel(nc, t)
    r = _run(nc, [arrays], core_ids=[0])
    return r.results[0]["out"].reshape(1, T, D)
```

```python
from collections import namedtuple
from contextlib import ExitStack

import numpy as np

import concourse.bass as bass
from concourse import mybir

F32 = mybir.dt.float32
F32R = mybir.dt.float32r
ACT = mybir.ActivationFunctionType
ALU = mybir.AluOpType
AX = mybir.AxisListType.X

P = 128
T = 1024
D = 1024
TT = T // P
KT = D // P
NH = T // 2
CW = 512
CT = CW // P
CONV_K = 31
CPAD = CONV_K - 1
HD = 64
RH = CW // HD
LORA = 64
GLORA = 160
CH = 64
BLK = 16
D_FF = 2816
FT = D_FF // P
RMS_EPS, LN_EPS, LNX_EPS, RMS_EPS_2 = 1e-6, 1e-5, 64e-5, 1e-5
DECAY = float(np.exp(-0.5))

LAYERS = 2
QH, KVH = 16, 4
KVW = KVH * HD
DI = 1024
SH = DI // HD
SG = 2
HG = SH // SG
NS = 128
XBC = DI + 2 * SG * NS
XT = XBC // P
O_Q, O_K, O_V, O_ZA = 0, D, D + KVW, D + 2 * KVW
O_ZS = O_ZA + D
O_XBC = O_ZS + DI
O_DT = O_XBC + XBC
IN_W = O_DT + SH
ALPHA = (2.0 * LAYERS) ** 0.25
CK2 = 4

COLS = {}
for _name, _n in [
    ("c", KT), ("ada_b", 4 * KT), ("pre_g", 2 * KT), ("mu", 15), ("conv_b", CT), ("conv_ln_g", CT),
    ("conv_ln_b", CT), ("w0", CT), ("a0", CT), ("k_k", CT), ("k_a", CT), ("r_k", CT),
    ("conv_w", CT * CONV_K), ("ffn_b", 2 * FT), ("ffn_w", 2 * FT * 3),
    ("conv_b_2", LAYERS * XT), ("conv_w_2", LAYERS * XT * CK2),
    ("norm_w_2", LAYERS * KT),
]:
    COLS[_name] = (sum(n for _, n in COLS.values()), _n)
NCOLS = sum(n for _, n in COLS.values())

CONSTS = {}
for _name, _n in [
    ("ident", P), ("ones", P), ("headones", P), ("mask_incl_up", P), ("mask_diag_up", P), ("mask_incl_up_2", P), ("mask_strict_up", P),
    ("mask_diag_low", P), ("mask_off_low", P), ("chunk_row", T), ("tri", P), ("neg_up", P), ("minus_last", P),
    ("ident_heads", HD),
]:
    CONSTS[_name] = (sum(n for _, n in CONSTS.values()), _n)
NCONSTS = sum(n for _, n in CONSTS.values())


def shape_constants():
    i, j = np.arange(P)[:, None], np.arange(P)[None, :]
    chunk = (i // CH) == (j // CH)
    block = (i // BLK) == (j // BLK)
    parts = {
        "ident": i == j, "ones": i >= 0 * j, "headones": (i // HD) == (j // HD),
        "mask_diag_up": block & (i < j), "mask_incl_up": chunk & (i <= j), "mask_strict_up": chunk & (i < j),
        "mask_incl_up_2": chunk & (i <= j), "ident_heads": (i % HD) == np.arange(HD)[None, :],
        "mask_diag_low": block & (i > j), "mask_off_low": chunk & ~block & (i > j),
        "chunk_row": np.broadcast_to(np.arange(T) % CH != 0, (P, T)), "tri": i <= j,
        "neg_up": np.where(i > j, -1e30, 0.0), "minus_last": np.where((i == P - 1) & (j >= 0), -1.0, 0.0),
    }
    consts = np.concatenate([np.asarray(parts[n]).astype(np.float32) for n in CONSTS], axis=1)
    q, s = np.arange(P)[:, None], np.arange(2 * P)[None, :]
    dist = q - s + P
    slopes = 2.0 ** (-8.0 * np.arange(1, QH + 1) / QH)
    alibi = np.where((dist >= 0) & (dist < P), -8.0 * slopes[:, None, None] * dist, -1e30)
    return consts, np.ascontiguousarray(alibi.transpose(1, 0, 2).astype(np.float32))


def flat(ap):
    return ap.rearrange("p a b -> p (a b)")


def alloc(m, ctx, name, shape, dtype=F32):
    m.tensors += 1
    return ctx.enter_context(m.nc.sbuf_tensor(f"{name}_sb{m.tensors}", shape, dtype))


class Machine:

    def __init__(self, nc, t):
        self.nc, self.t = nc, t
        self.ctx = ExitStack()
        self.tensors = 0
        self.phases = 0
        self.used = []


def make(nc, t):
    m = Machine(nc, t)
    sb = lambda name, shape: alloc(m, m.ctx, name, shape)
    m.PS = m.ctx.enter_context(nc.psum_tensor("PS", [P, 8, 512], F32))
    m.cols = sb("cols", [P, NCOLS])
    m.consts = sb("consts", [P, NCONSTS])
    m.mod_shift = sb("mod_shift", [P, 2, KT])
    m.mod_scale = sb("mod_scale", [P, 2, KT])
    m.small = sb("small", [P, 64])
    m.silu_c = sb("silu_c", [P, KT])
    m.HT = None
    m.col = lambda name, k=0, n=1: m.cols[:, COLS[name][0] + k:COLS[name][0] + k + n]
    m.const = lambda name: m.consts[:, CONSTS[name][0]:CONSTS[name][0] + CONSTS[name][1]]
    return m


class Chain:

    def __init__(self, eng, sem):
        self.eng, self.sem, self.n = eng, sem, 0

    def __call__(self, ins):
        self.n += 1
        ins.then_inc(self.sem, 1)
        self.eng.wait_ge(self.sem, self.n)


def phase(m, names):
    m.phases += 1
    handles = [m.nc.alloc_semaphore(f"{n}_{m.phases}") for n in names.split()]
    m.used += handles
    return namedtuple("Signals", names)(*handles)


def recycle(m):
    m.nc.clear_and_free_semaphores(m.used)
    m.used = []
    m.nc.all_engine_barrier()


class AdaColumns:
    signals = "w_in0 w_in1 used columns biased"

    def __init__(self, m, s, sub, slots, bank, width=512):
        self.m, self.s, self.sub, self.slots, self.bank, self.width = m, s, sub, slots, bank, width
        self.blocks = 2 * D // width

    def load(self, sp, b):
        if b >= 2:
            sp.wait_ge(self.s.used, b - 1)
        at = 3 * D * self.sub + b * self.width
        sp.dma_start(self.slots[b % 2], self.m.t.ada_w[:, at:at + self.width].rearrange("(k p) n -> p k n", p=P)
                     ).then_inc((self.s.w_in0, self.s.w_in1)[b % 2], 16)

    def products(self, pe, b):
        pe.wait_ge((self.s.w_in0, self.s.w_in1)[b % 2], 16 * (b // 2 + 1))
        for j in range(self.width // P):
            at = b * (self.width // P) + j
            for k in range(KT):
                last = pe.matmul(self.m.PS[:, self.bank, at:at + 1], self.slots[b % 2][:, k, j * P:(j + 1) * P],
                                 self.m.silu_c[:, k:k + 1], start=k == 0, stop=k == KT - 1)
        last.then_inc(self.s.used, 1)

    def finish(self, dve):
        m, s, i = self.m, self.s, self.sub
        dve.wait_ge(s.used, self.blocks)
        both = m.small[:, 32:32 + 2 * KT]
        m.nc.vector.tensor_tensor(both, m.PS[:, self.bank, 0:2 * KT], m.col("ada_b", 2 * KT * i, 2 * KT), ALU.add
                                  ).then_inc(s.biased, 1)
        dve.wait_ge(s.biased, 1)
        m.nc.vector.tensor_copy(m.mod_shift[:, i], both[:, 0:KT]).then_inc(s.columns, 1)
        m.nc.vector.scalar_tensor_tensor(out=m.mod_scale[:, i], in0=both[:, KT:2 * KT], scalar=1.0,
                                         in1=m.col("pre_g", KT * i, KT), op0=ALU.add, op1=ALU.mult
                                         ).then_inc(s.columns, 1)


def bank2(m, b, rows=P):
    return m.PS[0:rows, 2 * b:2 * b + 2, :].rearrange("p a b -> p (a b)")


class NormedIn:
    signals = ("in0 in1 in2 in3 in4 in5 in6 in7 sq eps rooted rstd normed turned high free low par_in silu "
               + AdaColumns.signals)

    def __init__(self, m, src, norm, HH, HL, room, ada_room=None):
        self.m, self.src, self.norm, self.HH, self.HL = m, src, norm, HH, HL
        self.X, self.ev = room[:, 0:TT], room[:, TT].rearrange("p (a b) -> p a b", a=2)
        self.s = s = phase(m, self.signals)
        self.x_in = [s.in0, s.in1, s.in2, s.in3, s.in4, s.in5, s.in6, s.in7]
        self.ada = AdaColumns(m, s, norm, ada_room, 0) if ada_room else None
        self.rstd, self.eps = m.small[:, TT:2 * TT], m.small[:, 2 * TT:2 * TT + 1]
        self.sums = m.small[:, 0:TT]

    def at(self, n):
        return slice(None), n % KT, slice(n // KT * NH, (n // KT + 1) * NH)

    def scale_shift(self, n):
        k = n % KT
        return self.m.mod_scale[:, self.norm, k:k + 1], self.m.mod_shift[:, self.norm, k:k + 1]

    def sync(self, sp):
        m, s = self.m, self.s
        if self.ada:
            sp.dma_start(m.cols[:], m.t.cols).then_inc(s.par_in, 16)
            sp.dma_start(m.consts[:], m.t.consts).then_inc(s.par_in, 16)
            for b in range(2):
                self.ada.load(sp, b)
        for k in range(TT):
            sp.dma_start(self.X[:, k], self.src[k * P:(k + 1) * P]).then_inc(self.x_in[k], 16)
            if self.ada and k in (3, TT - 1):
                self.ada.load(sp, 2 + k // 4)

    def tensor(self, pe):
        m, s = self.m, self.s
        if self.ada:
            pe.wait_ge(s.silu, 1)
            for b in range(4):
                self.ada.products(pe, b)
            pe.wait_ge(s.biased, 1)
        for n in range(2 * KT):
            half, k = n // KT, n % KT
            if k == 0:
                pe.wait_ge(s.normed, 4 * half + 4)
            if half:
                pe.wait_ge(s.free, k + 1)
            for j in range(4):
                last = pe.transpose(m.PS[:, k, j * P:(j + 1) * P], self.X[:, 4 * half + j, k * P:(k + 1) * P],
                                    m.const("ident"))
            last.then_inc(s.turned, 1)
        pe.wait_ge(s.low, 2 * KT)

    def scalar(self, act):
        m, s, nc = self.m, self.s, self.m.nc
        if self.ada:
            act.wait_ge(s.par_in, 32)
            nc.scalar.activation(m.silu_c[:], m.col("c", 0, KT), ACT.Silu).then_inc(s.silu, 1)
        act.wait_ge(s.eps, 1)
        junk = self.HH[:, 0]
        for k in range(TT):
            act.wait_ge(self.x_in[k], 16)
            if k:
                act.wait_ge(s.sq, k)
            nc.scalar.activation(junk, self.X[:, k], ACT.Square, accum_out=self.sums[:, k:k + 1]).then_inc(s.sq, 1)
            act.wait_ge(s.sq, k + 1)
            nc.scalar.activation(self.rstd[:, k:k + 1], self.sums[:, k:k + 1], ACT.Sqrt, scale=1.0 / D,
                                 bias=self.eps).then_inc(s.rooted, 1)
        if self.ada:
            act.wait_ge(s.columns, 2)
        for n in range(2 * KT):
            scale, shift = self.scale_shift(n)
            act.wait_ge(s.turned, n + 1)
            nc.scalar.activation(self.HH[self.at(n)], m.PS[:, n % KT, :], ACT.Identity, scale=scale, bias=shift
                                 ).then_inc(s.high, 1)

    def vector(self, dve):
        m, s, v = self.m, self.s, self.m.nc.vector
        v.memset(self.eps, RMS_EPS).then_inc(s.eps, 1)
        for k in range(TT):
            dve.wait_ge(s.rooted, k + 1)
            v.reciprocal(self.rstd[:, k:k + 1], self.rstd[:, k:k + 1]).then_inc(s.rstd, 1)
            dve.wait_ge(s.rstd, k + 1)
            v.tensor_scalar(self.X[:, k], self.X[:, k], self.rstd[:, k:k + 1], None, ALU.mult).then_inc(s.normed, 1)
        if self.ada:
            self.ada.finish(dve)
            dve.wait_ge(s.columns, 2)
        for n in range(2 * KT):
            scale, shift = self.scale_shift(n)
            dve.wait_ge(s.high, n + 1)
            if n >= 2:
                dve.wait_ge(s.low, n - 1)
            v.tensor_scalar(self.ev[:, n % 2], m.PS[:, n % KT, :], scale, shift, ALU.mult, ALU.add
                            ).then_inc(s.free, 1)

    def gpsimd(self, pool, steps):
        s = self.s
        for n in steps:
            pool.wait_ge(s.free, n + 1)
            self.m.nc.gpsimd.tensor_tensor(self.HL[self.at(n)], self.ev[:, n % 2], self.HH[self.at(n)],
                                           ALU.subtract).then_inc(s.low, 1)


def half_product(m, pe, WH, WL, HH, HL, bank, half):
    for k in range(KT):
        for a, b in ((WH, HH), (WH, HL), (WL, HH)):
            last = pe.matmul(m.PS[:, bank, :], a[:, k], b[:, k, half * NH:(half + 1) * NH],
                             start=k == 0 and a is WH and b is HH, stop=k == KT - 1 and a is WL)
    return last


def in_projection(m, MIX, RKVQ, LO, HH, HL, h):
    nc, t, PS = m.nc, m.t, m.PS
    with ExitStack() as ctx:
        RAW = alloc(m, ctx, "w_raw", [P, 2, KT, P])
        WH = alloc(m, ctx, "w_high", [P, 2, KT, P], F32R)
        WL = alloc(m, ctx, "w_low", [P, 2, KT, P], F32R)
        om = alloc(m, ctx, "one_minus_mu", [P, 15])
        U = RKVQ[:, 3 * CT:4 * CT].rearrange("p (a b) t -> p a (b t)", a=2)[:, :, 0:CPAD + T]
        s = phase(m, "raw0 raw1 whigh split tile om pad sig gated part shifted conv")
        raw_in = [s.raw0, s.raw1]
        block = ctx.enter_context(nc.Block())

        jobs, others = [], [("rkv", i) for i in range(3 * CT)] + [("lora", i) for i in range(3)]
        for q in range(CT):
            jobs += [("gate", q), ("u", q)] + others[:3]
            others = others[3:]
        jobs += others
        N = len(jobs)
        column = {"u": 0, "gate": CW, "rkv": 2 * CW, "lora": 5 * CW}
        width = lambda job: GLORA - P if job == ("lora", 2) else P
        rows = width
        gates = [j for j in jobs if j[0] == "gate"]
        us = [j for j in jobs if j[0] == "u"]
        shifts = [j for j in jobs if j[0] in ("rkv", "lora")]
        pair = lambda n: n % 4

        def free(eng, n):
            job = jobs[n]
            if job[0] == "gate":
                eng.wait_ge(s.sig, gates.index(job) + 1)
            elif job[0] == "u":
                eng.wait_ge(s.gated, us.index(job) + 1)
            else:
                eng.wait_ge(s.shifted, shifts.index(job) + 1)

        @block.sync
        def _(sp):
            h.sync(sp)
            for n, job in enumerate(jobs):
                if n >= 2:
                    sp.wait_ge(s.split, n - 1)
                at, w = column[job[0]] + job[1] * P, width(job)
                sp.dma_start(RAW[:, n % 2, :, 0:w], t.w_in[:, at:at + w].rearrange("(k p) n -> p k n", p=P)
                             ).then_inc(raw_in[n % 2], 16)

        @block.gpsimd
        def _(pool):
            h.gpsimd(pool, range(KT))
            for n in range(N):
                if n == 1:
                    h.gpsimd(pool, range(KT, 2 * KT))
                pool.wait_ge(raw_in[n % 2], 16 * (n // 2 + 1))
                if n >= 2:
                    pool.wait_ge(s.tile, n - 1)
                nc.gpsimd.tensor_copy(WH[:, n % 2], RAW[:, n % 2]).then_inc(s.whigh, 1)
                pool.wait_ge(s.whigh, n + 1)
                nc.gpsimd.tensor_tensor(WL[:, n % 2], RAW[:, n % 2], WH[:, n % 2], ALU.subtract).then_inc(s.split, 1)

        @block.tensor
        def _(pe):
            h.tensor(pe)
            for n in range(N):
                pe.wait_ge(s.split, n + 1)
                if n >= 4:
                    free(pe, n - 4)
                for half in range(2):
                    last = half_product(m, pe, WH[:, n % 2], WL[:, n % 2], HH, HL, 2 * pair(n) + half, half)
                last.then_inc(s.tile, 1)

        @block.scalar
        def _(act):
            h.scalar(act)
            act.wait_ge(s.om, 1)
            for n, (kind, i) in enumerate(jobs):
                if kind == "u":
                    continue
                act.wait_ge(s.tile, n + 1)
                if kind == "gate":
                    nc.scalar.activation(MIX[:, i], bank2(m, pair(n)), ACT.Sigmoid).then_inc(s.sig, 1)
                elif kind == "rkv":
                    nc.scalar.activation(RKVQ[:, i], bank2(m, pair(n)), ACT.Identity, scale=om[:, i:i + 1]
                                         ).then_inc(s.part, 1)
                else:
                    r = rows((kind, i))
                    nc.scalar.activation(LO[0:r, i], bank2(m, pair(n), r), ACT.Identity,
                                         scale=om[0:r, 12 + i:13 + i]).then_inc(s.part, 1)
            for i in range(3):
                r = (LORA, P, GLORA - P)[i]
                act.wait_ge(s.shifted, len(shifts) - 2 + i)
                nc.scalar.activation(LO[0:r, i], LO[0:r, i], ACT.Sigmoid if i else ACT.Tanh)

        @block.vector
        def _(dve):
            v = nc.vector
            h.vector(dve)
            v.tensor_scalar(om[:], m.col("mu", 0, 15), -1.0, 1.0, ALU.mult, ALU.add).then_inc(s.om, 1)
            v.memset(U[:, :, 0:CPAD], 0.0).then_inc(s.pad, 1)
            dve.wait_ge(s.pad, 1)
            taps = []

            def tap():
                q, k = taps.pop(0)
                out, u = MIX[:, q], U[:, q % 2, k:k + T]
                w = m.col("conv_w", q * CONV_K + k)
                if k == 0:
                    ins = v.tensor_scalar(out, u, w, m.col("conv_b", q), ALU.mult, ALU.add)
                else:
                    ins = v.scalar_tensor_tensor(out=out, in0=u, scalar=w, in1=out, op0=ALU.mult, op1=ALU.add)
                ins.then_inc(s.conv, 1)
                dve.wait_ge(s.conv, q * CONV_K + k + 1)

            for n, (kind, i) in enumerate(jobs):
                if kind == "u":
                    while taps and taps[0][0] <= i - 2:
                        tap()
                    dve.wait_ge(s.tile, n + 1)
                    dve.wait_ge(s.sig, i + 1)
                    v.tensor_tensor(U[:, i % 2, CPAD:CPAD + T], bank2(m, pair(n)), MIX[:, i], ALU.mult
                                    ).then_inc(s.gated, 1)
                    dve.wait_ge(s.gated, i + 1)
                    taps += [(i, k) for k in range(CONV_K)]
                elif kind in ("rkv", "lora"):
                    at = i if kind == "rkv" else 12 + i
                    r = rows((kind, i))
                    dst = (RKVQ if kind == "rkv" else LO)[0:r, i, 1:T]
                    dve.wait_ge(s.part, shifts.index((kind, i)) + 1)
                    v.scalar_tensor_tensor(out=dst, in0=bank2(m, pair(n), r)[:, 0:T - 1],
                                           scalar=m.col("mu", at)[0:r], in1=dst, op0=ALU.mult, op1=ALU.add
                                           ).then_inc(s.shifted, 1)
                for _ in range(min(8, len(taps))):
                    tap()
            while taps:
                tap()


def conv_branch(m, MIX, GM, room, rows):
    nc, t, PS = m.nc, m.t, m.PS
    with ExitStack() as ctx:
        mean = alloc(m, ctx, "mean", [P, T])
        rstd = alloc(m, ctx, "rstd", [P, T])
        sq = alloc(m, ctx, "squares", [P, CT, T])
        silu_cb = alloc(m, ctx, "silu_c_wide", [P, KT, P])
        s = phase(m, "eps sums mean centred sq root chain out rows_in silub g_in0 g_in1 gate_used gate_free "
                     "gain")
        block = ctx.enter_context(nc.Block())
        eps = m.small[:, 0:1]
        g_in = [s.g_in0, s.g_in1]
        gate_at = [(2 + 3 * (g // 2)) * D + (g % 2) * 512 for g in range(4)]

        @block.sync
        def _(sp):
            for g in range(4):
                if g >= 2:
                    sp.wait_ge(s.gate_used, g - 1)
                sp.dma_start(room[g % 2], t.ada_w[:, gate_at[g]:gate_at[g] + 512].rearrange("(k p) n -> p k n", p=P)
                             ).then_inc(g_in[g % 2], 16)

        @block.gpsimd
        def _(pool):
            for i, g in enumerate((t.mix_post_g, t.ffn_post_g)):
                pool.dma_start(rows[:, i, 0], t.ada_b[:, (3 * i + 2) * D:(3 * i + 3) * D].to_broadcast([P, D])
                               ).then_inc(s.rows_in, 16)
                pool.dma_start(rows[:, i, 1], g.to_broadcast([P, D])).then_inc(s.rows_in, 16)

        @block.tensor
        def _(pe):
            def sum_tiles(src, bank):
                for half in range(2):
                    for q in range(CT):
                        last = pe.matmul(PS[:, 2 * bank + half, :], m.const("ones"),
                                         src[:, q, half * NH:(half + 1) * NH], start=q == 0, stop=q == CT - 1)
                last.then_inc(s.sums, 1)

            sum_tiles(MIX, 0)
            pe.wait_ge(s.silub, KT)
            for g in range(4):
                if g == 2:
                    pe.wait_ge(s.sq, CT)
                    sum_tiles(sq, 1)
                pe.wait_ge(g_in[g % 2], 16 * (g // 2 + 1))
                if g >= 2:
                    pe.wait_ge(s.gate_free, 1)
                for k in range(KT):
                    last = pe.matmul(PS[:, 6 + g % 2, :], silu_cb[:, k], room[g % 2][:, k], start=k == 0,
                                     stop=k == KT - 1)
                last.then_inc(s.gate_used, 1)

        @block.scalar
        def _(act):
            act.wait_ge(s.sums, 1)
            nc.scalar.mul(mean[:], bank2(m, 0), 1.0 / CW).then_inc(s.mean, 1)
            for q in range(CT):
                act.wait_ge(s.centred, q + 1)
                nc.scalar.activation(sq[:, q], MIX[:, q], ACT.Square).then_inc(s.sq, 1)
            act.wait_ge(s.sums, 2)
            act.wait_ge(s.eps, 1)
            nc.scalar.activation(rstd[:], bank2(m, 1), ACT.Sqrt, scale=1.0 / CW, bias=eps).then_inc(s.root, 1)
            for q in range(CT):
                act.wait_ge(s.out, q + 1)
                nc.scalar.activation(MIX[:, q], MIX[:, q], ACT.Silu, scale=m.col("conv_ln_g", q),
                                     bias=m.col("conv_ln_b", q))

        @block.vector
        def _(dve):
            nc.vector.memset(eps, LN_EPS).then_inc(s.eps, 1)
            for k in range(KT):
                nc.vector.tensor_scalar(silu_cb[:, k], m.const("ones"), m.silu_c[:, k:k + 1], None, ALU.mult
                                        ).then_inc(s.silub, 1)
            dve.wait_ge(s.mean, 1)
            for q in range(CT):
                nc.vector.tensor_tensor(MIX[:, q], MIX[:, q], mean[:], ALU.subtract).then_inc(s.centred, 1)
            dve.wait_ge(s.root, 1)
            nc.vector.reciprocal(rstd[:], rstd[:]).then_inc(s.chain, 1)
            dve.wait_ge(s.chain, 1)
            for q in range(CT):
                nc.vector.tensor_tensor(MIX[:, q], MIX[:, q], rstd[:], ALU.mult).then_inc(s.out, 1)
            dve.wait_ge(s.rows_in, 64)
            for i in range(2):
                dve.wait_ge(s.gate_used, 2 * i + 2)
                nc.vector.tensor_tensor(GM[:, i], bank2(m, 3), rows[:, i, 0], ALU.add).then_inc(s.gate_free, 1)
                dve.wait_ge(s.gate_free, i + 1)
                nc.vector.tensor_tensor(GM[:, i], GM[:, i], rows[:, i, 1], ALU.mult).then_inc(s.gain, 1)


def rwkv_operands(m, RKVQ, LO, G2, A, CS, PC, bonus):
    nc, t, PS = m.nc, m.t, m.PS
    with ExitStack() as ctx:
        WA = alloc(m, ctx, "lora_w", [P, CW])
        rk_col = alloc(m, ctx, "rk_col", [P, CT, 2])
        om = alloc(m, ctx, "one_minus_ka", [P, CT])
        sq = alloc(m, ctx, "key_squares", [P, 2, T])
        nrm = alloc(m, ctx, "key_norm", [P, 2, T])
        tmp = alloc(m, ctx, "tmp", [P, 2, T])
        ex = alloc(m, ctx, "exps", [P, 3, T])
        ada_slots = alloc(m, ctx, "ada_slots", [P, 2, KT, 2 * P])
        SG_ = CS
        s = phase(m, "w_in g_in z sig sq ss root kkn dif e1 e2 e3 rk bonus e3_used chain "
                     + AdaColumns.signals)
        block = ctx.enter_context(nc.Block())
        ada = AdaColumns(m, s, 1, [ada_slots[:, 0], ada_slots[:, 1]], 6, 2 * P)
        R = lambda q: RKVQ[:, q]
        K = lambda q: RKVQ[:, CT + q]
        Q = lambda q: RKVQ[:, 3 * CT + q]

        @block.sync
        def _(sp):
            sp.dma_start(WA[0:LORA], t.w2).then_inc(s.w_in, 16)
            sp.dma_start(WA[LORA:P], t.a2).then_inc(s.w_in, 16)
            sp.dma_start(G2[:, 0], t.g2[0:P]).then_inc(s.g_in, 16)
            sp.dma_start(G2[0:GLORA - P, 1], t.g2[P:GLORA]).then_inc(s.g_in, 16)
            for b in range(ada.blocks):
                ada.load(sp, b)
            sp.wait_ge(s.g_in, 32)

        @block.tensor
        def _(pe):
            for q in range(CT):
                pe.wait_ge(s.sq, q + 1)
                if q >= 2:
                    pe.wait_ge(s.root, q - 1)
                for half in range(2):
                    last = pe.matmul(PS[:, 4 * (q % 2) + half, :], m.const("headones"),
                                     sq[:, q % 2, half * NH:(half + 1) * NH], start=True, stop=True)
                last.then_inc(s.ss, 1)
                if q:
                    ada.products(pe, q - 1)
            pe.wait_ge(s.w_in, 32)
            pe.wait_ge(s.root, CT)
            for q in range(CT):
                if q:
                    pe.wait_ge(s.sig, 2 * q)
                for side in range(2):
                    for half in range(2):
                        last = pe.matmul(PS[:, 2 * side + half, :],
                                         WA[LORA * side:LORA * side + LORA, q * P:(q + 1) * P],
                                         LO[LORA * side:LORA * side + LORA, 0, half * NH:(half + 1) * NH],
                                         start=True, stop=True)
                last.then_inc(s.z, 1)
            for q in range(CT):
                pe.wait_ge(s.rk, q + 1)
                for k in range(TT):
                    last = pe.matmul(PS[:, 7, k * RH + 2 * q:k * RH + 2 * q + 2], tmp[:, q % 2, k * P:(k + 1) * P],
                                     rk_col[:, q], start=True, stop=True)
                last.then_inc(s.bonus, 1)
            for b in range(CT - 1, ada.blocks):
                ada.products(pe, b)

        @block.scalar
        def _(act):
            for q in range(CT + 1):
                if q < CT:
                    if q >= 2:
                        act.wait_ge(s.ss, q - 1)
                    nc.scalar.activation(sq[:, q % 2], K(q), ACT.Square, scale=m.col("k_k", q)).then_inc(s.sq, 1)
                if q:
                    if q > 2:
                        act.wait_ge(s.kkn, q - 2)
                    act.wait_ge(s.ss, q)
                    nc.scalar.activation(nrm[:, (q - 1) % 2], bank2(m, 2 * ((q - 1) % 2)), ACT.Sqrt).then_inc(s.root, 1)
            for q in range(CT):
                act.wait_ge(s.z, q + 1)
                nc.scalar.activation(SG_[:, q], bank2(m, 0), ACT.Sigmoid, bias=m.col("w0", q)
                                     ).then_inc(s.sig, 1)
                nc.scalar.activation(A[:, q], bank2(m, 1), ACT.Sigmoid, bias=m.col("a0", q)
                                     ).then_inc(s.sig, 1)
            for q in range(CT):
                if q:
                    act.wait_ge(s.e3_used, q)
                act.wait_ge(s.dif, q + 1)
                nc.scalar.activation(ex[:, 0], tmp[:, q % 2], ACT.Exp, scale=-DECAY).then_inc(s.e1, 1)
                nc.scalar.activation(ex[:, 1], CS[:, q], ACT.Exp, scale=DECAY).then_inc(s.e2, 1)
                nc.scalar.activation(ex[:, 2], CS[:, q], ACT.Exp, scale=-DECAY).then_inc(s.e3, 1)

        @block.vector
        def _(dve):
            do = Chain(dve, s.chain)
            v = nc.vector
            do(v.tensor_scalar(om[:], m.col("k_a", 0, CT), -1.0, 1.0, ALU.mult, ALU.add))
            do(v.tensor_tensor(rk_col[:], m.col("r_k", 0, CT).unsqueeze(2).to_broadcast([P, CT, 2]),
                               m.const("headones")[:, 0:P:HD].unsqueeze(1).to_broadcast([P, CT, 2]), ALU.mult))
            for q in range(CT):
                v.tensor_scalar(Q(q), K(q), m.col("k_k", q), None, ALU.mult)
                dve.wait_ge(s.root, q + 1)
                n = nrm[:, q % 2]
                do(v.tensor_scalar(n, n, 1e-12, None, ALU.max))
                do(v.reciprocal(n, n))
                v.tensor_tensor(Q(q), Q(q), n, ALU.mult).then_inc(s.kkn, 1)
            for q in range(CT):
                dve.wait_ge(s.sig, 2 * q + 2)
                if q >= 2:
                    dve.wait_ge(s.bonus, q - 1)
                do(v.tensor_scalar(tmp[:, q % 2], A[:, q], m.col("k_a", q), om[:, q:q + 1], ALU.mult, ALU.add))
                do(v.tensor_tensor(K(q), K(q), tmp[:, q % 2], ALU.mult))
                v.tensor_tensor(tmp[:, q % 2], R(q), K(q), ALU.mult).then_inc(s.rk, 1)
            for q in range(CT):
                d = tmp[:, q % 2]
                if q < 2:
                    dve.wait_ge(s.bonus, q + 3)
                do(v.tensor_copy(d, SG_[:, q]))
                do(v.tensor_tensor_scan(CS[:, q], m.const("chunk_row"), d, 0.0, ALU.mult, ALU.add))
                if q >= 2:
                    dve.wait_ge(s.e1, q - 1)
                v.tensor_tensor(d, CS[:, q], d, ALU.subtract).then_inc(s.dif, 1)
                do(v.scalar_tensor_tensor(out=A[:, q], in0=A[:, q], scalar=-1.0, in1=Q(q), op0=ALU.mult,
                                          op1=ALU.mult))
                dve.wait_ge(s.e1, q + 1)
                v.tensor_tensor(Q(q), Q(q), ex[:, 0], ALU.mult)
                dve.wait_ge(s.e2, q + 1)
                v.tensor_tensor(A[:, q], A[:, q], ex[:, 1], ALU.mult)
                v.tensor_tensor(K(q), K(q), ex[:, 1], ALU.mult)
                dve.wait_ge(s.e3, q + 1)
                v.tensor_copy(PC[:, q], ex[:, 2, CH - 1::CH])
                v.tensor_tensor(R(q), R(q), ex[:, 2], ALU.mult).then_inc(s.e3_used, 1)
            v.tensor_copy(bonus[:], PS[:, 7, 0:TT * RH])
            ada.finish(dve)


def rwkv_recurrence(m, RKVQ, A, PC, LO, G2, bonus):
    nc, t, PS = m.nc, m.t, m.PS
    HB = 4
    with ExitStack() as ctx:
        tok = m.HT[:, 4:6].rearrange("p a (g i c) -> p (a g) i c", g=1, i=4)
        BR = m.HT[:, 6:8].rearrange("p g (h a c) -> p g h a c", h=HB, a=2)
        GR = alloc(m, ctx, "k_products", [P, 2, HB, 2, P])
        ND = alloc(m, ctx, "n_blocks", [P, 2, HB, P])
        NE = alloc(m, ctx, "n_rest", [P, 2, HB, P])
        P2 = alloc(m, ctx, "power2", [P, 2, 2, HB, P])
        P4 = alloc(m, ctx, "power4", [P, 2, 2, HB, P])
        IB = alloc(m, ctx, "block_inverse", [P, 2, HB, P])
        P8 = P2[:, :, 0]
        XR = P4[:, :, 0]
        FR = P4[:, :, 1]
        ZZ = ND
        WU = P2[:, :, 1]
        MT = alloc(m, ctx, "transition", [P, 2, 2, 2, HD])
        ZT = alloc(m, ctx, "read_out", [P, CT, P])
        S = alloc(m, ctx, "state", [P, CT, HD])
        Y = alloc(m, ctx, "y", [P, CW])
        Y2 = alloc(m, ctx, "y_tmp", [P, CW])
        VB = alloc(m, ctx, "v_bonus", [P, 2, CW])
        GT = alloc(m, ctx, "gate", [P, CW])
        LNX = alloc(m, ctx, "lnx_rows", [P, 2, CW])
        st = alloc(m, ctx, "stats", [P, 4, RH])
        s = phase(m, "rows_in pe order act dve pool eps chain achain init squared y_ready")
        block = ctx.enter_context(nc.Block())

        inner = [("TRa", "act"), ("TRb", "act"), ("PBa", "dve"), ("PBb", "dve"), ("N", "dve"), ("PGa", "dve"),
                 ("PGb", "dve"), ("SQ1a", "dve"), ("SQ1b", "act"), ("AP1", "dve"), ("SQ2a", "dve"),
                 ("SQ2b", "act"), ("AP2", "dve"), ("SQ3", "act"), ("GV", "act"), ("AP3", "dve"), ("FR", "act"),
                 ("Z", "act"), ("H1", "dve"), ("H2", "dve"), ("H3", "dve"), ("MT", "dve"), ("ZT", "dve")]
        plan = []
        for k in range(TT):
            for n, (name, eng) in enumerate(inner):
                plan += [(k, g, name, eng, 3 * g + n % 3) for g in range(2)]
                if name == "GV" and k:
                    plan.append((k - 1, 0, "YT", "act", 3 * 0 + (n + 1) % 3))
            plan += [(k, 0, "S0", "dve", 7), (k, 0, "GT", "act", 0), (k, 0, "S1", "dve", 7), (k, 0, "Y", "dve", 6)]
        plan.append((TT - 1, 0, "YT", "act", 1))
        count, filled, emptied, before, last_in = {"act": 0, "dve": 0}, {}, {}, {}, {}
        for n, (k, g, name, eng, bank) in enumerate(plan):
            count[eng] += 1
            key = (k, g, name)
            filled[key], emptied[key], before[key] = n + 1, (eng, count[eng]), last_in.get(bank)
            last_in[bank] = key
        banks = {(k, g, name): bank for k, g, name, _, bank in plan}

        def empty(eng, key):
            who, n = emptied[key]
            eng.wait_ge(s.act if who == "act" else s.dve, n)

        ftile = lambda g, h: 2 * g + h // 2
        hb = lambda h: HD * (h % 2)
        MIX_Y = RKVQ[:, 2 * CT:3 * CT]

        @block.sync
        def _(sp):
            sp.dma_start(LNX[:, 0], t.lnx_g.to_broadcast([P, CW])).then_inc(s.rows_in, 16)
            sp.dma_start(LNX[:, 1], t.lnx_b.to_broadcast([P, CW])).then_inc(s.rows_in, 16)

        @block.tensor
        def _(pe):
            pe.wait_ge(s.init, 1)
            fences = [0]

            def fence(ins):
                fences[0] += 1
                ins.then_inc(s.order, 1)
                pe.wait_ge(s.order, fences[0])

            for k, g, name, eng, bank in plan:
                key = (k, g, name)
                if before[key] is not None:
                    empty(pe, before[key])
                B = PS[:, bank, :]
                B4 = B.rearrange("p (h c) -> p h c", h=HB)
                cols = slice(k * P, (k + 1) * P)
                v, nb, kn, q = (tok[:, g, i] for i in range(4))
                if name in ("TRa", "TRb"):
                    if k and name == "TRa":
                        pe.wait_ge(s.pool, k * 2)
                    for i in range(2):
                        for f in range(2):
                            src = (RKVQ[:, 2 * CT + 2 * g + f], A[:, 2 * g + f], RKVQ[:, CT + 2 * g + f],
                                   RKVQ[:, 3 * CT + 2 * g + f])[2 * (name == "TRb") + i]
                            last = pe.transpose(B[:, (2 * i + f) * P:(2 * i + f + 1) * P], src[:, cols],
                                                m.const("ident"))
                elif name in ("PBa", "PBb", "PGa", "PGb"):
                    for i in range(2):
                        h = 2 * i + (name[2] == "b")
                        f, b = ftile(g, h), hb(h)
                        left = A[b:b + HD, f, cols] if name[1] == "B" else RKVQ[b:b + HD, CT + f, cols]
                        last = pe.matmul(B[:, i * 2 * P:(i + 1) * 2 * P].rearrange("p (a c) -> p a c", a=2), left,
                                         RKVQ[b:b + HD, f:f + 3 * CT + 1:3 * CT, cols], start=True, stop=True)
                elif name == "N":
                    for h in (0, 2, 1, 3):
                        if h == 1:
                            fence(last)
                        f, b = ftile(g, h), hb(h)
                        last = pe.matmul(B4[:, h], RKVQ[b:b + HD, 3 * CT + f, cols], A[b:b + HD, f, cols],
                                         start=True, stop=True)
                elif name in ("SQ1a", "SQ1b", "AP1", "SQ2a", "SQ2b", "AP2", "SQ3", "AP3", "FR", "Z", "H1", "H2",
                              "H3"):
                    needs = {"SQ1a": ("N", "PBb"), "SQ1b": (), "AP1": ("SQ1a",), "SQ2a": ("SQ1b",), "SQ2b": (),
                             "AP2": ("SQ2a", "AP1"), "SQ3": ("SQ2b",), "AP3": ("SQ3", "AP2"), "FR": ("AP3",),
                             "Z": ("GV",), "H1": ("FR", "Z"), "H2": ("H1",), "H3": ("H2",)}[name]
                    for need in needs:
                        empty(pe, (k, g, need))
                    for h in range(HB):
                        left, right = {
                            "SQ1a": (BR[:, g, h, 1], ND[:, g, h]), "SQ1b": (ND[:, g, h], BR[:, g, h, 1]),
                            "AP1": (P2[:, g, 0, h], IB[:, g, h]),
                            "SQ2a": (P2[:, g, 1, h], P2[:, g, 0, h]), "SQ2b": (P2[:, g, 0, h], P2[:, g, 1, h]),
                            "AP2": (P4[:, g, 0, h], IB[:, g, h]), "SQ3": (P4[:, g, 1, h], P4[:, g, 0, h]),
                            "AP3": (P8[:, g, h], IB[:, g, h]), "FR": (NE[:, g, h], IB[:, g, h]),
                            "Z": (IB[:, g, h], XR[:, g, h]), "H1": (FR[:, g, h], ZZ[:, g, h]),
                            "H2": (FR[:, g, h], WU[:, g, h]), "H3": (FR[:, g, h], WU[:, g, h]),
                        }[name]
                        last = pe.matmul(B4[:, h], left, right, start=True, stop=True)
                elif name == "GV":
                    empty(pe, (k, g, "PGb"))
                    empty(pe, (k, g, "TRa"))
                    for h in range(HB):
                        last = pe.matmul(B[:, h * HD:(h + 1) * HD], GR[:, g, h, 1], v[:, h * HD:(h + 1) * HD],
                                         start=True, stop=True)
                elif name == "MT":
                    empty(pe, (k, g, "H3"))
                    for c in range(2):
                        if c:
                            fence(last)
                        for h in range(HB):
                            rows, b = slice(c * CH, (c + 1) * CH), hb(h)
                            last = pe.matmul(B[b:b + HD, (2 * (h // 2) + c) * HD:(2 * (h // 2) + c + 1) * HD],
                                             WU[rows, g, h, 0:HD], nb[rows, h * HD:(h + 1) * HD],
                                             start=True, stop=True)
                elif name == "ZT":
                    for h in range(HB):
                        b = hb(h)
                        last = pe.matmul(B[b:b + HD, (h // 2) * P:(h // 2 + 1) * P], WU[:, g, h, 0:HD],
                                         BR[:, g, h, 0], start=True, stop=True)
                elif name in ("S0", "S1"):
                    c = int(name[1])
                    if c == 0:
                        for gg in range(2):
                            empty(pe, (k, gg, "MT"))
                            empty(pe, (k, gg, "ZT"))
                    else:
                        empty(pe, (k, 0, "S0"))
                    if c == 0:
                        if before[(k, 0, "Y")] is not None:
                            empty(pe, before[(k, 0, "Y")])
                    rows = slice(c * CH, (c + 1) * CH)
                    every = [(gg, h) for gg in range(2) for h in range(HB)]
                    out = lambda gg, h: B[hb(h):hb(h) + HD, ftile(gg, h) * HD:(ftile(gg, h) + 1) * HD]
                    y_at = lambda gg, h: slice((4 * gg + h) * HD, (4 * gg + h + 1) * HD)
                    for gg, h in every:
                        hs = slice(h * HD, (h + 1) * HD)
                        pe.matmul(out(gg, h), tok[rows, gg, 2, hs], tok[rows, gg, 0, hs],
                                  start=gg == 0 and h < 2, stop=False, skip_group_check=True)
                        last = pe.matmul(out(gg, h), tok[rows, gg, 1, hs], WU[rows, gg, h, HD:P], start=False,
                                         stop=False, skip_group_check=True)
                    if c == 0:
                        for gg, h in every:
                            pe.matmul(PS[:, 6, y_at(gg, h)], GR[:, gg, h, 0], tok[:, gg, 0, h * HD:(h + 1) * HD],
                                      start=gg == 0 and h == 0, stop=False, skip_group_check=True)
                            last = pe.matmul(PS[:, 6, y_at(gg, h)], BR[:, gg, h, 0], WU[:, gg, h, HD:P],
                                             start=False, stop=False, skip_group_check=True)
                    for odd in range(2):
                        fence(last)
                        for gg, h in every:
                            if h % 2 == odd:
                                f, b = ftile(gg, h), hb(h)
                                pe.matmul(out(gg, h), MT[b:b + HD, gg, h // 2, c], S[b:b + HD, f], start=False,
                                          stop=True, skip_group_check=True)
                                last = pe.matmul(PS[rows, 6, y_at(gg, h)], ZT[b:b + HD, f, rows], S[b:b + HD, f],
                                                 start=False, stop=True, skip_group_check=True)
                elif name == "Y":
                    pe.sem_inc(s.pe, 1)
                    continue
                elif name == "GT":
                    if k:
                        pe.wait_ge(s.y_ready, k)
                    pe.matmul(B, LO[:, 1, cols], G2[:, 0], start=True, stop=False)
                    last = pe.matmul(B, LO[0:GLORA - P, 2, cols], G2[0:GLORA - P, 1], start=False, stop=True)
                elif name == "YT":
                    pe.wait_ge(s.y_ready, k + 1)
                    for q_ in range(CT):
                        last = pe.transpose(B[:, q_ * P:(q_ + 1) * P], Y[:, q_ * P:(q_ + 1) * P], m.const("ident"))
                last.then_inc(s.pe, 1)
                if name == "S1":
                    pe.wait_ge(s.pe, filled[key])

        @block.scalar
        def _(act):
            def square(k):
                act.wait_ge(s.squared, 2 * k + 1)
                nc.scalar.activation(Y2[:], Y[:], ACT.Square).then_inc(s.achain, 1)

            def root(k):
                act.wait_ge(s.squared, 2 * k + 2)
                nc.scalar.activation(st[:, 1], st[:, 1], ACT.Sqrt, scale=1.0 / HD, bias=m.small[:, 0:1]
                                     ).then_inc(s.achain, 1)

            def last_turn(step):
                k, g, name, eng, bank = step
                act.wait_ge(s.pe, filled[k, g, name])
                nc.scalar.copy(MIX_Y[:, :, k * P:(k + 1) * P], PS[:, bank, :].rearrange("p (q c) -> p q c", q=CT)
                               ).then_inc(s.act, 1)

            for k, g, name, eng, bank in plan[:-1]:
                if eng != "act":
                    continue
                key = (k, g, name)
                act.wait_ge(s.pe, filled[key])
                B = PS[:, bank, :]
                ins = None
                if name == "TRa":
                    ins = nc.scalar.copy(tok[:, g, 0:2].rearrange("p a c -> p (a c)"), B)
                elif name == "TRb":
                    ins = nc.scalar.copy(tok[:, g, 2:4].rearrange("p a c -> p (a c)"), B)
                elif name == "GV":
                    act.wait_ge(s.act, emptied[(k, g, "TRb")][1])
                    nc.scalar.copy(XR[:, g, :, 0:HD], tok[:, g, 3].rearrange("p (h c) -> p h c", h=HB))
                    ins = nc.scalar.copy(XR[:, g, :, HD:P], B[:, 0:HB * HD].rearrange("p (h c) -> p h c", h=HB))
                elif name == "GT":
                    ins = nc.scalar.copy(GT[:], B)
                elif name == "YT":
                    ins = nc.scalar.copy(MIX_Y[:, :, k * P:(k + 1) * P], B.rearrange("p (q c) -> p q c", q=CT))
                else:
                    out = {"SQ1b": P2[:, g, 1], "SQ2b": P4[:, g, 1], "SQ3": P8[:, g], "FR": FR[:, g],
                           "Z": ZZ[:, g]}[name]
                    ins = nc.scalar.copy(flat(out), B)
                ins.then_inc(s.act, 1)
                if (g, name) == (1, "TRb") and k:
                    square(k - 1)
                if (g, name) == (1, "SQ1b") and k:
                    root(k - 1)
            square(TT - 1)
            root(TT - 1)
            last_turn(plan[-1])

        @block.gpsimd
        def _(pool):
            for k in range(TT):
                if k >= 2:
                    pool.wait_ge(s.y_ready, k - 1)
                for g in range(2):
                    empty(pool, (k, g, "TRa"))
                    nc.gpsimd.tensor_tensor(
                        VB[:, k % 2, g * 2 * P:(g + 1) * 2 * P].rearrange("p (h c) -> p h c", h=HB),
                        tok[:, g, 0].rearrange("p (h c) -> p h c", h=HB),
                        bonus[:, k * RH + g * HB:k * RH + (g + 1) * HB].unsqueeze(2).to_broadcast([P, HB, HD]),
                        ALU.mult).then_inc(s.pool, 1)

        @block.vector
        def _(dve):
            do = Chain(dve, s.chain)
            v = nc.vector
            v.memset(m.small[:, 0:1], LNX_EPS).then_inc(s.eps, 1)
            v.memset(S[:], 0.0).then_inc(s.init, 1)
            dve.wait_ge(s.rows_in, 32)
            heads = lambda ap: ap.rearrange("p (h c) -> p h c", h=RH)
            wide = lambda ap: ap.unsqueeze(2).to_broadcast([P, RH, HD])

            def mask(name, n=1):
                at = CONSTS[name][0]
                return m.consts[:, at:at + n * P].unsqueeze(1).to_broadcast([P, HB // n, n * P])

            def y_variance(k):
                dve.wait_ge(s.achain, 2 * k + 1)
                v.tensor_reduce(st[:, 1], heads(Y2[:]), AX, ALU.add).then_inc(s.squared, 1)

            def y_normed(k):
                dve.wait_ge(s.achain, 2 * k + 2)
                do(v.reciprocal(st[:, 2], st[:, 1]))
                do(v.tensor_tensor(heads(Y[:]), heads(Y[:]), wide(st[:, 2]), ALU.mult))

            def y_gained(k):
                do(v.tensor_tensor(Y[:], Y[:], LNX[:, 0], ALU.mult))
                do(v.tensor_tensor(Y[:], Y[:], LNX[:, 1], ALU.add))

            def y_gated(k):
                dve.wait_ge(s.pool, 2 * k + 2)
                do(v.tensor_tensor(Y[:], Y[:], VB[:, k % 2], ALU.add))
                empty(dve, (k, 0, "GT"))
                v.tensor_tensor(Y[:], Y[:], GT[:], ALU.mult).then_inc(s.y_ready, 1)

            after = {"N": y_variance, "AP1": y_normed, "SQ2a": y_gained, "AP2": y_gated}

            for k, g, name, eng, bank in plan:
                if eng != "dve":
                    continue
                key = (k, g, name)
                dve.wait_ge(s.pe, filled[key])
                B = PS[:, bank, :]
                B4 = B.rearrange("p (h c) -> p h c", h=HB)
                B2 = B.rearrange("p (h c) -> p h c", h=2)
                cols = slice(k * P, (k + 1) * P)
                if name in ("PBa", "PBb"):
                    h = int(name[2] == "b")
                    ins = v.tensor_tensor(BR[:, g, h:HB:2].rearrange("p h a c -> p h (a c)"), B2,
                                          mask("mask_incl_up", 2), ALU.mult)
                elif name in ("PGa", "PGb"):
                    h = int(name[2] == "b")
                    ins = v.tensor_tensor(GR[:, g, h:HB:2].rearrange("p h a c -> p h (a c)"), B2,
                                          mask("mask_incl_up_2", 2), ALU.mult)
                elif name == "N":
                    dve.wait_ge(s.dve, emptied[(k, g, "PBb")][1])
                    v.tensor_tensor(IB[:, g], BR[:, g, :, 1], mask("ident"), ALU.add)
                    v.tensor_tensor(ND[:, g], B4, mask("mask_diag_low"), ALU.mult)
                    ins = v.tensor_tensor(NE[:, g], B4, mask("mask_off_low"), ALU.mult)
                elif name in ("SQ1a", "SQ2a"):
                    ins = v.tensor_copy(flat((P2 if name == "SQ1a" else P4)[:, g, 0]), B)
                elif name in ("AP1", "AP2", "AP3"):
                    ins = v.tensor_tensor(flat(IB[:, g]), flat(IB[:, g]), B, ALU.add)
                elif name in ("H1", "H2", "H3"):
                    ins = v.tensor_tensor(flat(WU[:, g]), flat(ZZ[:, g]), B, ALU.add)
                elif name == "MT":
                    at = CONSTS["ident_heads"][0]
                    ident = m.consts[:, at:at + HD].unsqueeze(1).to_broadcast([P, 4, HD])
                    ins = v.tensor_tensor(MT[:, g].rearrange("p f c j -> p (f c) j"),
                                          B[:, 0:4 * HD].rearrange("p (f j) -> p f j", f=4), ident, ALU.add)
                elif name == "ZT":
                    ins = v.tensor_tensor(ZT[:, 2 * g:2 * g + 2], B[:, 0:2 * P].rearrange("p (f c) -> p f c", f=2),
                                          RKVQ[:, 2 * g:2 * g + 2, cols], ALU.add)
                elif name in ("S0", "S1"):
                    c = int(name[1])
                    ins = v.tensor_tensor(S[:], B[:, 0:CT * HD].rearrange("p (f i) -> p f i", f=CT),
                                          PC[:, :, 2 * k + c].unsqueeze(2).to_broadcast([P, CT, HD]), ALU.mult)
                elif name == "Y":
                    if k:
                        dve.wait_ge(s.pe, filled[(k - 1, 0, "YT")])
                    do(v.tensor_reduce(st[:, 0], heads(B), AX, ALU.add))
                    do(v.tensor_scalar(st[:, 0], st[:, 0], 1.0 / HD, None, ALU.mult))
                    ins = v.tensor_tensor(heads(Y[:]), heads(B), wide(st[:, 0]), ALU.subtract)
                ins.then_inc(s.dve, 1)
                if name == "Y":
                    dve.wait_ge(s.dve, emptied[key][1])
                    v.sem_inc(s.squared, 1)
                if g == 1 and k and name in after:
                    after[name](k - 1)
            for part in (y_variance, y_normed, y_gained, y_gated):
                part(TT - 1)


def out_projection(m, tiles, w, GM, X, dst):
    nc, t, PS = m.nc, m.t, m.PS
    with ExitStack() as ctx:
        W = alloc(m, ctx, "w_out", [P, KT, D])
        tmp = alloc(m, ctx, "scaled", [P, 2, D])
        junk = alloc(m, ctx, "junk", [P, D])
        s = phase(m, "w_in0 w_in1 x_in eps prod rooted ps_free chain done stored")
        block = ctx.enter_context(nc.Block())
        ss, rstd, eps = m.small[:, 0:TT], m.small[:, TT:2 * TT], m.small[:, 2 * TT:2 * TT + 1]

        @block.sync
        def _(sp):
            for half, sem in enumerate((s.w_in0, s.w_in1)):
                cols = slice(half * NH, (half + 1) * NH)
                sp.dma_start(W[:, :, cols], w[:, cols].rearrange("(k p) n -> p k n", p=P)).then_inc(sem, 16)
            sp.dma_start(X[:], t.x.rearrange("(k p) n -> p k n", p=P)).then_inc(s.x_in, 16)
            for k in range(TT):
                sp.wait_ge(s.done, 2 * k + 2)
                sp.dma_start(dst[k * P:(k + 1) * P], X[:, k]).then_inc(s.stored, 16)
            sp.wait_ge(s.stored, 16 * TT)

        @block.tensor
        def _(pe):
            for k in range(TT):
                if k >= 4:
                    pe.wait_ge(s.ps_free, k - 3)
                for half in range(2):
                    if k == 0:
                        pe.wait_ge(s.w_in1 if half else s.w_in0, 16)
                    for q in range(KT):
                        last = pe.matmul(PS[:, 2 * (k % 4) + half, :], tiles[q][:, k * P:(k + 1) * P],
                                         W[:, q, half * NH:(half + 1) * NH], start=q == 0, stop=q == KT - 1)
                last.then_inc(s.prod, 1)

        @block.scalar
        def _(act):
            act.wait_ge(s.eps, 1)
            for k in range(TT):
                act.wait_ge(s.prod, k + 1)
                nc.scalar.activation(junk[:], bank2(m, k % 4), ACT.Square, accum_out=ss[:, k:k + 1]
                                     ).then_inc(s.chain, 1)
                act.wait_ge(s.chain, k + 1)
                nc.scalar.activation(rstd[:, k:k + 1], ss[:, k:k + 1], ACT.Sqrt, scale=1.0 / D, bias=eps
                                     ).then_inc(s.rooted, 1)

        @block.vector
        def _(dve):
            v = nc.vector
            v.memset(eps, RMS_EPS).then_inc(s.eps, 1)
            dve.wait_ge(s.x_in, 16)
            for k in range(TT):
                dve.wait_ge(s.rooted, k + 1)
                v.reciprocal(rstd[:, k:k + 1], rstd[:, k:k + 1]).then_inc(s.done, 1)
                dve.wait_ge(s.done, 2 * k + 1)
                v.scalar_tensor_tensor(out=tmp[:, k % 2], in0=bank2(m, k % 4), scalar=rstd[:, k:k + 1],
                                       in1=GM, op0=ALU.mult, op1=ALU.mult).then_inc(s.ps_free, 1)
                dve.wait_ge(s.ps_free, k + 1)
                v.tensor_tensor(X[:, k], X[:, k], tmp[:, k % 2], ALU.add).then_inc(s.done, 1)


def up_projection(m, MID, HH, HL, h):
    nc, t, PS = m.nc, m.t, m.PS
    with ExitStack() as ctx:
        RAW = alloc(m, ctx, "up_raw", [P, 2, KT, P])
        WH = alloc(m, ctx, "up_high", [P, 2, KT, P], F32R)
        WL = alloc(m, ctx, "up_low", [P, 2, KT, P], F32R)
        Z = alloc(m, ctx, "z", [P, 2, T])
        s = phase(m, "raw0 raw1 raw_free ready high split tile_done ps_free tap2 chain silu mid")
        raw_in = [s.raw0, s.raw1]
        block = ctx.enter_context(nc.Block())
        col = lambda name, at: m.cols[:, bass.ds(at + COLS[name][0], 1)]

        @block.sync
        def _(sp):
            h.sync(sp)
            sp.sem_inc(s.raw_free, 2)
            with sp.Fori(0, FT // 2) as i:
                at = [[sp.snap(i * 2 * P + j * P + c * D_FF) for c in range(2)] for j in range(2)]
                for j in range(2):
                    for c in range(2):
                        sp.wait_ge(s.raw_free, i * 4 + 2 * j + c + 1)
                        sp.dma_start(RAW[:, c], t.w_up[:, bass.ds(at[j][c], P)].rearrange("(k p) n -> p k n", p=P)
                                     ).then_inc(raw_in[c], 16)

        @block.gpsimd
        def _(pool):
            h.gpsimd(pool, range(2 * KT))
            with pool.Fori(0, FT // 2) as i:
                for j in range(2):
                    for c in range(2):
                        pool.wait_ge(raw_in[c], i * 32 + 16 * j + 16)
                        pool.wait_ge(s.tile_done, i * 4 + 2 * j + c + 1)
                        pool.sem_inc(s.ready, 1)
                        nc.gpsimd.tensor_copy(WH[:, c], RAW[:, c]).then_inc(s.high, 1)
                        pool.wait_ge(s.high, i * 4 + 2 * j + c + 1)
                        nc.gpsimd.tensor_tensor(WL[:, c], RAW[:, c], WH[:, c], ALU.subtract).then_inc(s.split, 1)
                        pool.wait_ge(s.split, i * 4 + 2 * j + c + 1)
                        pool.sem_inc(s.raw_free, 1)

        @block.tensor
        def _(pe):
            h.tensor(pe)
            pe.sem_inc(s.tile_done, 2)
            with pe.Fori(0, FT // 2) as i:
                for j in range(2):
                    for c in range(2):
                        n = 2 * j + c
                        pe.wait_ge(s.split, i * 4 + n + 1)
                        pe.wait_ge(s.ps_free, i * 4 + n + 1)
                        half_product(m, pe, WH[:, c], WL[:, c], HH, HL, 2 * n, 0)
                        half_product(m, pe, WH[:, c], WL[:, c], HH, HL, 2 * n + 1, 1).then_inc(s.tile_done, 1)

        @block.scalar
        def _(act):
            h.scalar(act)
            with act.Fori(0, FT // 2) as i:
                for j in range(2):
                    act.wait_ge(s.mid, i * 2 + j + 1)
                    for c in range(2):
                        ch = i * 2 + (j + c * FT)
                        act.wait_ge(s.tile_done, i * 4 + 2 * j + c + 1 + 2)
                        nc.scalar.activation(Z[:, c], bank2(m, 2 * j + c), ACT.Identity,
                                             scale=col("ffn_w", i * 6 + (j + c * FT) * 3 + 2), bias=col("ffn_b", ch)
                                             ).then_inc(s.tap2, 1)
                    act.wait_ge(s.ps_free, i * 4 + 2 * j + 1 + 4)
                    nc.scalar.activation(Z[:, 0], Z[:, 0], ACT.Silu).then_inc(s.silu, 1)

        @block.vector
        def _(dve):
            v = nc.vector
            h.vector(dve)
            dve.sem_inc(s.ps_free, 4)
            dve.sem_inc(s.mid, 1)
            with dve.Fori(0, FT // 2) as i:
                for j in range(2):
                    for c in range(2):
                        n = 2 * j + c
                        dve.wait_ge(s.tap2, i * 4 + n + 1)
                        for tap in (1, 2):
                            z = Z[:, c, tap:T]
                            ins = v.scalar_tensor_tensor(out=z, in0=bank2(m, n)[:, 0:T - tap],
                                                         scalar=col("ffn_w", i * 6 + (j + c * FT) * 3 + 2 - tap),
                                                         in1=z, op0=ALU.mult, op1=ALU.add)
                            if tap == 1:
                                ins.then_inc(s.chain, 1)
                                dve.wait_ge(s.chain, i * 4 + n + 1)
                        ins.then_inc(s.ps_free, 1)
                    dve.wait_ge(s.silu, i * 2 + j + 1)
                    dve.wait_ge(s.ps_free, i * 4 + 2 * j + 2 + 4)
                    v.tensor_tensor(MID[:, bass.ds(i * 2 + j, 1), :].rearrange("p a b -> p (a b)"), Z[:, 0],
                                    Z[:, 1], ALU.mult).then_inc(s.mid, 1)


def down_projection(m, MID, GM, src, dst):
    nc, t, PS = m.nc, m.t, m.PS
    with ExitStack() as ctx:
        F = alloc(m, ctx, "f", [P, TT, D])
        X = alloc(m, ctx, "x_tokens", [P, TT, D])
        MH = alloc(m, ctx, "mid_high", [P, 2, T], F32R)
        ML = alloc(m, ctx, "mid_low", [P, 2, T], F32R)
        RAW = alloc(m, ctx, "down_raw", [P, 2, NH])
        WH = alloc(m, ctx, "down_high", [P, 2, NH], F32R)
        WL = alloc(m, ctx, "down_low", [P, 2, NH], F32R)
        s = phase(m, "raw0 raw1 x_in high low whigh split used prod moved eps sq rooted chain scaled out stored")
        raw_in = [s.raw0, s.raw1]
        block = ctx.enter_context(nc.Block())
        ss, rstd, eps = m.small[:, 0:2 * TT], m.small[:, 2 * TT:3 * TT], m.small[:, 3 * TT:3 * TT + 1]
        steps = [(half, q) for half in range(2) for q in range(FT)]

        @block.sync
        def _(sp):
            for i, (half, q) in enumerate(steps):
                if i >= 2:
                    sp.wait_ge(s.split, i - 1)
                sp.dma_start(RAW[:, i % 2], t.w_down[q * P:(q + 1) * P, half * NH:(half + 1) * NH]
                             ).then_inc(raw_in[i % 2], 16)
                if i == FT // 2:
                    sp.dma_start(X[:], src.rearrange("(k p) n -> p k n", p=P)).then_inc(s.x_in, 16)
            for k in range(TT):
                sp.wait_ge(s.out, k + 1)
                sp.dma_start(dst[k * P:(k + 1) * P], X[:, k]).then_inc(s.stored, 16)
            sp.wait_ge(s.stored, 16 * TT)

        @block.gpsimd
        def _(pool):
            for i in range(len(steps)):
                pool.wait_ge(raw_in[i % 2], 16 * (i // 2 + 1))
                if i >= 2:
                    pool.wait_ge(s.used, i - 1)
                nc.gpsimd.tensor_copy(WH[:, i % 2], RAW[:, i % 2]).then_inc(s.whigh, 1)
                pool.wait_ge(s.whigh, i + 1)
                nc.gpsimd.tensor_tensor(WL[:, i % 2], RAW[:, i % 2], WH[:, i % 2], ALU.subtract).then_inc(s.split, 1)
            pool.wait_ge(s.x_in, 16)
            for k in range(TT):
                pool.wait_ge(s.scaled, k + 1)
                nc.gpsimd.tensor_tensor(X[:, k], X[:, k], F[:, k], ALU.add).then_inc(s.out, 1)

        @block.tensor
        def _(pe):
            for i, (half, q) in enumerate(steps):
                pe.wait_ge(s.split, i + 1)
                pe.wait_ge(s.low, i + 1)
                for k in range(TT):
                    if q == 0 and half:
                        pe.wait_ge(s.moved, k + 1)
                    cols = slice(k * P, (k + 1) * P)
                    for a, b in ((MH, WH), (MH, WL), (ML, WH)):
                        last = pe.matmul(PS[:, k, :], a[:, i % 2, cols], b[:, i % 2],
                                         start=q == 0 and a is MH and b is WH, stop=q == FT - 1 and a is ML)
                    if q == FT - 1:
                        last.then_inc(s.prod, 1)
                if q < FT - 1:
                    last.then_inc(s.used, 1)
                else:
                    pe.wait_ge(s.prod, TT * (half + 1))
                    pe.sem_inc(s.used, 1)

        @block.scalar
        def _(act):
            act.wait_ge(s.eps, 1)

            def move(half):
                for k in range(TT):
                    f = F[:, k, half * NH:(half + 1) * NH]
                    act.wait_ge(s.prod, half * TT + k + 1)
                    nc.scalar.copy(f, PS[:, k, :]).then_inc(s.moved, 1)

            for i, (half, q) in enumerate(steps):
                if i == FT:
                    move(0)
                if i >= 2:
                    act.wait_ge(s.used, i - 1)
                nc.scalar.copy(MH[:, i % 2], MID[:, q]).then_inc(s.high, 1)
            move(1)
            for k in range(TT):
                act.wait_ge(s.moved, TT + k + 1)
                if k >= 2:
                    act.wait_ge(s.sq, k - 1)
                nc.scalar.activation(MH[:, k % 2], F[:, k], ACT.Square, accum_out=ss[:, k:k + 1]).then_inc(s.sq, 1)
                act.wait_ge(s.sq, k + 1)
                nc.scalar.activation(rstd[:, k:k + 1], ss[:, k:k + 1], ACT.Sqrt, scale=1.0 / D, bias=eps
                                     ).then_inc(s.rooted, 1)

        @block.vector
        def _(dve):
            do = Chain(dve, s.chain)
            v = nc.vector
            v.memset(eps, RMS_EPS).then_inc(s.eps, 1)
            for i, (half, q) in enumerate(steps):
                dve.wait_ge(s.high, i + 1)
                v.tensor_tensor(ML[:, i % 2], MID[:, q], MH[:, i % 2], ALU.subtract).then_inc(s.low, 1)
            for k in range(TT):
                dve.wait_ge(s.rooted, k + 1)
                do(v.reciprocal(rstd[:, k:k + 1], rstd[:, k:k + 1]))
                v.scalar_tensor_tensor(out=F[:, k], in0=F[:, k], scalar=rstd[:, k:k + 1], in1=GM,
                                       op0=ALU.mult, op1=ALU.mult).then_inc(s.scaled, 1)


class TurnedIn:

    def __init__(self, m, src, HH, HL):
        self.m, self.src, self.HH, self.HL = m, src, HH, HL
        self.s = s = phase(m, "in0 in1 in2 in3 in4 in5 in6 in7 turned high low")
        self.x_in = [s.in0, s.in1, s.in2, s.in3, s.in4, s.in5, s.in6, s.in7]

    def at(self, n):
        return slice(None), n % KT, slice(n // KT * NH, (n // KT + 1) * NH)

    def sync(self, sp):
        for k in range(TT if self.src is not None else 0):
            sp.dma_start(self.m.HT[:, k], self.src[k * P:(k + 1) * P]).then_inc(self.x_in[k], 16)

    def tensor(self, pe):
        m, s = self.m, self.s
        for n in range(2 * KT):
            half, k = n // KT, n % KT
            if k == 0 and self.src is not None:
                for j in range(4):
                    pe.wait_ge(self.x_in[4 * half + j], 16)
            if half:
                pe.wait_ge(s.low, k + 1)
            for j in range(4):
                last = pe.transpose(m.PS[:, k, j * P:(j + 1) * P], m.HT[:, 4 * half + j, k * P:(k + 1) * P],
                                    m.const("ident"))
            last.then_inc(s.turned, 1)
        pe.wait_ge(s.low, 2 * KT)

    def scalar(self, act):
        for n in range(2 * KT):
            act.wait_ge(self.s.turned, n + 1)
            self.m.nc.scalar.copy(self.HH[self.at(n)], self.m.PS[:, n % KT, :]).then_inc(self.s.high, 1)

    def vector(self, dve):
        for n in range(2 * KT):
            dve.wait_ge(self.s.high, n + 1)
            self.m.nc.vector.tensor_tensor(self.HL[self.at(n)], self.m.PS[:, n % KT, :], self.HH[self.at(n)],
                                           ALU.subtract).then_inc(self.s.low, 1)


class StepSizes:

    def __init__(self, m, ctx, dt_bias, a_log, DT, NA, EI, DE, CD, DA):
        self.m, self.dt_bias, self.a_log = m, dt_bias, a_log
        self.DT, self.NA, self.EI, self.DE, self.CD, self.DA = DT, NA, EI, DE, CD, DA
        self.rows = alloc(m, ctx, "dt_rows", [P, 2, SH])
        self.tmp = alloc(m, ctx, "dt_tmp", [P, 5, TT * SH])
        self.s = phase(m, "par_in ab e chain sums acs last ex")
        self.sums, self.ends = m.PS[:, 0, 0:TT * SH], m.PS[:, 2, 0:TT * SH]

    def sync(self, sp):
        sp.dma_start(self.rows[:, 0], self.dt_bias.to_broadcast([P, SH])).then_inc(self.s.par_in, 16)
        sp.dma_start(self.rows[:, 1], self.a_log.to_broadcast([P, SH])).then_inc(self.s.par_in, 16)

    def scalar_raw(self, act):
        s, nc = self.s, self.m.nc
        act.wait_ge(s.par_in, 32)
        nc.scalar.activation(self.rows[:, 1], self.rows[:, 1], ACT.Exp).then_inc(s.e, 1)
        act.wait_ge(s.ab, 1)
        nc.scalar.activation(self.tmp[:, 0], self.DT[:], ACT.Abs).then_inc(s.e, 1)
        act.wait_ge(s.e, 2)
        nc.scalar.activation(self.tmp[:, 1], self.tmp[:, 0], ACT.Exp, scale=-1.0).then_inc(s.e, 1)

    def scalar_sums(self, act):
        s, nc = self.s, self.m.nc
        act.wait_ge(s.sums, 1)
        nc.scalar.activation(self.EI[:], self.sums, ACT.Exp).then_inc(s.ex, 1)
        nc.scalar.mul(self.NA[:], self.sums, -1.0).then_inc(s.acs, 1)

    def scalar_ends(self, act):
        s, nc = self.s, self.m.nc
        act.wait_ge(s.last, 1)
        nc.scalar.activation(self.CD[:], self.ends, ACT.Exp).then_inc(s.ex, 1)
        act.wait_ge(s.ex, 3)
        nc.scalar.activation(self.DE[:], self.DE[:], ACT.Exp)

    def vector(self, dve):
        s, v = self.s, self.m.nc.vector
        do = Chain(dve, s.chain)
        ax, e, sv, z, poly = (self.tmp[:, i] for i in range(5))
        by_head = lambda ap: ap.rearrange("p (c h) -> p c h", h=SH)
        every = lambda row: row.unsqueeze(1).to_broadcast([P, TT, SH])
        dve.wait_ge(s.par_in, 32)
        v.tensor_tensor(by_head(self.DT[:]), by_head(self.DT[:]), every(self.rows[:, 0]), ALU.add).then_inc(s.ab, 1)
        dve.wait_ge(s.e, 3)
        do(v.tensor_scalar(sv, e, 2.0, None, ALU.add))
        do(v.reciprocal(sv, sv))
        do(v.tensor_tensor(sv, sv, e, ALU.mult))
        do(v.tensor_tensor(z, sv, sv, ALU.mult))
        do(v.tensor_scalar(poly, z, 2.0 / 17, 2.0 / 15, ALU.mult, ALU.add))
        for n in range(13, 0, -2):
            do(v.tensor_tensor(poly, poly, z, ALU.mult))
            do(v.tensor_scalar(poly, poly, 2.0 / n, None, ALU.add))
        do(v.tensor_tensor(poly, poly, sv, ALU.mult))
        do(v.scalar_tensor_tensor(out=self.DT[:], in0=self.DT[:], scalar=0.0, in1=poly, op0=ALU.max, op1=ALU.add))
        do(v.scalar_tensor_tensor(out=by_head(self.DA[:]), in0=by_head(self.DT[:]), scalar=-1.0,
                                  in1=every(self.rows[:, 1]), op0=ALU.mult, op1=ALU.mult))
        dve.wait_ge(s.acs, 1)
        dve.wait_ge(s.last, 1)
        dve.wait_ge(s.ex, 2)
        v.tensor_tensor(self.DE[:], self.ends, self.NA[:], ALU.add).then_inc(s.ex, 1)

    def tensor_sums(self, pe):
        pe.wait_ge(self.s.chain, 5 + 2 * 7 + 3)
        pe.matmul(self.sums, self.m.const("tri"), self.DA[:], start=True, stop=True).then_inc(self.s.sums, 1)

    def tensor_ends(self, pe):
        pe.wait_ge(self.s.acs, 1)
        pe.matmul(self.ends, self.m.const("minus_last"), self.NA[:], start=True, stop=True).then_inc(self.s.last, 1)


def projections_and_attention(m, layer, w, sinks, HH, HL, x, step, attn_d, xbc_d, gate_d):
    nc, t, PS = m.nc, m.t, m.PS
    G4 = 4
    with ExitStack() as ctx:
        KH = alloc(m, ctx, "k", [P, 4, T])
        V = alloc(m, ctx, "v", [P, TT, KVW])
        RAW = alloc(m, ctx, "w_raw", [P, 3, KT, P])
        WH = alloc(m, ctx, "w_high", [P, 2, KT, P], F32R)
        WL = alloc(m, ctx, "w_low", [P, 2, KT, P], F32R)
        ST = alloc(m, ctx, "staged", [P, 2, T])
        BIAS = alloc(m, ctx, "alibi", [P, 2, G4, 2 * P])
        SC = alloc(m, ctx, "scores", [P, 2, G4, 2 * P])
        PT = alloc(m, ctx, "probs_turned", [P, 2, 2, G4 * P])
        SK = alloc(m, ctx, "sinks", [P, QH])
        MX, NM, DN, ES, RD = (alloc(m, ctx, n, [P, 2, G4]) for n in (
            "maxima", "minus_max", "sums", "sink_terms", "inverse_sums"))
        QT = m.HT[:, 0:4]
        AT = m.HT[:, 4:8]
        s = phase(m, "raw0 raw1 raw2 split wchain tile act_free dve_free tap silu stage0 stage1 bias0 bias1 sink_in "
                     "swapped scored biased neg exps rden chain probs turned moved0 moved1 outed gated "
                     "stored small small_free")
        raw_in, stage, bias_in = [s.raw0, s.raw1, s.raw2], [s.stage0, s.stage1], [s.bias0, s.bias1]
        block = ctx.enter_context(nc.Block())

        units = [(g, nb) for g in range(KVH) for nb in range(TT)]
        N = len(units)
        lo = lambda nb: P if nb == 0 else 0

        first = [("k", 0), ("k", 1), ("v", 0), ("v", 1), ("dt", 0), ("q", 0), ("q", 1), ("za", 0), ("za", 1)]
        rest = [("xbc", i) for i in range(XT)] + [("zs", i) for i in range(KT)]
        beside = []
        for g in range(KVH):
            ahead = [] if g == KVH - 1 else [("q", 2 * g + 2), ("q", 2 * g + 3), ("za", 2 * g + 2), ("za", 2 * g + 3)]
            beside += ahead + rest[:TT - len(ahead)]
            rest = rest[TT - len(ahead):]
        jobs = first + beside
        F = len(first)
        where = {job: n for n, job in enumerate(jobs)}
        column = {"q": O_Q, "k": O_K, "v": O_V, "za": O_ZA, "zs": O_ZS, "xbc": O_XBC, "dt": IN_W - P}
        staged = [job for job in jobs if job[0] in ("v", "dt", "xbc", "zs")]
        slot = {job: j % 2 for j, job in enumerate(staged)}
        before = {job: sum(o[0] in ("xbc", "zs") for o in staged[:j] if slot[o] == slot[job])
                  for j, job in enumerate(staged)}
        dve_jobs = [job for job in jobs if job[0] == "xbc"]
        act_jobs = [job for job in jobs if job[0] != "xbc"]

        def free(eng, n):
            if jobs[n][0] == "xbc":
                eng.wait_ge(s.dve_free, dve_jobs.index(jobs[n]) + 1)
            else:
                eng.wait_ge(s.act_free, act_jobs.index(jobs[n]) + 1)

        pair = lambda n: 2 + n % 2

        @block.sync
        def _(sp):
            x.sync(sp)
            step.sync(sp)
            sp.dma_start(SK[:], sinks.to_broadcast([P, QH])).then_inc(s.sink_in, 16)
            for n, (kind, i) in enumerate(jobs):
                if n >= 3:
                    sp.wait_ge(s.split, n - 2)
                at = column[kind] + i * P
                sp.dma_start(RAW[:, n % 3], w[:, at:at + P].rearrange("(k p) n -> p k n", p=P)
                             ).then_inc(raw_in[n % 3], 16)
                if n == 4:
                    free(sp, where["k", 1])
                    sp.dma_start(KH[0:HD, 2:4], KH[HD:P, 0:2]).then_inc(s.swapped, 16)
                    sp.dma_start(KH[HD:P, 2:4], KH[0:HD, 0:2]).then_inc(s.swapped, 16)
                if n >= 5 and (n - 5) % TT == 0 and (n - 5) // TT < KVH:
                    g = (n - 5) // TT
                    if g >= 2:
                        sp.wait_ge(s.biased, TT * (g - 1))
                    sp.dma_start(BIAS[:, g % 2], t.alibi[:, G4 * g:G4 * g + G4]).then_inc(bias_in[g % 2], 16)

        @block.tensor
        def _(pe):
            def half_tile(n, half):
                if half == 0:
                    pe.wait_ge(s.split, n + 1)
                    if n >= 2:
                        free(pe, n - 2)
                bank = 2 * pair(n) + half
                cols = slice(half * NH, (half + 1) * NH)
                for k in range(KT):
                    for a, b in ((WH, HH), (WH, HL), (WL, HH)):
                        last = pe.matmul(PS[:, bank, :], a[:, n % 2, k], b[:, k, cols],
                                         start=k == 0 and a is WH and b is HH, stop=k == KT - 1 and a is WL)
                if half:
                    last.then_inc(s.tile, 1)

            def scores(u):
                g, nb = units[u]
                if u >= 2:
                    pe.wait_ge(s.gated, u - 1)
                if u == 1:
                    pe.wait_ge(step.s.ex, 3)
                if nb == 0:
                    free(pe, where["q", 2 * g + 1])
                for i in range(G4):
                    at, b = (i // 2) * 2 * P, HD * (i % 2)
                    last = pe.matmul(PS[:, 2 * (u % 2) + i % 2, at + lo(nb):at + 2 * P],
                                     QT[b:b + HD, 2 * (g % 2) + i // 2, nb * P:(nb + 1) * P],
                                     KH[b:b + HD, g // 2 + (2 if i % 2 != g % 2 else 0),
                                        (nb - 1) * P + lo(nb):(nb + 1) * P], start=True, stop=True)
                last.then_inc(s.scored, 1)

            def turn(u):
                g, nb = units[u]
                pe.wait_ge(s.probs, u + 1)
                for a in range(2):
                    if a == 0 and nb == 0:
                        pe.sem_inc(s.turned, 1)
                        continue
                    for i in range(G4):
                        at = ((i % 2) * 2 + i // 2) * P
                        last = pe.transpose(PS[:, 2 * (u % 2) + a, at:at + P], SC[:, u % 2, i, a * P:(a + 1) * P],
                                            m.const("ident"))
                    last.then_inc(s.turned, 1)

            def out(u):
                g, nb = units[u]
                pe.wait_ge(s.moved0, u + 1)
                pe.wait_ge(s.moved1, u + 1)
                for odd in range(2):
                    for a in range(1 if nb == 0 else 0, 2):
                        last = pe.matmul(PS[odd * HD:(odd + 1) * HD, 2 * (u % 2), 0:2 * P],
                                         V[:, nb - 1 + a, g * HD:(g + 1) * HD],
                                         PT[:, u % 2, a, odd * 2 * P:(odd + 1) * 2 * P],
                                         start=a == 0 or nb == 0, stop=a == 1)
                last.then_inc(s.outed, 1)

            x.tensor(pe)
            for n, job in enumerate(first):
                half_tile(n, 0)
                half_tile(n, 1)
                if job[0] == "dt":
                    free(pe, where["v", 1])
                    for l in range(TT):
                        for c in range(2):
                            last = pe.transpose(PS[:, l // 2, (l % 2) * KVW + c * P:(l % 2) * KVW + (c + 1) * P],
                                                ST[:, slot["v", c], l * P:(l + 1) * P], m.const("ident"))
                    last.then_inc(s.small, 1)
                if job == ("q", 0):
                    free(pe, where["dt", 0])
                    pe.wait_ge(s.small_free, 1)
                    for l in range(TT):
                        last = pe.transpose(PS[:, l // 4, (l % 4) * P:(l % 4 + 1) * P],
                                            ST[:, slot["dt", 0], l * P:(l + 1) * P], m.const("ident"))
                    last.then_inc(s.small, 1)
                if job == ("za", 0):
                    pe.wait_ge(s.small_free, 2)
                    step.tensor_sums(pe)
            step.tensor_ends(pe)
            pe.wait_ge(s.swapped, 32)
            scores(0)
            for u in range(N):
                if u:
                    turn(u - 1)
                half_tile(F + u, 0)
                if u:
                    out(u - 1)
                half_tile(F + u, 1)
                if u + 1 < N:
                    scores(u + 1)
            turn(N - 1)
            out(N - 1)

        @block.gpsimd
        def _(pool):
            def split(n):
                pool.wait_ge(raw_in[n % 3], 16 * (n // 3 + 1))
                if n >= 2:
                    pool.wait_ge(s.tile, n - 1)
                nc.gpsimd.tensor_copy(WH[:, n % 2], RAW[:, n % 3]).then_inc(s.wchain, 1)
                pool.wait_ge(s.wchain, n + 1)
                nc.gpsimd.tensor_tensor(WL[:, n % 2], RAW[:, n % 3], WH[:, n % 2], ALU.subtract).then_inc(s.split, 1)

            for n in range(F + 1):
                split(n)
            for u in range(N):
                g, nb = units[u]
                if F + u + 1 < len(jobs):
                    split(F + u + 1)
                pool.wait_ge(s.rden, u + 1)
                p = SC[:, u % 2, :, lo(nb):2 * P]
                nc.gpsimd.tensor_tensor(p, p, RD[:, u % 2].unsqueeze(2).to_broadcast([P, G4, 2 * P - lo(nb)]),
                                        ALU.mult).then_inc(s.probs, 1)

        @block.scalar
        def _(act):
            def store(job):
                dst = (xbc_d if job[0] == "xbc" else gate_d)[job[1]]
                act.dma_start(dst, ST[:, slot[job]]).then_inc(stage[slot[job]], 16)

            def store_attention(g):
                act.wait_ge(s.gated, TT * (g + 1))
                act.dma_start(attn_d[2 * g:2 * g + 2].rearrange("k p t -> p k t"),
                              AT[:, 2 * (g % 2):2 * (g % 2) + 2]).then_inc(s.stored, 16)

            silus = [0]

            def evacuate(n):
                kind, i = jobs[n]
                act.wait_ge(s.tile, n + 1)
                src = bank2(m, pair(n))
                if kind in ("v", "dt", "xbc", "zs"):
                    st = ST[:, slot[kind, i]]
                    if before[kind, i]:
                        act.wait_ge(stage[slot[kind, i]], 16 * before[kind, i])
                    elif kind in ("dt", "xbc", "zs"):
                        act.wait_ge(s.small, 1 if kind == "dt" else 2)
                if kind == "k":
                    nc.scalar.copy(KH[:, i], src).then_inc(s.act_free, 1)
                elif kind == "q":
                    g = i // 2
                    if g >= 2:
                        act.wait_ge(s.scored, TT * (g - 1))
                    nc.scalar.copy(QT[:, i % 4], src).then_inc(s.act_free, 1)
                elif kind == "za":
                    g = i // 2
                    if g >= 2:
                        act.wait_ge(s.stored, 16 * (g - 1))
                    nc.scalar.activation(AT[:, i % 4], src, ACT.Silu).then_inc(s.act_free, 1)
                elif kind in ("v", "dt"):
                    nc.scalar.copy(st, src).then_inc(s.act_free, 1)
                elif kind == "zs":
                    nc.scalar.activation(st, src, ACT.Silu).then_inc(s.act_free, 1)
                    act.wait_ge(s.act_free, act_jobs.index((kind, i)) + 1)
                    store((kind, i))
                else:
                    ch = layer * XT + i
                    nc.scalar.activation(st, src, ACT.Identity, bias=m.col("conv_b_2", ch),
                                         scale=m.col("conv_w_2", ch * CK2 + CK2 - 1)).then_inc(s.tap, 1)

            def finish(n):
                job = jobs[n]
                if job[0] == "xbc":
                    act.wait_ge(s.dve_free, dve_jobs.index(job) + 1)
                    nc.scalar.activation(ST[:, slot[job]], ST[:, slot[job]], ACT.Silu).then_inc(s.silu, 1)
                    silus[0] += 1
                    act.wait_ge(s.silu, silus[0])
                    store(job)

            def exps(u):
                g, nb = units[u]
                act.wait_ge(s.neg, u + 1)
                nc.scalar.activation(ES[:, u % 2], ES[:, u % 2], ACT.Exp).then_inc(s.exps, 1)
                for i in range(G4):
                    p = SC[:, u % 2, i, lo(nb):2 * P]
                    nc.scalar.activation(p, p, ACT.Exp, bias=NM[:, u % 2, i:i + 1],
                                         accum_out=DN[:, u % 2, i:i + 1]).then_inc(s.exps, 1)

            def move0(u):
                if units[u][1] == 0:
                    act.sem_inc(s.moved0, 1)
                    return
                act.wait_ge(s.turned, 2 * u + 1)
                if u >= 2:
                    act.wait_ge(s.outed, u - 1)
                nc.scalar.copy(PT[:, u % 2, 0], PS[:, 2 * (u % 2), :]).then_inc(s.moved0, 1)

            x.scalar(act)
            for n in range(F - 1):
                evacuate(n)
                if jobs[n] == ("dt", 0):
                    act.wait_ge(s.small, 1)
                    nc.scalar.copy(V[:], PS[:, 0:4, :].rearrange("p a b -> p (a b)").rearrange(
                        "p (l c) -> p l c", l=TT)).then_inc(s.small_free, 1)
                if jobs[n] == ("q", 0):
                    act.wait_ge(s.small, 2)
                    nc.scalar.copy(step.DT[:].rearrange("p (l h) -> p l h", l=TT), PS[:, 0:2, :].rearrange(
                        "p a (b c) -> p (a b) c", b=4)[:, :, P - SH:P]).then_inc(s.small_free, 1)
                    step.scalar_raw(act)
                if jobs[n] == ("za", 0):
                    step.scalar_sums(act)
            step.scalar_ends(act)
            for u in range(N + 1):
                if u:
                    move0(u - 1)
                if u < N:
                    exps(u)
                evacuate(F + u - 1)
                if u:
                    finish(F + u - 2)
                if u > 1 and u % TT == 1:
                    store_attention(u // TT - 1)
            store_attention(KVH - 1)
            act.wait_ge(s.stored, 16 * KVH)
            act.wait_ge(stage[0], 16 * sum(slot[j] == 0 for j in staged if j[0] in ("xbc", "zs")))
            act.wait_ge(stage[1], 16 * sum(slot[j] == 1 for j in staged if j[0] in ("xbc", "zs")))

        @block.vector
        def _(dve):
            do = Chain(dve, s.chain)
            v = nc.vector

            def bias(u):
                g, nb = units[u]
                dve.wait_ge(s.scored, u + 1)
                if nb == 0:
                    dve.wait_ge(bias_in[g % 2], 16 * (g // 2 + 1))
                if u >= 2:
                    dve.wait_ge(s.turned, 2 * (u - 1))
                for i in range(G4):
                    h, at = G4 * g + i, (i // 2) * 2 * P
                    ins = v.tensor_tensor_reduce(
                        SC[:, u % 2, i, lo(nb):2 * P], PS[:, 2 * (u % 2) + i % 2, at + lo(nb):at + 2 * P],
                        BIAS[:, g % 2, i, lo(nb):2 * P], HD ** -0.5, SK[:, h:h + 1], ALU.add, ALU.max,
                        MX[:, u % 2, i:i + 1])
                ins.then_inc(s.biased, 1)
                dve.wait_ge(s.biased, u + 1)
                do(v.tensor_tensor(ES[:, u % 2], SK[:, G4 * g:G4 * g + G4], MX[:, u % 2], ALU.subtract))
                v.tensor_scalar(NM[:, u % 2], MX[:, u % 2], -1.0, None, ALU.mult).then_inc(s.neg, 1)

            def move1(u):
                dve.wait_ge(s.turned, 2 * u + 2)
                if u >= 2:
                    dve.wait_ge(s.outed, u - 1)
                v.tensor_copy(PT[:, u % 2, 1], PS[:, 2 * (u % 2) + 1, :]).then_inc(s.moved1, 1)

            def inverse(u):
                dve.wait_ge(s.exps, 5 * u + 5)
                do(v.tensor_tensor(DN[:, u % 2], DN[:, u % 2], ES[:, u % 2], ALU.add))
                v.reciprocal(RD[:, u % 2], DN[:, u % 2]).then_inc(s.rden, 1)

            def taps(n):
                kind, i = jobs[n]
                if kind != "xbc":
                    return
                dve.wait_ge(s.tap, dve_jobs.index((kind, i)) + 1)
                ch, st = layer * XT + i, ST[:, slot[kind, i]]
                for tap in range(1, CK2):
                    ins = v.scalar_tensor_tensor(out=st[:, tap:T], in0=bank2(m, pair(n))[:, 0:T - tap],
                                                 scalar=m.col("conv_w_2", ch * CK2 + CK2 - 1 - tap),
                                                 in1=st[:, tap:T], op0=ALU.mult, op1=ALU.add)
                    if tap < CK2 - 1:
                        do(ins)
                ins.then_inc(s.dve_free, 1)

            def gate(u):
                g, nb = units[u]
                dve.wait_ge(s.outed, u + 1)
                if nb == 0:
                    free(dve, where["za", 2 * g + 1])
                a = AT[:, 2 * (g % 2):2 * (g % 2) + 2, nb * P:(nb + 1) * P]
                v.tensor_tensor(a, PS[:, 2 * (u % 2), 0:2 * P].rearrange("p (i q) -> p i q", i=2), a, ALU.mult
                                ).then_inc(s.gated, 1)

            x.vector(dve)
            dve.wait_ge(s.small_free, 2)
            step.vector(dve)
            dve.wait_ge(s.sink_in, 16)
            for u in range(N + 1):
                if u < N:
                    bias(u)
                if u:
                    move1(u - 1)
                if u < N:
                    inverse(u)
                if u:
                    taps(F + u - 1)
                    gate(u - 1)


def state_space(m, d_skip, xbc_d, gate_d, DT, DA, NA, EI, DE, CD):
    nc, t, PS, HT = m.nc, m.t, m.PS, m.HT
    BF16 = mybir.dt.bfloat16
    GW = DI // SG
    with ExitStack() as ctx:
        SQ = alloc(m, ctx, "gated_squares", [P, KT, P])
        RS = alloc(m, ctx, "inverse_rms", [P, 2, SG, P])
        XB = alloc(m, ctx, "xbc", [P, XT, T])
        ZS = alloc(m, ctx, "z_gate", [P, KT, T])
        E = alloc(m, ctx, "decays", [P, SH, P])
        XS = alloc(m, ctx, "x_by_token", [P, DI])
        XDT = alloc(m, ctx, "x_dt", [P, DI])
        XDE = alloc(m, ctx, "x_dt_decayed", [P, DI])
        Y = alloc(m, ctx, "y", [P, 2, DI])
        tmp = alloc(m, ctx, "y_tmp", [P, DI])
        BC = alloc(m, ctx, "b_and_cb", [P, 512])
        S = alloc(m, ctx, "state", [P, DI])
        DS = alloc(m, ctx, "skip_rows", [P, SH])
        eps = m.small[:, 0:1]
        identb = ctx.enter_context(nc.sbuf_tensor(f"ident_bf16_{m.phases}", [P, P], BF16))
        negb = ctx.enter_context(nc.sbuf_tensor(f"neg_bf16_{m.phases}", [P, 4, P], BF16))
        s = phase(m, "rows_in x_in0 x_in1 z_in pe act dve pool masks m_ready chain y_sum squared inverse normed")
        block = ctx.enter_context(nc.Block())

        order = [("B", "act", 7, 1), ("R0", "act", 4, 1), ("X", "act", 0, 2), ("R1", "act", 5, 1),
                 ("R2", "act", 4, 1), ("R3", "act", 5, 1), ("G", "dve", 0, 2),
                 ("YO", "dve", 2, 2), ("ST", "dve", 6, 2), ("SS", "act", 4, 1), ("YD", "dve", 0, 2)]
        plan = [(c - (name in ("G", "SS")), name, eng, bank, n) for c in range(TT) for name, eng, bank, n in order
                if name not in ("G", "SS") or c]
        plan += [(TT - 1, "G", "dve", 0, 2), (TT - 1, "SS", "act", 4, 1)]
        count, filled, emptied, before, last_in = {"act": 0, "dve": 0}, {}, {}, {}, {}
        for i, (c, name, eng, bank, n) in enumerate(plan):
            count[eng] += 1
            filled[c, name], emptied[c, name] = i + 1, (eng, count[eng])
            before[c, name] = sorted({last_in[b] for b in range(bank, bank + n) if b in last_in})
            for b in range(bank, bank + n):
                last_in[b] = (c, name)

        def empty(eng, key):
            who, n = emptied[key]
            eng.wait_ge(s.act if who == "act" else s.dve, n)

        by_head = lambda ap: ap.rearrange("p (h c) -> p h c", h=SH)
        wide = lambda ap, c: ap[:, c * SH:(c + 1) * SH].unsqueeze(2).to_broadcast([P, SH, HD])

        @block.sync
        def _(sp):
            sp.dma_start(DS[:], d_skip.to_broadcast([P, SH])).then_inc(s.rows_in, 16)
            for cols, sem in ((slice(0, P), s.x_in0), (slice(P, T), s.x_in1)):
                sp.dma_start(XB[:, :, cols], xbc_d[:, :, cols].rearrange("k p t -> p k t")).then_inc(sem, 16)
            sp.dma_start(ZS[:], gate_d.rearrange("k p t -> p k t")).then_inc(s.z_in, 16)

        @block.tensor
        def _(pe):
            pe.wait_ge(s.masks, 3)
            pe.wait_ge(s.x_in0, 16)
            for c, name, eng, bank, n in plan:
                if (c, name) == (1, "B"):
                    pe.wait_ge(s.x_in1, 16)
                for key in before[c, name]:
                    empty(pe, key)
                B = PS[:, bank, :]
                cols = slice(c * P, (c + 1) * P)
                if name == "X":
                    for q in range(KT):
                        last = pe.transpose(PS[:, bank + q // 4, (q % 4) * P:(q % 4 + 1) * P], XB[:, q, cols],
                                            m.const("ident"))
                elif name == "B":
                    for g in range(SG):
                        pe.transpose(B[:, g * P:(g + 1) * P], XB[:, KT + g, cols], m.const("ident"))
                    for g in range(SG):
                        last = pe.matmul(B[:, (2 + g) * P:(3 + g) * P], XB[:, KT + g, cols],
                                         XB[:, KT + SG + g, cols], start=True, stop=True)
                elif name[0] == "R":
                    r = int(name[1])
                    pe.matmul(B, identb[:], negb[:].rearrange("p a b -> p (a b)"), start=True, stop=False,
                              skip_group_check=True)
                    for i in range(4):
                        at = c * SH + 4 * r + i
                        last = pe.matmul(B[:, i * P:(i + 1) * P], DA[:, at:at + 1].to_broadcast([P, P]),
                                         m.const("tri"), start=False, stop=i == 3, skip_group_check=True)
                elif name == "G":
                    pe.wait_ge(s.y_sum, c + 1)
                    for q in range(KT):
                        last = pe.transpose(PS[:, bank + q // 4, (q % 4) * P:(q % 4 + 1) * P],
                                            Y[:, c % 2, q * P:(q + 1) * P], m.const("ident"))
                elif name == "SS":
                    pe.wait_ge(s.squared, c + 1)
                    for g in range(SG):
                        for q in range(KT // SG):
                            last = pe.matmul(B[:, g * P:(g + 1) * P], m.const("ones"), SQ[:, g * (KT // SG) + q],
                                             start=q == 0, stop=q == KT // SG - 1)
                elif name == "YO":
                    if c:
                        empty(pe, (c - 1, "ST"))
                    for g in range(SG):
                        last = pe.matmul(PS[:, bank + g, :], XB[:, KT + SG + g, cols], S[:, g * GW:(g + 1) * GW],
                                         start=True, stop=True)
                elif name == "ST":
                    empty(pe, (c, "B"))
                    pe.wait_ge(s.pool, 3 * c + 3)
                    for g in range(SG):
                        last = pe.matmul(PS[:, bank + g, :], BC[:, g * P:(g + 1) * P], XDE[:, g * GW:(g + 1) * GW],
                                         start=True, stop=True)
                elif name == "YD":
                    pe.wait_ge(s.m_ready, 4 * c + 4)
                    for h in range(SH):
                        last = pe.matmul(PS[:, bank + h // 8, (h % 8) * HD:(h % 8 + 1) * HD], E[:, h],
                                         XDT[:, h * HD:(h + 1) * HD], start=True, stop=True)
                last.then_inc(s.pe, 1)

        @block.scalar
        def _(act):
            def squares(c):
                empty(act, (c, "G"))
                if c:
                    act.wait_ge(s.pe, filled[c - 1, "SS"])
                nc.scalar.activation(SQ[:], HT[:, :, c * P:(c + 1) * P], ACT.Square).then_inc(s.squared, 1)

            for c, name, eng, bank, n in plan:
                if eng != "act":
                    continue
                if name == "SS":
                    squares(c)
                act.wait_ge(s.pe, filled[c, name])
                B = PS[:, bank, :]
                both = bank2(m, bank // 2)
                if name == "X":
                    if c:
                        act.wait_ge(s.pool, 3 * c)
                    ins = nc.scalar.copy(XS[:], both)
                elif name == "B":
                    ins = nc.scalar.copy(BC[:], B)
                elif name[0] == "R":
                    for i in range(4):
                        h = 4 * int(name[1]) + i
                        ins = nc.scalar.activation(E[:, h], B[:, i * P:(i + 1) * P], ACT.Exp,
                                                   bias=NA[:, c * SH + h:c * SH + h + 1])
                elif name == "SS":
                    if c >= 2:
                        act.wait_ge(s.normed, c - 1)
                    ins = nc.scalar.activation(RS[:, c % 2], B[:, 0:SG * P].rearrange("p (g n) -> p g n", g=SG),
                                               ACT.Sqrt, scale=1.0 / GW, bias=eps)
                ins.then_inc(s.act, 1)

        @block.gpsimd
        def _(pool):
            pool.wait_ge(s.rows_in, 16)
            v = nc.gpsimd
            for c in range(TT):
                empty(pool, (c, "X"))
                if c:
                    pool.wait_ge(s.pe, filled[c - 1, "YD"])
                v.tensor_tensor(by_head(XDT[:]), by_head(XS[:]), wide(DT, c), ALU.mult).then_inc(s.pool, 1)
                if c >= 2:
                    pool.wait_ge(s.pe, filled[c - 2, "G"])
                v.tensor_tensor(by_head(Y[:, c % 2]), by_head(XS[:]), DS[:].unsqueeze(2).to_broadcast([P, SH, HD]),
                                ALU.mult).then_inc(s.pool, 1)
                pool.wait_ge(s.pool, 3 * c + 1)
                v.tensor_tensor(by_head(XDE[:]), by_head(XDT[:]), wide(DE, c), ALU.mult).then_inc(s.pool, 1)

        @block.vector
        def _(dve):
            v = nc.vector
            do = Chain(dve, s.chain)
            v.tensor_copy(identb[:], m.const("ident")).then_inc(s.masks, 1)
            v.tensor_copy(negb[:], m.const("neg_up").unsqueeze(1).to_broadcast([P, 4, P])).then_inc(s.masks, 1)
            v.memset(eps, RMS_EPS_2)
            v.memset(S[:], 0.0).then_inc(s.masks, 1)
            dve.wait_ge(s.rows_in, 16)


            def gate(c):
                dve.wait_ge(s.z_in, 16)
                dve.wait_ge(s.pe, filled[c, "G"])
                v.tensor_tensor(HT[:, :, c * P:(c + 1) * P],
                                PS[:, 0:2, :].rearrange("p a (b c) -> p (a b) c", b=4),
                                ZS[:, :, c * P:(c + 1) * P], ALU.mult).then_inc(s.dve, 1)

            def normalise(c):
                empty(dve, (c, "SS"))
                v.reciprocal(RS[:, c % 2], RS[:, c % 2]).then_inc(s.inverse, 1)
                dve.wait_ge(s.inverse, c + 1)
                h = HT[:, :, c * P:(c + 1) * P].rearrange("p (g k) n -> p g k n", g=SG)
                v.tensor_tensor(h, h, RS[:, c % 2].unsqueeze(2).to_broadcast([P, SG, KT // SG, P]), ALU.mult
                                ).then_inc(s.normed, 1)

            for c in range(TT):
                for r in range(4):
                    empty(dve, (c, "B"))
                    empty(dve, (c, f"R{r}"))
                    cb = BC[:, (2 + r // 2) * P:(3 + r // 2) * P].unsqueeze(1).to_broadcast([P, 4, P])
                    v.tensor_tensor(E[:, 4 * r:4 * r + 4], E[:, 4 * r:4 * r + 4], cb, ALU.mult).then_inc(s.m_ready, 1)
                if c:
                    gate(c - 1)
                pair = lambda b: PS[:, b:b + 2, :].rearrange("p a (h c) -> p (a h) c", c=HD)
                y = by_head(Y[:, c % 2])
                dve.wait_ge(s.pe, filled[c, "YO"])
                v.tensor_tensor(by_head(tmp[:]), pair(2), wide(EI, c), ALU.mult).then_inc(s.dve, 1)
                do(v.tensor_tensor(by_head(S[:]), by_head(S[:]), wide(CD, c), ALU.mult))
                dve.wait_ge(s.dve, emptied[c, "YO"][1])
                dve.wait_ge(s.pool, 3 * c + 2)
                do(v.tensor_tensor(Y[:, c % 2], Y[:, c % 2], tmp[:], ALU.add))
                dve.wait_ge(s.pe, filled[c, "ST"])
                v.tensor_tensor(S[:], S[:], PS[:, 6:8, :].rearrange("p a b -> p (a b)"), ALU.add).then_inc(s.dve, 1)
                dve.wait_ge(s.pe, filled[c, "YD"])
                v.tensor_tensor(y, y, pair(0), ALU.add).then_inc(s.dve, 1)
                dve.wait_ge(s.dve, emptied[c, "YD"][1])
                v.sem_inc(s.y_sum, 1)
                if c:
                    normalise(c - 1)
            gate(TT - 1)
            normalise(TT - 1)


def mix_and_norm(m, layer, w, ln_g, ln_b, attn_d, src, dst):
    nc, t, PS, HT = m.nc, m.t, m.PS, m.HT
    Q = 2 * KT
    with ExitStack() as ctx:
        AR = alloc(m, ctx, "attn_raw", [P, 2, T])
        AH = alloc(m, ctx, "mixed_high", [P, Q, T], F32R)
        AL = alloc(m, ctx, "mixed_low", [P, Q, T], F32R)
        RAW = alloc(m, ctx, "w_raw", [P, 3, NH])
        WH = alloc(m, ctx, "w_high", [P, 2, NH], F32R)
        WL = alloc(m, ctx, "w_low", [P, 2, NH], F32R)
        LN = alloc(m, ctx, "ln_rows", [P, 2, D])
        s = phase(m, "a_in0 a_in1 raw0 raw1 raw2 x_in rows_in high low split wchain used prod added eps summed "
                     "centred squared root chain scaled out stored")
        a_in, raw_in = [s.a_in0, s.a_in1], [s.raw0, s.raw1, s.raw2]
        block = ctx.enter_context(nc.Block())
        sums, mean, rstd, eps, squares = (m.small[:, i * TT:(i + 1) * TT] for i in range(5))
        eps = eps[:, 0:1]
        X = HT
        tiles = list(range(KT, Q)) + list(range(KT))

        @block.sync
        def _(sp):
            for i in range(2 * Q):
                half, q = i // Q, tiles[i % Q]
                if i >= 3:
                    sp.wait_ge(s.split, i - 2)
                sp.dma_start(RAW[:, i % 3], w[q * P:(q + 1) * P, half * NH:(half + 1) * NH]
                             ).then_inc(raw_in[i % 3], 16)
                if i == KT:
                    sp.wait_ge(s.low, KT)
                    sp.dma_start(X[:], src.rearrange("(k p) n -> p k n", p=P)).then_inc(s.x_in, 16)
            for k in range(TT):
                sp.wait_ge(s.out, k + 1)
                sp.dma_start(dst[k * P:(k + 1) * P], X[:, k]).then_inc(s.stored, 16)
            sp.wait_ge(s.stored, 16 * TT)

        @block.tensor
        def _(pe):
            for i in range(2 * Q):
                half, q = i // Q, tiles[i % Q]
                pe.wait_ge(s.split, i + 1)
                if not half:
                    pe.wait_ge(s.low, i + 1)
                for k in range(TT):
                    if i == Q:
                        pe.wait_ge(s.added, k + 1)
                    cols = slice(k * P, (k + 1) * P)
                    for a, b in ((AH, WH), (AH, WL), (AL, WH)):
                        last = pe.matmul(PS[:, k, :], a[:, q, cols], b[:, i % 2],
                                         start=i % Q == 0 and a is AH and b is WH, stop=i % Q == Q - 1 and a is AL)
                    if i % Q == Q - 1:
                        last.then_inc(s.prod, 1)
                if i % Q < Q - 1:
                    last.then_inc(s.used, 1)
                else:
                    pe.wait_ge(s.prod, TT * (half + 1))
                    pe.sem_inc(s.used, 1)

        @block.gpsimd
        def _(pool):
            pool.dma_start(LN[:, 0], ln_g.to_broadcast([P, D])).then_inc(s.rows_in, 16)
            pool.dma_start(LN[:, 1], ln_b.to_broadcast([P, D])).then_inc(s.rows_in, 16)
            for i in range(2 * Q):
                pool.wait_ge(raw_in[i % 3], 16 * (i // 3 + 1))
                if i >= 2:
                    pool.wait_ge(s.used, i - 1)
                nc.gpsimd.tensor_copy(WH[:, i % 2], RAW[:, i % 3]).then_inc(s.wchain, 1)
                pool.wait_ge(s.wchain, i + 1)
                nc.gpsimd.tensor_tensor(WL[:, i % 2], RAW[:, i % 3], WH[:, i % 2], ALU.subtract).then_inc(s.split, 1)
            pool.wait_ge(s.rows_in, 32)
            for k in range(TT):
                pool.wait_ge(s.scaled, k + 1)
                nc.gpsimd.tensor_tensor(X[:, k], X[:, k], LN[:, 1], ALU.add).then_inc(s.out, 1)

        @block.scalar
        def _(act):
            for i in range(Q):
                q = tiles[i]
                if q >= KT:
                    nc.scalar.mul(AH[:, q], HT[:, q - KT], m.col("norm_w_2", layer * KT + q - KT)).then_inc(s.high, 1)
                else:
                    if q >= 2:
                        act.wait_ge(s.low, KT + q - 1)
                    act.dma_start(AR[:, q % 2], attn_d[q]).then_inc(a_in[q % 2], 16)
                    act.wait_ge(a_in[q % 2], 16 * (q // 2 + 1))
                    nc.scalar.copy(AH[:, q], AR[:, q % 2]).then_inc(s.high, 1)
            act.wait_ge(s.eps, 1)
            for k in range(TT + 1):
                if k < TT:
                    act.wait_ge(s.added, TT + k + 1)
                    if k:
                        act.wait_ge(s.summed, k)
                    nc.scalar.activation(AR[:, 0], X[:, k], ACT.Identity, accum_out=sums[:, k:k + 1]
                                         ).then_inc(s.summed, 1)
                if k:
                    act.wait_ge(s.centred, k)
                    if k > 1:
                        act.wait_ge(s.squared, k - 1)
                    nc.scalar.activation(AR[:, 1], X[:, k - 1], ACT.Square, accum_out=squares[:, k - 1:k]
                                         ).then_inc(s.squared, 1)
                    act.wait_ge(s.squared, k)
                    nc.scalar.activation(rstd[:, k - 1:k], squares[:, k - 1:k], ACT.Sqrt, scale=1.0 / D, bias=eps
                                         ).then_inc(s.root, 1)

        @block.vector
        def _(dve):
            v = nc.vector
            do = Chain(dve, s.chain)
            v.memset(eps, LN_EPS).then_inc(s.eps, 1)
            for i in range(Q):
                q = tiles[i]
                dve.wait_ge(s.high, i + 1)
                if q >= KT:
                    v.scalar_tensor_tensor(out=AL[:, q], in0=HT[:, q - KT],
                                           scalar=m.col("norm_w_2", layer * KT + q - KT), in1=AH[:, q],
                                           op0=ALU.mult, op1=ALU.subtract).then_inc(s.low, 1)
                else:
                    v.tensor_tensor(AL[:, q], AR[:, q % 2], AH[:, q], ALU.subtract).then_inc(s.low, 1)
            def centre(k):
                dve.wait_ge(s.summed, k + 1)
                do(v.tensor_scalar(mean[:, k:k + 1], sums[:, k:k + 1], 1.0 / D, None, ALU.mult))
                v.tensor_scalar(X[:, k], X[:, k], mean[:, k:k + 1], None, ALU.subtract).then_inc(s.centred, 1)

            def normalise(k):
                dve.wait_ge(s.root, k + 1)
                do(v.reciprocal(rstd[:, k:k + 1], rstd[:, k:k + 1]))
                v.scalar_tensor_tensor(out=X[:, k], in0=X[:, k], scalar=rstd[:, k:k + 1], in1=LN[:, 0],
                                       op0=ALU.mult, op1=ALU.mult).then_inc(s.scaled, 1)

            dve.wait_ge(s.x_in, 16)
            dve.wait_ge(s.rows_in, 32)
            for half in range(2):
                for k in range(TT):
                    x = X[:, k, half * NH:(half + 1) * NH]
                    dve.wait_ge(s.prod, half * TT + k + 1)
                    v.scalar_tensor_tensor(out=x, in0=x, scalar=ALPHA, in1=PS[:, k, :], op0=ALU.mult, op1=ALU.add
                                           ).then_inc(s.added, 1)
                    if half and k:
                        centre(k - 1)
                    if half and k >= 2:
                        normalise(k - 2)
            centre(TT - 1)
            normalise(TT - 2)
            normalise(TT - 1)


def first_block(m, x_mid, dst):
    nc, t = m.nc, m.t
    with ExitStack() as whole:
        GM = alloc(m, whole, "gates", [P, 2, D])
        with ExitStack() as mixing:
            MIX = alloc(m, mixing, "mix", [P, CT, T])
            RKVQ = alloc(m, mixing, "rkvq", [P, 4 * CT, T])
            LO = alloc(m, mixing, "lora", [P, 3, T])
            by_block = lambda ap: ap.rearrange("p a (b n) -> p (a b) n", n=512)
            with ExitStack() as parts:
                HH, HL = (alloc(m, parts, n, [P, KT, T], F32R) for n in ("h_high", "h_low"))
                h = NormedIn(m, t.x, 0, HH, HL, RKVQ, [by_block(MIX[:]), by_block(RKVQ[:, 3 * CT:4 * CT])])
                in_projection(m, MIX, RKVQ, LO, HH, HL, h)
            m.HT = alloc(m, mixing, "HT", [P, KT, T])
            conv_branch(m, MIX, GM, [by_block(m.HT[:, 0:4]), by_block(m.HT[:, 4:8])],
                        RKVQ[:, 3 * CT:4 * CT].rearrange("p (a b) t -> p a b t", a=2))
            with ExitStack() as inner:
                G2 = alloc(m, inner, "g2", [P, 2, CW])
                PC = alloc(m, inner, "chunk_decay", [P, CT, T // CH])
                bonus = alloc(m, inner, "bonus", [P, TT * RH])
                rwkv_operands(m, RKVQ, LO, G2, m.HT[:, 0:CT], m.HT[:, CT:2 * CT], PC, bonus)
                rwkv_recurrence(m, RKVQ, m.HT[:, 0:CT], PC, LO, G2, bonus)
            tiles = [MIX[:, q] for q in range(CT)] + [RKVQ[:, 2 * CT + q] for q in range(CT)]
            out_projection(m, tiles, t.w_out, GM[:, 0], m.HT, x_mid)
        with ExitStack() as ctx:
            MID = alloc(m, ctx, "mid", [P, FT, T])
            with ExitStack() as parts:
                HH, HL = (alloc(m, parts, n, [P, KT, T], F32R) for n in ("h_high", "h_low"))
                up_projection(m, MID, HH, HL, NormedIn(m, x_mid, 1, HH, HL, MID))
            down_projection(m, MID, GM[:, 1], x_mid, dst)


def second_layer(m, i, src, dst):
    t = m.t
    row = lambda ap: ap[i:i + 1]
    scratch = lambda name, tiles: m.nc.dram_tensor(f"{name}_{i}", (tiles, P, T), F32, kind="Internal").ap()
    attn_d, xbc_d, gate_d = scratch("attn", KT), scratch("xbc", XT), scratch("gate", KT)
    with ExitStack() as whole:
        DT, DA, NA, EI, DE, CD = (alloc(m, whole, n, [P, TT * SH]) for n in ("dt", "dta", "na", "ei", "de", "cd"))
        with ExitStack() as ctx:
            HH, HL = (alloc(m, ctx, n, [P, KT, T], F32R) for n in ("x_high", "x_low"))
            x = TurnedIn(m, src if i == 0 else None, HH, HL)
            step = StepSizes(m, ctx, row(t.dt_bias_2), row(t.a_log_2), DT, NA, EI, DE, CD, DA)
            projections_and_attention(m, i, t.w_in_2[i], row(t.sinks_2), HH, HL, x, step, attn_d, xbc_d, gate_d)
        state_space(m, row(t.d_skip_2), xbc_d, gate_d, DT, DA, NA, EI, DE, CD)
        mix_and_norm(m, i, t.w_out_2[i], row(t.ln_g_2), row(t.ln_b_2), attn_d, src, dst)


def hybrid_kernel(nc, t):
    m = make(nc, t)
    between = lambda name: nc.dram_tensor(name, (T, D), F32, kind="Internal").ap()
    x_mid, x1, x2 = between("after_mixing"), between("after_first_block"), between("after_first_layer")
    first_block(m, x_mid, x1)
    m.HT = alloc(m, m.ctx, "HT_2", [P, KT, T])
    recycle(m)
    second_layer(m, 0, x1, x2)
    recycle(m)
    second_layer(m, 1, x2, t.out)
    m.ctx.close()




def laid_out(inputs):
    import numpy as _np

    a = {k: _np.ascontiguousarray(v) for k, v in inputs.items()}
    column = lambda v: v.reshape(-1, P).T
    taps = lambda w: _np.transpose(w.reshape(w.shape[0], -1, P), (2, 1, 0)).reshape(P, -1)
    mu = _np.zeros((15 * P,), a["rwkv_mu"].dtype)
    mu[:a["rwkv_mu"].shape[1]] = a["rwkv_mu"][0]
    ada = a["ada_b"][0].reshape(6, D)
    parts = {
        "c": column(a["c"][0]), "ada_b": _np.concatenate([column(ada[i]) for i in (0, 1, 3, 4)], axis=1),
        "pre_g": _np.concatenate([column(a["mix_pre_g"][0]), column(a["ffn_pre_g"][0])], axis=1),
        "mu": column(mu), "conv_b": column(a["conv_dw_b"][0]), "conv_ln_g": column(a["conv_ln_g"][0]),
        "conv_ln_b": column(a["conv_ln_b"][0]), "w0": column(a["w0"][0]), "a0": column(a["a0"][0]),
        "k_k": column(a["k_k"][0]), "k_a": column(a["k_a"][0]), "r_k": column(a["r_k"][0].reshape(-1)),
        "conv_w": taps(a["conv_dw_w"][0]), "ffn_b": column(a["ffn_dw_b"][0]), "ffn_w": taps(a["ffn_dw_w"][0]),
        "conv_b_2": _np.concatenate([column(a["conv_b_2"][i]) for i in range(LAYERS)], axis=1),
        "norm_w_2": _np.concatenate([column(a["ssm_norm_w_2"][i]) for i in range(LAYERS)], axis=1),
        "conv_w_2": _np.concatenate([taps(a["conv_w_2"][i]) for i in range(LAYERS)], axis=1),
    }
    consts, alibi = shape_constants()
    arrays = {
        "cols": _np.ascontiguousarray(_np.concatenate([parts[n] for n in COLS], axis=1)),
        "consts": consts, "alibi": alibi, "x": a["x"][0],
    }
    for name in ("ada_w", "w_in", "w_out", "w_up", "w_down", "w2", "a2", "g2"):
        arrays[name] = a[name][0]
    for name in ("ada_b", "mix_post_g", "ffn_post_g", "lnx_g", "lnx_b"):
        arrays[name] = a[name]
    for name in ("w_in_2", "w_out_2"):
        arrays[name] = a[name]
    for name in ("dt_bias_2", "a_log_2", "d_skip_2", "sinks_2", "ln_g_2", "ln_b_2"):
        arrays[name] = a[name]
    return {k: _np.ascontiguousarray(v) for k, v in arrays.items()}


def kernel(**inputs):
    from collections import namedtuple as _namedtuple

    import concourse.bacc as _bacc
    from concourse import mybir as _mybir
    from concourse.bass_utils import run_bass_kernel_spmd as _run

    nc = _bacc.Bacc("TRN2", target_bir_lowering=False, num_devices=1)
    arrays = laid_out(inputs)
    tensors = {
        n: nc.dram_tensor(n, a.shape, _mybir.dt.from_np(a.dtype), kind="ExternalInput").ap()
        for n, a in arrays.items()
    }
    tensors["out"] = nc.dram_tensor("out", (T, D), F32, kind="ExternalOutput").ap()
    t = _namedtuple("Tensors", list(tensors))(*tensors.values())
    hybrid_kernel(nc, t)
    r = _run(nc, [arrays], core_ids=[0])
    return r.results[0]["out"].reshape(1, T, D)
```
